# Optimizing a Trainium2 kernel written in Bass

```python
import jax, jax.numpy as jnp
from jax import lax
import numpy as np

D_MODEL = 1024
BATCH = 1
SEQ = 256
DEPTH = 1

N_META = 16
NORM_EPS = 1e-5
GLA_HEADS = 4
GLA_KEY = D_MODEL // 2
GLA_VAL = D_MODEL
GLA_DK = GLA_KEY // GLA_HEADS
GLA_DV = GLA_VAL // GLA_HEADS
GLA_GATE_RANK = 16
GLA_GATE_NORM = 16.0
GLA_CHUNK = 64
RWKV_HEAD = 64
RWKV_WIDTH = D_MODEL
RWKV_HEADS = RWKV_WIDTH // RWKV_HEAD
RWKV_DECAY_RANK = 64
RWKV_A_RANK = 64
RWKV_GATE_RANK = 160
RWKV_GN_EPS = 64e-5
N_EXPERTS = 32
TOP_K = 4
D_EXPERT = D_MODEL
SWIGLU_LIMIT = 7.0
SWIGLU_ALPHA = 1.702
IN_SPLITS = (GLA_KEY, GLA_KEY, GLA_VAL, GLA_VAL, GLA_GATE_RANK,
             RWKV_WIDTH, RWKV_WIDTH, RWKV_WIDTH, RWKV_DECAY_RANK, RWKV_A_RANK, RWKV_GATE_RANK,
             D_MODEL, D_MODEL)
D_IN = sum(IN_SPLITS)

kernel_name = 'hybrid_gla_rwkv7_moe_block'

def rmsnorm(x, g):
    xf = x.astype(jnp.float32)
    y = xf * lax.rsqrt(jnp.mean(xf * xf, axis=-1, keepdims=True) + NORM_EPS)
    return (y * g).astype(x.dtype)

def token_shift(z):
    return jnp.pad(z, ((0, 0), (1, 0), (0, 0)))[:, :-1]

def gla_branch(q, k, v, r, a_low, w_gla_a2, b_gla_a, gla_norm_g):
    B, L, _ = q.shape
    f32 = jnp.float32
    C = GLA_CHUNK
    pad = (-N_META) % C
    gk = jax.nn.log_sigmoid((a_low @ w_gla_a2 + b_gla_a).astype(f32)) / GLA_GATE_NORM

    def chunks(z, dh):
        z = jnp.pad(z.astype(f32), ((0, 0), (pad, 0), (0, 0)))
        return z.reshape(B, -1, C, GLA_HEADS, dh).transpose(0, 3, 1, 2, 4)

    qc = chunks(q, GLA_DK) * GLA_DK ** -0.5
    kc = chunks(k, GLA_DK)
    vc = chunks(v, GLA_DV)
    b = jnp.cumsum(chunks(gk, GLA_DK), axis=3)
    b_ref = b[:, :, :, C // 2 - 1:C // 2]
    A = jnp.einsum('bhnid,bhnjd->bhnij', qc * jnp.exp(b - b_ref), kc * jnp.exp(b_ref - b))
    A = jnp.where(jnp.tril(jnp.ones((C, C), dtype=bool)), A, 0.0)
    o_intra = jnp.einsum('bhnij,bhnjv->bhniv', A, vc)
    b_last = b[:, :, :, -1:]
    chunk_kv = jnp.einsum('bhncd,bhncv->bhndv', kc * jnp.exp(b_last - b), vc)
    chunk_decay = jnp.exp(b_last[:, :, :, 0])

    def step(S, inp):
        d, kv = inp
        return d[..., None] * S + kv, S

    S0 = jnp.zeros((B, GLA_HEADS, GLA_DK, GLA_DV), f32)
    _, S_start = lax.scan(step, S0, (jnp.moveaxis(chunk_decay, 2, 0), jnp.moveaxis(chunk_kv, 2, 0)))
    S_start = jnp.moveaxis(S_start, 0, 2)
    o_inter = jnp.einsum('bhncd,bhndv->bhncv', qc * jnp.exp(b), S_start)
    o = (o_intra + o_inter).transpose(0, 2, 3, 1, 4).reshape(B, -1, GLA_HEADS, GLA_DV)[:, pad:]
    o = o * lax.rsqrt(jnp.mean(o * o, axis=-1, keepdims=True) + NORM_EPS) * gla_norm_g
    o = o.reshape(B, L, GLA_VAL) * jax.nn.silu(r.astype(f32))
    return o.astype(q.dtype)

def rwkv7_branch(pr, pk, pv, pw, pa, pg, mu_r, mu_k, mu_v, mu_w, mu_a, mu_g,
                 w_decay2, b_decay, w_a2, b_a, w_gate2, k_k, k_a, r_k, ln_x_g, ln_x_b):
    B, L, _ = pr.shape
    f32 = jnp.float32
    lerp = lambda z, mu: (z + (token_shift(z) - z) * mu).astype(f32)
    r = lerp(pr, mu_r)
    k = lerp(pk, mu_k)
    v = lerp(pv, mu_v)
    w_log = -jax.nn.softplus(-(b_decay + jnp.tanh(lerp(pw, mu_w)) @ w_decay2)) - 0.5
    decay = jnp.exp(-jnp.exp(w_log))
    a = jax.nn.sigmoid(b_a + lerp(pa, mu_a) @ w_a2)
    g = jax.nn.sigmoid(lerp(pg, mu_g)) @ w_gate2
    heads = lambda z: z.reshape(B, L, RWKV_HEADS, RWKV_HEAD)
    r, k, v, decay, a = heads(r), heads(k), heads(v), heads(decay), heads(a)
    kk = k * k_k.reshape(RWKV_HEADS, RWKV_HEAD)
    kk = kk / jnp.maximum(jnp.sqrt(jnp.sum(kk * kk, axis=-1, keepdims=True)), 1e-12)
    k = k * (1.0 + (a - 1.0) * k_a.reshape(RWKV_HEADS, RWKV_HEAD))

    def step(S, inp):
        r_t, w_t, k_t, v_t, a_t, b_t = inp
        sa = jnp.einsum('bhij,bhj->bhi', S, a_t)
        S = S * w_t[:, :, None, :] + sa[..., None] * b_t[:, :, None, :] + v_t[..., None] * k_t[:, :, None, :]
        return S, jnp.einsum('bhij,bhj->bhi', S, r_t)

    tm = lambda z: jnp.moveaxis(z, 1, 0)
    S0 = jnp.zeros((B, RWKV_HEADS, RWKV_HEAD, RWKV_HEAD), f32)
    _, ys = lax.scan(step, S0, (tm(r), tm(decay), tm(k), tm(v), tm(-kk), tm(kk * a)))
    y = jnp.moveaxis(ys, 0, 1)
    mean = jnp.mean(y, axis=-1, keepdims=True)
    var = jnp.mean(jnp.square(y - mean), axis=-1, keepdims=True)
    y = (y - mean) * lax.rsqrt(var + RWKV_GN_EPS)
    y = y * ln_x_g.reshape(RWKV_HEADS, RWKV_HEAD) + ln_x_b.reshape(RWKV_HEADS, RWKV_HEAD)
    y = y + jnp.sum(r * k * r_k, axis=-1, keepdims=True) * v
    return (y.reshape(B, L, RWKV_WIDTH) * g).astype(pr.dtype)

def moe_ffn(u, w_router, b_router, w_exp_gu, b_exp_gu, w_exp_down, b_exp_down):
    B, L, D = u.shape
    ut = u.reshape(B * L, D)
    logits = (ut @ w_router + b_router).astype(jnp.float32)
    top_vals, top_idx = lax.top_k(logits, TOP_K)
    probs = jax.nn.softmax(top_vals, axis=-1)
    comb = jnp.sum(jax.nn.one_hot(top_idx, N_EXPERTS, dtype=jnp.float32) * probs[..., None], axis=1)
    comb = comb.astype(ut.dtype)

    def expert(acc, p):
        w_gu, b_gu, w_dn, b_dn, c_e = p
        h = ut @ w_gu + b_gu
        gate, up = h[:, :D_EXPERT], h[:, D_EXPERT:]
        gate = jnp.minimum(gate, SWIGLU_LIMIT)
        up = jnp.clip(up, -SWIGLU_LIMIT, SWIGLU_LIMIT)
        out = ((up + 1.0) * (gate * jax.nn.sigmoid(gate * SWIGLU_ALPHA))) @ w_dn + b_dn
        return acc + c_e[:, None] * out, None

    acc, _ = lax.scan(expert, jnp.zeros_like(ut), (w_exp_gu, b_exp_gu, w_exp_down, b_exp_down, comb.T))
    return acc.reshape(B, L, D)

def setup_inputs(seed: int = 0) -> dict:
    key = jax.random.key(seed)
    ks = list(jax.random.split(key, 48))
    it = iter(ks)
    D, Ly = D_MODEL, DEPTH
    nrm = lambda shape, s: jax.random.normal(next(it), shape, jnp.float32) * s
    uni = lambda shape, lo, hi: jax.random.uniform(next(it), shape, jnp.float32, lo, hi)
    gain = lambda shape: 1.0 + nrm(shape, 0.02)
    return {
        'x': nrm((BATCH, SEQ, D), 1.0),
        'meta_tokens': nrm((N_META, D), 1.0),
        'norm_mix_g': gain((Ly, D)),
        'w_in': nrm((Ly, D, D_IN), D ** -0.5),
        'w_gla_a2': nrm((Ly, GLA_GATE_RANK, GLA_KEY), GLA_GATE_RANK ** -0.5),
        'b_gla_a': nrm((Ly, GLA_KEY), 1.0),
        'gla_norm_g': gain((Ly, GLA_DV)),
        'w_gla_o': nrm((Ly, GLA_VAL, D), GLA_VAL ** -0.5),
        'mu_r': uni((Ly, RWKV_WIDTH), 0.0, 1.0),
        'mu_k': uni((Ly, RWKV_WIDTH), 0.0, 1.0),
        'mu_v': uni((Ly, RWKV_WIDTH), 0.0, 1.0),
        'mu_w': uni((Ly, RWKV_DECAY_RANK), 0.0, 1.0),
        'mu_a': uni((Ly, RWKV_A_RANK), 0.0, 1.0),
        'mu_g': uni((Ly, RWKV_GATE_RANK), 0.0, 1.0),
        'w_decay2': nrm((Ly, RWKV_DECAY_RANK, RWKV_WIDTH), RWKV_DECAY_RANK ** -0.5),
        'b_decay': uni((Ly, RWKV_WIDTH), -5.0, 1.0),
        'w_a2': nrm((Ly, RWKV_A_RANK, RWKV_WIDTH), RWKV_A_RANK ** -0.5),
        'b_a': nrm((Ly, RWKV_WIDTH), 0.1),
        'w_gate2': nrm((Ly, RWKV_GATE_RANK, RWKV_WIDTH), RWKV_GATE_RANK ** -0.5),
        'k_k': 0.85 + nrm((Ly, RWKV_WIDTH), 0.02),
        'k_a': gain((Ly, RWKV_WIDTH)),
        'r_k': nrm((Ly, RWKV_HEADS, RWKV_HEAD), 0.1),
        'ln_x_g': gain((Ly, RWKV_WIDTH)),
        'ln_x_b': nrm((Ly, RWKV_WIDTH), 0.01),
        'w_rwkv_o': nrm((Ly, RWKV_WIDTH, D), RWKV_WIDTH ** -0.5),
        'w_out': nrm((Ly, D, D), D ** -0.5),
        'norm_ffn_g': gain((Ly, D)),
        'w_router': nrm((Ly, D, N_EXPERTS), D ** -0.5),
        'b_router': nrm((Ly, N_EXPERTS), 0.01),
        'w_exp_gu': nrm((Ly, N_EXPERTS, D, 2 * D_EXPERT), D ** -0.5),
        'b_exp_gu': nrm((Ly, N_EXPERTS, 2 * D_EXPERT), 0.01),
        'w_exp_down': nrm((Ly, N_EXPERTS, D_EXPERT, D), D_EXPERT ** -0.5),
        'b_exp_down': nrm((Ly, N_EXPERTS, D), 0.01),
        'norm_final_g': gain((D,)),
    }

def reference(x, meta_tokens, norm_mix_g, w_in, w_gla_a2, b_gla_a, gla_norm_g, w_gla_o,
              mu_r, mu_k, mu_v, mu_w, mu_a, mu_g, w_decay2, b_decay, w_a2, b_a, w_gate2,
              k_k, k_a, r_k, ln_x_g, ln_x_b, w_rwkv_o, w_out, norm_ffn_g,
              w_router, b_router, w_exp_gu, b_exp_gu, w_exp_down, b_exp_down, norm_final_g):
    B = x.shape[0]
    meta = jnp.broadcast_to(meta_tokens[None].astype(x.dtype), (B, N_META, D_MODEL))
    h = jnp.concatenate([meta, x], axis=1)
    offsets = [int(o) for o in np.cumsum(IN_SPLITS)[:-1]]
    for l in range(DEPTH):
        u = rmsnorm(h, norm_mix_g[l])
        P = u @ w_in[l]
        (gq, gk_, gv, gr, ga, rr, rk, rv, rw, ra, rg, gate_gla, gate_rwkv) = jnp.split(P, offsets, axis=-1)
        o_gla = gla_branch(gq, gk_, gv, gr, ga, w_gla_a2[l], b_gla_a[l], gla_norm_g[l]) @ w_gla_o[l]
        o_rwkv = rwkv7_branch(rr, rk, rv, rw, ra, rg, mu_r[l], mu_k[l], mu_v[l], mu_w[l], mu_a[l], mu_g[l],
                              w_decay2[l], b_decay[l], w_a2[l], b_a[l], w_gate2[l], k_k[l], k_a[l], r_k[l],
                              ln_x_g[l], ln_x_b[l]) @ w_rwkv_o[l]
        mix = jax.nn.sigmoid(gate_gla) * o_gla + jax.nn.sigmoid(gate_rwkv) * o_rwkv
        h = h + mix @ w_out[l]
        h = h + moe_ffn(rmsnorm(h, norm_ffn_g[l]), w_router[l], b_router[l],
                        w_exp_gu[l], b_exp_gu[l], w_exp_down[l], b_exp_down[l])
    return rmsnorm(h, norm_final_g)[:, N_META:]


_drawn_inputs = setup_inputs


def setup_inputs(seed=0):
    import zlib

    import numpy as np

    out = dict(_drawn_inputs(seed))
    spreads = {}
    factors = {'mu_w': 3.11,
     'k_k': 2.853,
     'ln_x_g': 2.705,
     'ln_x_b': 5.121,
     'b_exp_gu': 8.0,
     'b_exp_down': 8.0,
     'norm_final_g': 2.832}
    for name, (base, spread) in spreads.items():
        noise = np.random.default_rng([zlib.crc32(name.encode()), seed]).standard_normal(out[name].shape)
        drawn = base * np.exp(spread * noise) if base else spread * noise
        out[name] = __import__('jax').numpy.asarray(drawn.astype(out[name].dtype))
    for name, factor in factors.items():
        out[name] = (out[name] * factor).astype(out[name].dtype)
    return out
```

```python
import concourse.bass as bass
from concourse import mybir
from contextlib import ExitStack
import numpy as np

P = 128
D = 1024
SEQ = 256
N_META = 16
T = SEQ + N_META
KC = D // P
CHUNK = 64
PAD = -N_META % CHUNK
NCHUNK = (T + PAD) // CHUNK
TP = NCHUNK * CHUNK
GH, GDK, GDV = 4, 128, 256
HEAD = 64
NORM_EPS = 1e-5
RWKV_GN_EPS = 64e-5
GATE_NORM = 16.0
DECAY_SCALE = float(np.exp(-0.5))
NE = 32
TOPK = 4
FE = 1024
LIMIT = 7.0
ALPHA = 1.702
SLOTS = 64
BLOCKS = SEQ // SLOTS
ITEMS = NE + SEQ * TOPK // SLOTS + 1
PIECE = 4096
RING = 6
LEVELS = 6

PARAMS = {}
_at = 0
for _name, _n in (("norm_mix_g", 8), ("b_gla_a", 4), ("gla_norm_g", 2), ("b_decay", 8), ("b_a", 8),
                  ("k_k", 8), ("r_k", 8), ("ln_x_g", 8), ("ln_x_b", 8), ("norm_ffn_g", 8),
                  ("mu_r", 8), ("mu_k", 8), ("mu_v", 8), ("mu_w", 1), ("mu_a", 1), ("mu_g", 2), ("k_a", 8)):
    PARAMS[_name] = _at
    _at += _n
NPARAM = _at
MU = PARAMS["mu_r"]

CONSTS = {}
_at = 0
for _name, _n in (("ident", P), ("ones", P), ("half_ones", P), ("half_ident", CHUNK), ("causal", 2 * CHUNK),
                  ("levels", LEVELS * CHUNK), ("scan", TP)):
    CONSTS[_name] = _at
    _at += _n
NCONST = _at
MOE_CONSTS = {}
_at = 0
for _name, _n in (("before", P), ("slot_ids", BLOCKS * 2 * SLOTS), ("row_id", 1), ("ids", P)):
    MOE_CONSTS[_name] = _at
    _at += _n
NMOE_CONST = _at


def constants():
    p = np.arange(P)[:, None]
    s, t = p % CHUNK, np.arange(CHUNK)[None, :]
    levels = []
    for l in range(LEVELS):
        b = 1 << l
        levels.append((t // (2 * b) == s // (2 * b)) & (t // b % 2 == 1) & (s // b % 2 == 0))
    scan = np.broadcast_to(np.arange(TP)[None, :] % CHUNK != 0, (P, TP))
    parts = [np.eye(P), np.ones((P, P)), p // HEAD == np.arange(P)[None, :] // HEAD, s == t,
             np.concatenate([s < t, s <= t], 1), *levels, scan]
    slots = np.tile(np.arange(SLOTS)[None, :], (P, 2))
    moe = [p < np.arange(P)[None, :], *[slots + SLOTS * b for b in range(BLOCKS)], p,
           np.broadcast_to(np.arange(P)[None, :], (P, P))]
    return (np.concatenate([np.asarray(x, np.float32) for x in parts], 1),
            np.concatenate([np.asarray(x, np.float32) for x in moe], 1))


def block_kernel(nc, A):
    f32, i32, u32 = mybir.dt.float32, mybir.dt.int32, mybir.dt.uint32
    ALU, ACT, AX = mybir.AluOpType, mybir.ActivationFunctionType, mybir.AxisListType
    ds = bass.ds

    with ExitStack() as ctx:
        ctx.enter_context(nc.allow_non_contiguous_dma("rows of a piece"))
        FLOATS = 53000
        arena = ctx.enter_context(nc.sbuf_tensor("arena", [P, FLOATS], f32))
        ps = ctx.enter_context(nc.psum_tensor("ps", [P, 8 * 512], f32))
        sems = {}

        def sem(name):
            if name not in sems:
                sems[name] = ctx.enter_context(nc.semaphore(name))
            return sems[name]

        def at(off, *shape):
            n = int(np.prod(shape))
            assert off + n <= FLOATS
            v = arena[:, off:off + n]
            if len(shape) == 2:
                v = v.rearrange("p (a b) -> p a b", a=shape[0])
            elif len(shape) == 3:
                v = v.rearrange("p (a b c) -> p a b c", a=shape[0], b=shape[1])
            return v

        def bank(b, *shape):
            n = int(np.prod(shape))
            v = ps[:, 512 * b:512 * b + n]
            if len(shape) == 2:
                v = v.rearrange("p (a b) -> p a b", a=shape[0])
            elif len(shape) == 3:
                v = v.rearrange("p (a b c) -> p a b c", a=shape[0], b=shape[1])
            return v

        used = [0]

        def take(n):
            used[0] += n
            return used[0] - n

        ring = [take(PIECE) for _ in range(RING)]
        o_h, o_u = take(KC * T), take(KC * T)
        o_late = take(GH * TP)
        o_gk = take(GH * TP)
        o_rb = take(KC * TP)
        take(3 * KC * SEQ - (2 * GH + KC) * TP)
        o_gv, o_ra, o_rk, o_rr, o_rv = (take(KC * TP) for _ in range(5))
        o_const, o_par, o_om = take(NCONST), take(NPARAM), take(NPARAM - MU)
        o_coefg, o_coefr, o_sg = take(GH * NCHUNK), take(KC * NCHUNK), take(2 * T)
        eps = at(take(4), 4)
        o_x = take(FLOATS - used[0])

        hT, uT = at(o_h, KC, T), at(o_u, KC, T)
        gq, gk, gv = at(o_late, GH, TP), at(o_gk, GH, TP), at(o_gv, KC, TP)
        ra, rb, rk, rr, rv = (at(o, KC, TP) for o in (o_ra, o_rb, o_rk, o_rr, o_rv))
        late = at(o_late, 3 * KC, SEQ)
        par = at(o_par, NPARAM)
        om = at(o_om, NPARAM - MU)

        def pcol(name, m=0, n=P):
            return par[0:n, PARAMS[name] + m:PARAMS[name] + m + 1]

        def omcol(name, m=0, n=P):
            c = PARAMS[name] - MU + m
            return om[0:n, c:c + 1]

        def const(name, n):
            return at(o_const + CONSTS[name], n)

        ident, ones, half_ones = const("ident", P), const("ones", P), const("half_ones", P)
        half_ident = const("half_ident", CHUNK)
        causal = const("causal", 2 * CHUNK)
        scan_mask = const("scan", TP)
        levels = at(o_const + CONSTS["levels"], LEVELS, CHUNK)
        coefg, coefr = at(o_coefg, GH, NCHUNK), at(o_coefr, KC, NCHUNK)
        sg = at(o_sg, 2, T)

        def piece(j, n, w):
            return at(ring[j], n, w)

        o_t = ring[4]
        w_decay2, w_a2, w_gla_a2 = at(o_t, D), at(o_t + D, D), at(o_t + 2 * D, GH * GDK)
        gaT, rwT, raT = (at(o_t + 2560 + i * T, T) for i in range(3))
        g_abs, g_min = at(o_t + 3376, GH, T), at(o_t + 4464, GH, T)
        rk_tmp = [[at(o_t + 5552 + (2 * j + i) * T, T) for j in range(2)] for i in range(2)]
        c_ar = at(o_t, KC, 2 * CHUNK)
        c_b, c_k, c_v = (at(o_t + 1024 + 512 * i, KC, CHUNK) for i in range(3))
        c_mb, c_mk = at(o_t + 2560, KC, 2 * CHUNK), at(o_t + 3584, KC, 2 * CHUNK)
        t_b, t_k, t_v = (at(o_t + 4608 + 512 * i, KC, CHUNK) for i in range(3))
        inv, invT, prod = (at(o_t + 6144 + 512 * i, KC, CHUNK) for i in range(3))
        c_nt = [at(o_t + 7680, KC, CHUNK), at(o_x, KC, CHUNK)]
        c_r, c_sa = c_v, c_k
        state = at(o_x + 512, KC, CHUNK)
        g_q, g_k = at(o_x + 1024, GH, CHUNK), at(o_x + 1280, GH, CHUNK)
        g_v = at(o_x + 1536, KC, CHUNK)
        g_a = at(o_x + 2048, GH, CHUNK)
        tg_k = at(o_x + 2304, GH * GDK)
        tg_v, g_state = at(o_h, GH * GDV), at(o_h + 1024, GH, GDV)
        assert o_x + 2816 <= FLOATS
        w_gate2 = at(o_x, 2, D)
        sq_g = at(o_u, KC, SEQ)
        g_std = at(o_x + 2 * D, GH, SEQ)
        rv_sq, rs1 = at(o_rv, KC, T), at(o_rk, T)
        h2T, u2T, rs2 = hT[:, :, N_META:], at(o_u, KC, SEQ), at(o_x + 2 * D, SEQ)

        mused = [o_gv]

        def mtake(n):
            mused[0] += n
            assert mused[0] <= o_gv + 5 * KC * TP
            return mused[0] - n

        u2 = at(mtake(2 * D), 2, D)
        acc = at(mtake(2 * D), 2, D)
        b_gu = at(mtake(2 * FE), 2 * FE)
        b_dn = at(mtake(D), D)
        g_fin = at(mtake(D), D)
        o_mc = mtake(NMOE_CONST)
        before = at(o_mc + MOE_CONSTS["before"], P)
        slot_ids = at(o_mc + MOE_CONSTS["slot_ids"], BLOCKS * 2 * SLOTS)
        row_id = at(o_mc + MOE_CONSTS["row_id"], 1)
        ids = at(o_mc + MOE_CONSTS["ids"], P)
        w_r = at(mtake(KC * NE), KC, NE)
        b_r = at(mtake(NE), NE)
        logits, chosen, comb, pos = (at(mtake(2 * NE), 2, NE) for _ in range(4))
        top = at(mtake(16), 2, 8)
        top_i = at(mtake(16), 2, 8)
        top_f = at(mtake(16), 2, 8)
        probs, negmax, psums = at(mtake(8), 2, 4), at(mtake(2), 2), at(mtake(2), 2)
        one_hot = at(mtake(NE), NE)
        count, extra, ends, cmp_e, cmp_x = (at(mtake(NE), NE) for _ in range(5))
        item_eb = at(mtake(2), 2)
        bc_e, bc_b = at(mtake(P), P), at(mtake(P), P)
        item_e = at(mtake(NE + P), NE + P)
        item_b = at(mtake(NE + P), NE + P)
        item_ei = at(mtake(NE + P), NE + P)
        item_bi = at(mtake(NE + P), NE + P)
        nitems = at(mtake(2), 2)
        combT = at(mtake(2 * P), 2, P)
        sel = at(mtake(SLOTS), SLOTS)
        gat = at(mtake(2 * SLOTS), 2, SLOTS)
        scat = at(mtake(4 * SLOTS), 2, 2 * SLOTS)
        lused = [o_late]

        def ltake(n):
            lused[0] += n
            assert lused[0] <= o_late + 3 * KC * SEQ
            return lused[0] - n

        scatT = at(ltake(2 * P), 2, P)
        xg = at(ltake(512), 512)
        xT = at(ltake(512), 4, 2, SLOTS)
        h_gate, h_sig, h_up = (at(ltake(512), 512) for _ in range(3))
        actT = at(ltake(512), 4, 2, SLOTS)
        ye = at(ltake(512), 512)
        fin = at(ltake(2 * D), 2, D)
        fss, frs = at(ltake(2), 2), at(ltake(2), 2)

        class Own:

            def __init__(self, eng, name):
                self.eng, self.sem, self.base, self.n = eng, sem(name), 0, 0

            def done(self, ins):
                ins.then_inc(self.sem, 1)
                self.n += 1

            def wait(self):
                self.eng.wait_ge(self.sem, self.base + self.n)

            def link(self, ins):
                self.done(ins)
                self.wait()

            def enter(self, i, per):
                self.start, self.n, self.per = self.n, 0, per
                self.base = self.start + i * per

            def leave(self, trips):
                assert self.n == self.per, (self.n, self.per)
                self.base, self.n = 0, self.start + trips * self.per

        PRODUCTS = {"h_sumsq": 1, "small_projected": 4, "gate_projected": 4, "lora_projected": 8, "key_sumsq": 1, "bonus_sum": 1, "y_sum": 1, "y_sumsq": 1, "g_sumsq": 1, "out_gate": 1, "h2_sumsq": 1, "logits": 1, "u2_turned": 2, "counted": 1, "h2_turned": 1, "comb_turned": 1, "dn_bias": 1, "items_spread": 1}

        def product(name, n=1):
            names = list(PRODUCTS)
            return sum(PRODUCTS[x] for x in names[:names.index(name)]) + n

        def apart(eng, name):
            eng.sem_inc(sem(name), 1)

        block = ctx.enter_context(nc.Block())
        A_ = A

        @block.sync
        def _(sp):
            sp.dma_start(hT[:, :, :], A_["hT"]).then_inc(sem("h_loaded"), 16)
            sp.dma_start(at(o_const, NCONST), A_["consts"]).then_inc(sem("params_loaded"), 16)
            sp.dma_start(par, A_["params"]).then_inc(sem("params_loaded"), 16)
            sp.dma_start(piece(0, KC, 304), A_["w_small"]).then_inc(sem("slot0"), 16)
            sp.dma_start(w_gla_a2[0:16, :], A_["w_gla_a2"]).then_inc(sem("lora_loaded"), 16)
            sp.dma_start(w_decay2[0:64, :], A_["w_decay2"]).then_inc(sem("lora_loaded"), 16)
            sp.dma_start(w_a2[0:64, :], A_["w_a2"]).then_inc(sem("lora_loaded"), 16)
            sp.dma_start(piece(1, KC, 512), A_["w_gla"][0]).then_inc(sem("slot1"), 16)
            sp.dma_start(piece(2, KC, 512), A_["w_gla"][1]).then_inc(sem("slot2"), 16)
            sp.dma_start(piece(3, KC, 384), A_["w_rwkv"][1]).then_inc(sem("slot3"), 16)
            sp.wait_ge(sem("slot0_free"), 1)
            sp.dma_start(piece(0, KC, 384), A_["w_rwkv"][0]).then_inc(sem("slot0"), 16)
            for h in (2, 3):
                j = 1 + h % 2
                sp.wait_ge(sem(f"slot{j}_free"), 1)
                sp.dma_start(piece(j, KC, 512), A_["w_gla"][h]).then_inc(sem(f"slot{j}"), 16)
            with sp.Fori(1, KC // 2) as i:
                for odd, j, first in ((0, 0, 1), (1, 3, 0)):
                    sp.wait_ge(sem(f"slot{j}_free"), first + i)
                    sp.dma_start(piece(j, KC, 384), A_["w_rwkv"][ds(2 * i + odd, 1)].rearrange("a p k n -> (a p) k n")
                                 ).then_inc(sem(f"slot{j}"), 16)
            with sp.Fori(0, 3) as i:
                for odd in range(2):
                    j = 1 + odd
                    sp.wait_ge(sem(f"slot{j}_free"), 2 + i)
                    sp.dma_start(piece(j, KC, 512), A_["w_mid"][ds(2 * i + odd, 1)].rearrange("a p k n -> (a p) k n")
                                 ).then_inc(sem(f"slot{j}"), 16)
            with sp.Fori(0, 3) as i:
                for odd, j, first in ((0, 0, 5), (1, 3, 4)):
                    sp.wait_ge(sem(f"slot{j}_free"), first + i)
                    sp.dma_start(piece(j, KC, 512), A_["w_mid"][ds(6 + 2 * i + odd, 1)].rearrange("a p k n -> (a p) k n")
                                 ).then_inc(sem(f"slot{j}"), 16)
            FREE = {0: 8, 1: 5, 2: 5, 3: 7, 4: 0, 5: 0}
            sp.wait_ge(sem("state_product"), NCHUNK)
            sp.wait_ge(sem("state_ready"), NCHUNK)
            sp.wait_ge(sem("y_stored"), NCHUNK)
            for j in (1, 2, 4, 5, 0, 3):
                if FREE[j]:
                    sp.wait_ge(sem(f"slot{j}_free"), FREE[j])
                if j < 4:
                    src = A_["w_gu"][0, 256 * j:256 * j + 256, :].rearrange("(k p) n -> p k n", p=P)
                    sp.dma_start(piece(j, 2, 2048), src).then_inc(sem(f"slot{j}"), 16)
                else:
                    src = A_["w_dn"][0, 512 * (j - 4):512 * (j - 4) + 512, :].rearrange("(k p) n -> p k n", p=P)
                    sp.dma_start(piece(j, 4, 1024), src).then_inc(sem(f"slot{j}"), 16)
            sp.wait_ge(sem("items_ready"), 1)
            n_items = sp.value_load(nitems.bitcast(i32)[0:1, 0:1], min_val=NE, max_val=ITEMS)
            with sp.Fori(1, n_items) as w:
                e = sp.value_load(item_ei.bitcast(i32)[0:1, ds(w, 1)], min_val=0, max_val=NE - 1)
                for j in range(RING):
                    sp.wait_ge(sem(f"slot{j}_free"), w + FREE[j])
                    if j < 4:
                        src = A_["w_gu"][ds(e, 1), 256 * j:256 * j + 256, :].rearrange("a (k p) n -> (a p) k n", p=P)
                        sp.dma_start(piece(j, 2, 2048), src).then_inc(sem(f"slot{j}"), 16)
                    else:
                        src = A_["w_dn"][ds(e, 1), 512 * (j - 4):512 * (j - 4) + 512, :].rearrange(
                            "a (k p) n -> (a p) k n", p=P)
                        sp.dma_start(piece(j, 4, 1024), src).then_inc(sem(f"slot{j}"), 16)
            sp.wait_ge(sem("final_ready"), 2)
            sp.dma_start(A_["out"].rearrange("(a p) d -> p a d", p=P), fin[:, :, :]).then_inc(sem("stored"), 16)
            sp.wait_ge(sem("stored"), 16)

        @block.tensor
        def _(pe):
            mm, tr = nc.tensor.matmul, nc.tensor.transpose

            def project(dst, lhs, rhs):
                for k in range(KC):
                    last = mm(dst, lhs(k), rhs(k), start=(k == 0), stop=(k == KC - 1))
                return last

            pe.wait_ge(sem("params_loaded"), 32)
            pe.wait_ge(sem("h_squared"), 1)
            project(bank(0, T), lambda k: ones, lambda k: rv_sq[:, k, :]).then_inc(sem("product"), 1)
            pe.wait_ge(sem("slot0"), 16)
            pe.wait_ge(sem("u_ready"), KC)
            small = piece(0, KC, 304)
            for b, (c0, n) in enumerate(((0, 16), (16, 64), (80, 64), (144, 128), (272, 32))):
                last = project(bank(1 + b, T)[0:n, :], lambda k: small[:, k, c0:c0 + n], lambda k: uT[:, k, :])
                last.then_inc(sem("product" if b < 4 else "slot0_free"), 1)
            pe.wait_ge(sem("lora_loaded"), 48)
            pe.wait_ge(sem("ga_ready"), 1)
            pe.wait_ge(sem("small_evacuated"), 4)
            for h in range(GH):
                mm(bank(h, T), w_gla_a2[0:16, P * h:P * h + P], gaT[0:16, :], start=True, stop=True
                   ).then_inc(sem("product"), 1)
            pe.wait_ge(sem("rw_ready"), 1)
            for m in range(KC):
                b = 4 + 2 * (m % 2)
                if m >= 2:
                    pe.wait_ge(sem("lora_evacuated"), 2 * (m - 1))
                mm(bank(b, T), w_decay2[0:64, P * m:P * m + P], rwT[0:64, :], start=True, stop=True)
                mm(bank(b + 1, T), w_a2[0:64, P * m:P * m + P], raT[0:64, :], start=True, stop=True
                   ).then_inc(sem("product"), 1)
            pe.wait_ge(sem("gate_read"), GH)
            pe.wait_ge(sem("gate_min_read"), GH)
            pe.wait_ge(sem("lora_evacuated"), 2 * KC)
            with pe.Fori(0, 2) as i:
                for odd in range(2):
                    w = piece(1 + odd, KC, 512)
                    pe.wait_ge(sem(f"slot{1 + odd}"), 16 * i + 16)
                    pe.wait_ge(sem("gla_v_evacuated"), 2 * i + 0)
                    pe.wait_ge(sem("gla_qk_evacuated"), 2 * i + 0)
                    for b in range(4):
                        last = project(bank(4 * odd + b, T), lambda k: w[:, k, P * b:P * b + P], lambda k: uT[:, k, :])
                        last.then_inc(sem("gla_projected" if b < 3 else f"slot{1 + odd}_free"), 1)
            pe.wait_ge(sem("gla_v_evacuated"), GH)
            pe.wait_ge(sem("gla_qk_evacuated"), GH)
            with pe.Fori(0, KC // 2) as i:
                for odd, j in ((0, 0), (1, 3)):
                    w = piece(j, KC, 384)
                    pe.wait_ge(sem(f"slot{j}"), 16 * i + (32 if j == 0 else 16))
                    pe.wait_ge(sem("rkv_evacuated"), 2 * i)
                    for b in range(3):
                        last = project(bank(4 * odd + b, T), lambda k: w[:, k, P * b:P * b + P], lambda k: uT[:, k, :])
                        last.then_inc(sem("rkv_projected" if b < 2 else f"slot{j}_free"), 1)
            pe.wait_ge(sem("rkv_evacuated"), KC)
            pe.wait_ge(sem("key_squared"), KC)
            for m in range(KC):
                last = mm(bank(m, T), half_ones, hT[:, m, :], start=True, stop=True)
            last.then_inc(sem("product"), 1)

            halves = (slice(0, 64), slice(64, 128))
            pairs = [(m, h) for m in range(KC) for h in halves]
            pe.wait_ge(sem("key_norm_read"), 1)
            with pe.Fori(0, NCHUNK) as c:
                pe.wait_ge(sem("staged_dve"), c + 1)
                pe.wait_ge(sem("staged_act"), c + 1)
                pe.wait_ge(sem("g_state_ready"), c)
                apart(pe, "pe_passed")
                for m, h in pairs:
                    last = mm(bank(0, KC, 2 * CHUNK)[h, m, :], c_b[h, m, :], c_ar[h, m, :], start=True, stop=True)
                last.then_inc(sem("scores_b"), 1)
                pe.wait_ge(sem("tg_k_ready"), c)
                pe.wait_ge(sem("g_out_stored"), c)
                apart(pe, "pe_passed")
                for m, h in pairs:
                    last = mm(bank(2, KC, 2 * CHUNK)[h, m, :], c_k[h, m, :], c_ar[h, m, :], start=True, stop=True)
                last.then_inc(sem("scores_k"), 1)
                for b, src, busy in ((4, c_b, "y_stored"), (5, c_k, "state_ready"), (6, c_v, "rhs_ready")):
                    pe.wait_ge(sem(busy), c)
                    apart(pe, "pe_passed")
                    for m, h in pairs:
                        last = mm(bank(b, KC, CHUNK)[h, m, :], src[h, m, :], half_ident[h, :], start=True, stop=True)
                    last.then_inc(sem("turned"), 1)
                pe.wait_ge(sem("invT_ready"), LEVELS * c + 1)
                pe.wait_ge(sem("sa_ready"), c)
                apart(pe, "pe_passed")
                for m, h in pairs:
                    last = mm(bank(7, KC, CHUNK)[h, m, :], invT[h, m, :], half_ident[h, :], start=True, stop=True)
                last.then_inc(sem("inv_turned"), 1)
                pe.wait_ge(sem("staged_pool"), c + 1)
                pe.wait_ge(sem("mask_b_done"), c + 1)
                apart(pe, "pe_passed")
                for u in range(KC):
                    last = tr(bank(0, KC, P)[0:64, u, :], g_v[:, u, :], ident)
                last.then_inc(sem("g_v_turned"), 1)
                pe.wait_ge(sem("mask_k_done"), c + 1)
                apart(pe, "pe_passed")
                for h in range(GH):
                    last = tr(bank(2, GH, P)[0:64, h, :], g_k[:, h, :], ident)
                last.then_inc(sem("g_k_turned"), 1)
                for h in range(GH):
                    last = mm(bank(3, GH, CHUNK)[0:64, h, :], g_k[:, h, :], g_q[:, h, :], start=True, stop=True)
                last.then_inc(sem("g_scores"), 1)
                pe.wait_ge(sem("turned_read"), 3 * c + 3)
                pe.wait_ge(sem("state_ready"), c)
                apart(pe, "pe_passed")
                for m, h in pairs:
                    mm(bank(6, KC, CHUNK)[h, m, :], c_ar[h, m, 0:CHUNK], state[h, m, :], start=True, stop=False)
                    last = mm(bank(6, KC, CHUNK)[h, m, :], c_mk[h, m, 0:CHUNK], t_v[h, m, :], start=False, stop=True)
                last.then_inc(sem("rhs_product"), 1)
                for l in range(1, LEVELS):
                    pe.wait_ge(sem("level_ready"), (LEVELS - 1) * c + l)
                    if l == 1:
                        pe.wait_ge(sem("inv_first"), c + 1)
                    else:
                        pe.wait_ge(sem("inv_ready"), (LEVELS - 2) * c + l - 1)
                    apart(pe, "pe_passed")
                    for m, h in pairs:
                        last = mm(bank(7, KC, CHUNK)[h, m, :], c_nt[l % 2][h, m, :], inv[h, m, :], start=True, stop=True)
                    last.then_inc(sem("level_product"), 1)
                    if l == 2:
                        pe.wait_ge(sem("g_a_ready"), c + 1)
                        pe.wait_ge(sem("g_state_ready"), c)
                        apart(pe, "pe_passed")
                        for u in range(KC):
                            mm(bank(3, KC, CHUNK)[:, u, :], tg_v[0:64, P * u:P * u + P], g_a[0:64, u // 2, :],
                               start=True, stop=False)
                            last = mm(bank(3, KC, CHUNK)[:, u, :], g_state[:, u // 2, P * (u % 2):P * (u % 2) + P],
                                      g_q[:, u // 2, :], start=False, stop=True)
                        last.then_inc(sem("g_out"), 1)
                        for h in range(GH):
                            last = mm(bank(0, GH, GDV)[:, h, :], tg_k[0:64, P * h:P * h + P],
                                      tg_v[0:64, GDV * h:GDV * h + GDV], start=True, stop=True)
                        last.then_inc(sem("g_increment"), 1)
                    pe.wait_ge(sem("prod_ready"), (LEVELS - 1) * c + l)
                    pe.wait_ge(sem("invT_ready"), LEVELS * c + l)
                    apart(pe, "pe_passed")
                    if l < LEVELS - 1:
                        for m, h in pairs:
                            last = mm(bank(4, KC, CHUNK)[h, m, :], invT[h, m, :], prod[h, m, :], start=True, stop=True)
                        last.then_inc(sem("inv_step"), 1)
                    for m, h in pairs:
                        last = mm(bank(5, KC, CHUNK)[h, m, :], prod[h, m, :], invT[h, m, :], start=True, stop=True)
                    last.then_inc(sem("invT_step"), 1)
                pe.wait_ge(sem("invT_ready"), LEVELS * c + LEVELS)
                pe.wait_ge(sem("rhs_ready"), c + 1)
                apart(pe, "pe_passed")
                for m, h in pairs:
                    last = mm(bank(7, KC, CHUNK)[h, m, :], invT[h, m, :], c_r[h, m, :], start=True, stop=True)
                last.then_inc(sem("sa_product"), 1)
                pe.wait_ge(sem("sa_ready"), c + 1)
                apart(pe, "pe_passed")
                for m, h in pairs:
                    mm(bank(4, KC, CHUNK)[h, m, :], state[h, m, :], c_ar[h, m, CHUNK:], start=True, stop=False)
                    mm(bank(4, KC, CHUNK)[h, m, :], c_sa[h, m, :], c_mb[h, m, CHUNK:], start=False, stop=False)
                    last = mm(bank(4, KC, CHUNK)[h, m, :], t_v[h, m, :], c_mk[h, m, CHUNK:], start=False, stop=True)
                last.then_inc(sem("y_product"), 1)
                for m, h in pairs:
                    mm(bank(5, KC, CHUNK)[h, m, :], t_b[h, m, :], c_sa[h, m, :], start=True, stop=False)
                    last = mm(bank(5, KC, CHUNK)[h, m, :], t_k[h, m, :], t_v[h, m, :], start=False, stop=True)
                last.then_inc(sem("state_product"), 1)

            now = slice(N_META, T)
            real = slice(CHUNK, TP)
            for name in ("g_state_ready", "g_out_stored", "y_stored", "state_ready"):
                pe.wait_ge(sem(name), NCHUNK)
            with pe.Fori(0, 3) as i:
                for odd in range(2):
                    w = piece(1 + odd, KC, 512)
                    pe.wait_ge(sem(f"slot{1 + odd}"), 16 * i + 48)
                    pe.wait_ge(sem("late_evacuated"), 2 * i)
                    for b in range(4):
                        last = project(bank(4 * odd + b, SEQ), lambda k: w[:, k, P * b:P * b + P],
                                       lambda k: uT[:, k, now])
                        last.then_inc(sem("late_projected" if b < 3 else f"slot{1 + odd}_free"), 1)
            pe.wait_ge(sem("late_evacuated"), 6)
            pe.wait_ge(sem("bonus_in"), 1)
            for m in range(KC):
                last = mm(bank(0, KC, SEQ)[:, m, :], half_ones, rr[:, m, real], start=True, stop=True)
            last.then_inc(sem("product"), 1)
            for m in range(KC):
                last = mm(bank(4, KC, SEQ)[:, m, :], half_ones, ra[:, m, real], start=True, stop=True)
            last.then_inc(sem("product"), 1)
            pe.wait_ge(sem("bonus_done"), 1)
            pe.wait_ge(sem("y_squared"), 1)
            for m in range(KC):
                last = mm(bank(0, KC, SEQ)[:, m, :], half_ones, rr[:, m, real], start=True, stop=True)
            last.then_inc(sem("product"), 1)
            pe.wait_ge(sem("y_centred"), 1)
            pe.wait_ge(sem("g_squared"), 1)
            for h in range(GH):
                for w in range(2):
                    last = mm(bank(4, GH, SEQ)[:, h, :], ones, sq_g[:, 2 * h + w, :], start=(w == 0), stop=(w == 1))
            last.then_inc(sem("product"), 1)
            pe.wait_ge(sem("gate2_loaded"), 32)
            pe.wait_ge(sem("y_std"), 1)
            for m in range(KC):
                mm(bank(0, KC, SEQ)[:, m, :], w_gate2[:, 0, P * m:P * m + P], sg[:, 0, now], start=True, stop=False)
                last = mm(bank(0, KC, SEQ)[:, m, :], w_gate2[0:32, 1, P * m:P * m + P], sg[0:32, 1, now],
                          start=False, stop=True)
            last.then_inc(sem("product"), 1)
            for n, (src, ready) in enumerate(((gv, "g_branch"), (ra, "r_branch"), (rr, "mixed"))):
                pe.wait_ge(sem(ready), 1)
                if n == 0:
                    pe.wait_ge(sem("g_std"), 1)
                for odd, j, first in ((0, 0, 6), (1, 3, 5)):
                    w = piece(j, KC, 512)
                    pe.wait_ge(sem(f"slot{j}"), 16 * (first + n - (0 if j == 0 else 0)))
                    b0 = (4, 0, 4)[n] + 2 * odd
                    for u in range(4):
                        last = project(bank(b0, 4, SEQ)[:, u, :], lambda k: w[:, k, P * u:P * u + P],
                                       lambda k: src[:, k, real])
                    last.then_inc(sem(f"slot{j}_free"), 1)
            pe.wait_ge(sem("h2_squared"), 1)
            project(bank(0, SEQ), lambda k: ones, lambda k: rv[:, k, real]).then_inc(sem("product"), 1)
            pe.wait_ge(sem("u2_ready"), KC)
            pe.wait_ge(sem("moe_loaded"), 96)
            for blk in range(2):
                for k in range(KC):
                    mm(bank(1, 2, NE)[:, blk, :], u2T[:, k, P * blk:P * blk + P], w_r[:, k, :],
                       start=(k == 0), stop=False)
                last = mm(bank(1, 2, NE)[:, blk, :], ones[0:1, :], b_r[0:1, :], start=False, stop=True)
            last.then_inc(sem("product"), 1)
            for blk in range(2):
                for k in range(KC):
                    last = tr(bank(4 + 2 * blk, KC, P)[:, k, :], u2T[:, k, P * blk:P * blk + P], ident)
                last.then_inc(sem("product"), 1)
            pe.wait_ge(sem("chosen_ready"), 1)
            mm(bank(0, 3, NE)[:, 0, :], before, chosen[:, 0, :], start=True, stop=True)
            mm(bank(0, 3, NE)[:, 1, :], ones, chosen[:, 0, :], start=True, stop=False)
            mm(bank(0, 3, NE)[:, 1, :], before, chosen[:, 1, :], start=False, stop=True)
            mm(bank(0, 3, NE)[:, 2, :], ones, chosen[:, 0, :], start=True, stop=False)
            mm(bank(0, 3, NE)[:, 2, :], ones, chosen[:, 1, :], start=False, stop=True).then_inc(sem("product"), 1)
            pe.wait_ge(sem("u2_kept"), 2)
            for blk in range(2):
                for k in range(KC):
                    last = tr(bank(4 + 2 * blk, KC, P)[:, k, :], h2T[:, k, P * blk:P * blk + P], ident)
            last.then_inc(sem("product"), 1)
            for blk in range(2):
                last = tr(bank(2, 2, P)[0:NE, blk, :], comb[:, blk, :], ident)
            last.then_inc(sem("product"), 1)
            pe.wait_ge(sem("combT_ready"), 1)
            pe.wait_ge(sem("h2_kept"), 2)
            for blk in range(2):
                for half in range(2):
                    last = mm(bank(4 + 2 * blk + half, 512), combT[0:NE, blk, :], b_dn[0:NE, 512 * half:512 * half + 512],
                              start=True, stop=True)
            last.then_inc(sem("product"), 1)
            pe.wait_ge(sem("extra_items"), 1)
            mm(bank(3, 2, P)[:, 0, :], bc_e, ident, start=True, stop=True)
            mm(bank(3, 2, P)[:, 1, :], bc_b, ident, start=True, stop=True).then_inc(sem("product"), 1)

            def gather(n):
                pe.wait_ge(sem("gather_ready"), n)
                for blk in range(2):
                    for half in range(2):
                        last = mm(bank(2, 512)[64 * half:64 * half + 64, :], gat[:, blk, :],
                                  u2[:, blk, 512 * half:512 * half + 512], start=(blk == 0), stop=(blk == 1))
                last.then_inc(sem("gathered"), 1)

            def turn_x(n):
                pe.wait_ge(sem("xg_ready"), n)
                for q in range(4):
                    last = tr(bank(3, 4, P)[:, q, :], xg[:, P * q:P * q + P], ident)
                last.then_inc(sem("x_turned"), 1)

            def scatter():
                for blk in range(2):
                    for half in range(2):
                        h = slice(64 * half, 64 * half + 64)
                        last = mm(bank(4 + 2 * blk + half, 512), scatT[h, blk, :], ye[h, :], start=True, stop=True)
                last.then_inc(sem("scattered"), 1)

            pe.wait_ge(sem("combT_ready"), 1)
            pe.wait_ge(sem("items_kept"), 1)
            pe.wait_ge(sem("bias_added"), 1)
            gather(1)
            turn_x(1)
            pe.wait_ge(sem("loop_buffers"), 1)
            n_items = pe.value_load(nitems.bitcast(i32)[0:1, 0:1], min_val=NE, max_val=ITEMS)
            with pe.Fori(0, n_items) as w:
                pe.wait_ge(sem("x_ready"), w + 1)
                pe.wait_ge(sem("select_ready"), w + 1)
                pe.wait_ge(sem("act_ready"), w)
                for b in range(2):
                    for half in range(2):
                        mm(bank(b, 512)[64 * half:64 * half + 64, :], sel, b_gu[:, FE * b + 512 * half:FE * b + 512 * half + 512],
                           start=True, stop=False)
                for k in range(KC):
                    j, first = k // 2, (8, 5, 5, 7)[k // 2]
                    if k % 2 == 0:
                        pe.wait_ge(sem(f"slot{j}"), 16 * w + 16 * (first + 1))
                    wk = piece(j, 2, 2048)
                    for b in range(2):
                        for half in range(2):
                            last = mm(bank(b, 512)[64 * half:64 * half + 64, :], xT[:, k % 4, k // 4, :],
                                      wk[:, k % 2, FE * b + 512 * half:FE * b + 512 * half + 512],
                                      start=False, stop=(k == KC - 1))
                    if k % 2:
                        last.then_inc(sem(f"slot{j}_free"), 1)
                pe.wait_ge(sem("ye_ready"), w)
                pe.wait_ge(sem("scatT_ready"), w)
                pe.wait_ge(sem("acc_added"), w)
                scatter()
                gather(w + 2)
                turn_x(w + 2)
                pe.wait_ge(sem("acc_added"), w + 1)
                for blk in range(2):
                    last = tr(bank(4, 2, P)[:, blk, :], scat[:, blk, :], ident)
                last.then_inc(sem("scat_turned"), 1)
                pe.wait_ge(sem("act_ready"), w + 1)
                for q in range(4):
                    last = tr(bank(2, 4, P)[:, q, :], h_up[:, P * q:P * q + P], ident)
                last.then_inc(sem("act_turned"), 1)
                pe.wait_ge(sem("actT_ready"), w + 1)
                pe.wait_ge(sem("x_ready"), w + 2)
                for k in range(KC):
                    j = 4 + k // 4
                    if k % 4 == 0:
                        pe.wait_ge(sem(f"slot{j}"), 16 * w + 16)
                    wk = piece(j, 4, 1024)
                    for half in range(2):
                        last = mm(bank(3, 512)[64 * half:64 * half + 64, :], actT[:, k % 4, k // 4, :],
                                  wk[:, k % 4, 512 * half:512 * half + 512], start=(k == 0), stop=(k == KC - 1))
                    if k % 4 == 3:
                        last.then_inc(sem(f"slot{j}_free"), 1)
            pe.wait_ge(sem("ye_ready"), n_items)
            pe.wait_ge(sem("scatT_ready"), n_items)
            pe.wait_ge(sem("acc_added"), n_items)
            scatter()

        @block.scalar
        def _(act):
            own = Own(act, "act_own")
            f = nc.scalar.activation
            act.wait_ge(sem("h_loaded"), 16)
            f(rv_sq, hT, ACT.Square).then_inc(sem("h_squared"), 1)
            act.wait_ge(sem("dve_eps"), 1)
            act.wait_ge(sem("product"), product("h_sumsq", 1))
            f(rs1, bank(0, T), ACT.Sqrt, scale=1.0 / D, bias=eps[:, 0:1]).then_inc(sem("h_std"), 1)
            act.wait_ge(sem("one_minus"), 1)
            act.wait_ge(sem("product"), product("small_projected", 1))
            f(gaT[0:16, :], bank(1, T)[0:16, :], ACT.Copy).then_inc(sem("ga_ready"), 1)
            smalls = ((rwT, 64, "mu_w", 0), (raT, 64, "mu_a", 0), (sg[:, 0, :], 128, "mu_g", 0), (sg[:, 1, :], 32, "mu_g", 1))
            for n, (dst, rows, mu, m) in enumerate(smalls):
                if n < 3:
                    act.wait_ge(sem("product"), product("small_projected", n + 2))
                else:
                    act.wait_ge(sem("slot0_free"), 1)
                f(dst[0:rows, :], bank(2 + n, T)[0:rows, :], ACT.Copy, scale=omcol(mu, m, rows)).then_inc(sem("small_part"), 1)
            for h in range(GH):
                act.wait_ge(sem("product"), product("gate_projected", h + 1))
                f(g_abs[:, h, :], bank(h, T), ACT.Abs, bias=pcol("b_gla_a", h)).then_inc(sem("gate_read"), 1)
            act.wait_ge(sem("gate_read"), GH)
            own.link(f(g_abs, g_abs, ACT.Exp, scale=-1.0))
            f(g_abs, g_abs, ACT.Ln, bias=eps[:, 2:3]).then_inc(sem("gate_log"), 1)
            act.wait_ge(sem("small_evacuated"), 4)
            own.link(f(rwT[0:64, :], rwT[0:64, :], ACT.Tanh))
            f(sg[:, 0, :], sg[:, 0, :], ACT.Sigmoid).then_inc(sem("rw_ready"), 1)
            own.done(f(sg[0:32, 1, :], sg[0:32, 1, :], ACT.Sigmoid))
            act.wait_ge(sem("pads_cleared"), 1)
            for m in range(KC):
                act.wait_ge(sem("product"), product("lora_projected", m + 1))
                b = 4 + 2 * (m % 2)
                f(ra[:, m, PAD:], bank(b, T), ACT.Sigmoid, bias=pcol("b_decay", m)).then_inc(sem("lora_evacuated"), 1)
                f(rb[:, m, PAD:], bank(b + 1, T), ACT.Sigmoid, bias=pcol("b_a", m)).then_inc(sem("lora_evacuated"), 1)
            act.wait_ge(sem("g_log_decay"), 1)
            f(gk, gq, ACT.Exp, scale=-1.0 / GATE_NORM).then_inc(sem("g_decay"), 1)
            act.wait_ge(sem("g_decay"), 1)
            f(gq, gq, ACT.Exp, scale=1.0 / GATE_NORM).then_inc(sem("g_decay"), 1)
            f(coefg, coefg, ACT.Exp, scale=1.0 / GATE_NORM).then_inc(sem("g_decay"), 1)
            act.wait_ge(sem("r_log_decay"), 1)
            f(rr, rk, ACT.Exp, scale=-DECAY_SCALE).then_inc(sem("r_decay"), 1)
            act.wait_ge(sem("r_decay"), 1)
            f(rk, rk, ACT.Exp, scale=DECAY_SCALE).then_inc(sem("r_decay"), 1)
            f(ra, ra, ACT.Exp, scale=-DECAY_SCALE).then_inc(sem("r_decay"), 1)
            f(coefr, coefr, ACT.Exp, scale=-DECAY_SCALE).then_inc(sem("r_decay"), 1)
            with act.Fori(0, 2) as i:
                for odd in range(2):
                    act.wait_ge(sem(f"slot{1 + odd}_free"), i + 1)
                    apart(act, "act_passed")
                    for u in range(2):
                        ins = f(gv[:, ds(4 * i + 2 * odd + u, 1), PAD:].rearrange("p a t -> p (a t)"),
                                bank(4 * odd + 2 + u, T), ACT.Copy)
                    ins.then_inc(sem("gla_v_evacuated"), 1)
            act.wait_ge(sem("rv_free"), 1)
            with act.Fori(0, KC // 2) as i:
                own.enter(i, 2)
                for odd, j in ((0, 0), (1, 3)):
                    act.wait_ge(sem("rkv_projected"), 4 * i + 2 * odd + 1)
                    rt, kt = rk_tmp[odd]
                    m = 2 * i + odd
                    act.wait_ge(sem("rkv_evacuated"), 2 * i)
                    apart(act, "act_passed")
                    f(rt, bank(4 * odd, T), ACT.Copy, scale=om[:, ds(m + PARAMS["mu_r"] - MU, 1)]).then_inc(sem("rkv_part"), 1)
                    act.wait_ge(sem("rkv_projected"), 4 * i + 2 * odd + 2)
                    apart(act, "act_passed")
                    f(kt, bank(4 * odd + 1, T), ACT.Copy, scale=om[:, ds(m + PARAMS["mu_k"] - MU, 1)]).then_inc(sem("rkv_part"), 1)
                    act.wait_ge(sem(f"slot{j}_free"), i + (2 if j == 0 else 1))
                    apart(act, "act_passed")
                    f(rv[:, ds(m, 1), PAD:].rearrange("p a t -> p (a t)"), bank(4 * odd + 2, T), ACT.Copy,
                      scale=om[:, ds(m + PARAMS["mu_v"] - MU, 1)]).then_inc(sem("rkv_part"), 1)
                    act.wait_ge(sem("key_lerped"), 2 * i + odd + 1)
                    apart(act, "act_passed")
                    own.done(f(hT[:, ds(m, 1), :].rearrange("p a t -> p (a t)"), kt, ACT.Copy, scale=par[:, ds(m + PARAMS["k_k"], 1)]))
                    own.wait()
                    apart(act, "act_passed")
                    f(hT[:, ds(m, 1), :].rearrange("p a t -> p (a t)"), hT[:, ds(m, 1), :].rearrange("p a t -> p (a t)"),
                      ACT.Square).then_inc(sem("key_squared"), 1)
            own.leave(KC // 2)
            act.wait_ge(sem("product"), product("key_sumsq", 1))
            for m in range(KC):
                ins = f(hT[:, m, :], bank(m, T), ACT.Sqrt)
            ins.then_inc(sem("key_norm_read"), 1)

            act.wait_ge(sem("factors_done"), 1)
            with act.Fori(0, NCHUNK) as c:
                cols = ds(CHUNK * c, CHUNK)
                act.wait_ge(sem("state_product"), c)
                apart(act, "act_passed")
                f(c_k, rk[:, :, cols], ACT.Copy)
                f(c_v, rv[:, :, cols], ACT.Copy).then_inc(sem("staged_act"), 1)
                for n, (b, dst) in enumerate(((4, t_b), (5, t_k), (6, t_v))):
                    act.wait_ge(sem("turned"), 3 * c + n + 1)
                    f(dst, bank(b, KC, CHUNK), ACT.Copy).then_inc(sem("turned_read"), 1)
                act.wait_ge(sem("inv_turned"), c + 1)
                f(inv, bank(7, KC, CHUNK), ACT.Copy).then_inc(sem("inv_first"), 1)
                act.wait_ge(sem("g_v_turned"), c + 1)
                act.wait_ge(sem("g_increment"), c)
                f(tg_v[0:64, :], bank(0, GH * GDV)[0:64, :], ACT.Copy).then_inc(sem("tg_v_ready"), 1)
                act.wait_ge(sem("g_k_turned"), c + 1)
                f(tg_k[0:64, :], bank(2, GH * GDK)[0:64, :], ACT.Copy).then_inc(sem("tg_k_ready"), 1)
                act.wait_ge(sem("g_scores"), c + 1)
                f(g_a[0:64, :, :], bank(3, GH, CHUNK)[0:64, :, :], ACT.Copy).then_inc(sem("g_scores_read"), 1)
                act.wait_ge(sem("rhs_product"), c + 1)
                f(c_r, bank(6, KC, CHUNK), ACT.Copy).then_inc(sem("rhs_ready"), 1)
                for l in range(1, LEVELS):
                    act.wait_ge(sem("level_product"), (LEVELS - 1) * c + l)
                    f(prod, bank(7, KC, CHUNK), ACT.Copy).then_inc(sem("prod_ready"), 1)
                    if l == 2:
                        act.wait_ge(sem("g_out"), c + 1)
                        apart(act, "act_passed")
                        f(gv[:, :, cols], bank(3, KC, CHUNK), ACT.Copy).then_inc(sem("g_out_stored"), 1)
                act.wait_ge(sem("sa_product"), c + 1)
                f(c_sa, bank(7, KC, CHUNK), ACT.Copy).then_inc(sem("sa_ready"), 1)
                act.wait_ge(sem("y_product"), c + 1)
                apart(act, "act_passed")
                f(ra[:, :, cols], bank(4, KC, CHUNK), ACT.Copy).then_inc(sem("y_stored"), 1)

            real = slice(CHUNK, TP)
            act.wait_ge(sem("state_product"), NCHUNK)
            act.wait_ge(sem("state_ready"), NCHUNK)
            act.wait_ge(sem("g_state_ready"), NCHUNK)
            act.dma_start(w_gate2[:, 0, :], A_["w_gate2"][0:128, :]).then_inc(sem("gate2_loaded"), 16)
            act.dma_start(w_gate2[0:32, 1, :], A_["w_gate2"][128:160, :]).then_inc(sem("gate2_loaded"), 16)
            act.dma_start(hT[:, :, :], A_["hT"]).then_inc(sem("h_loaded"), 16)
            with act.Fori(0, 3) as i:
                for odd in range(2):
                    for b in range(4):
                        if b < 3:
                            act.wait_ge(sem("late_projected"), 6 * i + 3 * odd + b + 1)
                        else:
                            act.wait_ge(sem(f"slot{1 + odd}_free"), i + 3)
                        apart(act, "act_passed")
                        ins = f(late[:, ds(8 * i + 4 * odd + b, 1), :].rearrange("p a t -> p (a t)"),
                                bank(4 * odd + b, SEQ), ACT.Copy)
                    ins.then_inc(sem("late_evacuated"), 1)
            act.wait_ge(sem("late_evacuated"), 6)
            f(sq_g, gv[:, :, real], ACT.Square).then_inc(sem("g_squared"), 1)
            act.wait_ge(sem("y_centred"), 1)
            act.wait_ge(sem("product"), product("bonus_sum", 1))
            f(rr[:, :, real], ra[:, :, real], ACT.Square).then_inc(sem("y_squared"), 1)
            act.wait_ge(sem("product"), product("y_sumsq", 1))
            f(rk[:, :, real], bank(0, KC, SEQ), ACT.Sqrt, scale=1.0 / HEAD, bias=eps[:, 1:2]).then_inc(sem("y_std"), 1)
            act.wait_ge(sem("product"), product("g_sumsq", 1))
            f(g_std, bank(4, GH, SEQ), ACT.Sqrt, scale=1.0 / GDV, bias=eps[:, 0:1]).then_inc(sem("g_std"), 1)
            f(sq_g, late[:, 0:KC, :], ACT.Sigmoid).then_inc(sem("r_sigmoid"), 1)
            f(late[:, KC:, :], late[:, KC:, :], ACT.Sigmoid).then_inc(sem("gates_ready"), 1)
            act.wait_ge(sem("y_normed"), 1)
            for m in range(KC):
                ins = f(ra[:, m, real], ra[:, m, real], ACT.Identity, scale=pcol("ln_x_g", m), bias=pcol("ln_x_b", m))
            ins.then_inc(sem("y_affine"), 1)
            act.wait_ge(sem("h2_ready"), 2)
            f(rv[:, :, real], h2T, ACT.Square).then_inc(sem("h2_squared"), 1)
            act.wait_ge(sem("product"), product("h2_sumsq", 1))
            f(rs2, bank(0, SEQ), ACT.Sqrt, scale=1.0 / D, bias=eps[:, 0:1]).then_inc(sem("h2_std"), 1)
            act.wait_ge(sem("product"), product("h2_sumsq", 1))
            act.wait_ge(sem("b_gu_cleared"), 1)
            act.dma_start(w_r[:, :, :], A_["w_router"]).then_inc(sem("moe_loaded"), 16)
            act.dma_start(b_r[0:1, :], A_["b_router"]).then_inc(sem("moe_loaded"), 16)
            act.dma_start(at(o_mc, NMOE_CONST), A_["moe_consts"]).then_inc(sem("moe_loaded"), 16)
            act.dma_start(b_gu[0:NE, :], A_["b_gu"]).then_inc(sem("moe_loaded"), 16)
            act.dma_start(b_dn[0:NE, :], A_["b_dn"]).then_inc(sem("moe_loaded"), 16)
            act.dma_start(g_fin[:, :], A_["norm_final_g"].broadcast_to((P, D))).then_inc(sem("moe_loaded"), 16)
            act.wait_ge(sem("top_ready"), 1)
            for blk in range(2):
                own.link(f(negmax[:, blk:blk + 1], top[:, blk, 0:1], ACT.Copy, scale=-1.0))
                ins = f(probs[:, blk, :], top[:, blk, 0:TOPK], ACT.Exp, bias=negmax[:, blk:blk + 1],
                        accum_out=psums[:, blk:blk + 1])
                ins.then_inc(sem("probs_ready"), 1)
            for blk in range(2):
                act.wait_ge(sem("product"), product("u2_turned", blk + 1))
                f(u2[:, blk, :], bank(4 + 2 * blk, D), ACT.Copy).then_inc(sem("u2_kept"), 1)
            act.wait_ge(sem("product"), product("h2_turned", 1))
            for blk in range(2):
                f(acc[:, blk, :], bank(4 + 2 * blk, D), ACT.Copy).then_inc(sem("h2_kept"), 1)
            act.wait_ge(sem("product"), product("comb_turned", 1))
            f(combT[0:NE, :, :], bank(2, 2, P)[0:NE, :, :], ACT.Copy).then_inc(sem("combT_ready"), 1)

            def keep_x(n):
                act.wait_ge(sem("gathered"), n)
                f(xg, bank(2, 512), ACT.Copy).then_inc(sem("xg_ready"), 1)
                act.wait_ge(sem("x_turned"), n)
                f(xT.rearrange("p a b c -> p (a b c)"), bank(3, 512), ACT.Copy).then_inc(sem("x_ready"), 1)

            act.wait_ge(sem("items_kept"), 1)
            keep_x(1)
            n_items = act.value_load(nitems.bitcast(i32)[0:1, 0:1], min_val=NE, max_val=ITEMS)
            with act.Fori(0, n_items) as w:
                act.wait_ge(sem("gate_clamped"), w + 1)
                f(h_sig, h_gate, ACT.Sigmoid, scale=ALPHA).then_inc(sem("gate_sigmoid"), 1)
                keep_x(w + 2)
                act.wait_ge(sem("scat_turned"), w + 1)
                f(scatT.rearrange("p a b -> p (a b)"), bank(4, 2 * P), ACT.Copy).then_inc(sem("scatT_ready"), 1)
                act.wait_ge(sem("act_turned"), w + 1)
                f(actT.rearrange("p a b c -> p (a b c)"), bank(2, 512), ACT.Copy).then_inc(sem("actT_ready"), 1)
                act.wait_ge(sem("slot5_free"), w + 1)
                f(ye, bank(3, 512), ACT.Copy).then_inc(sem("ye_ready"), 1)
            act.wait_ge(sem("acc_added"), n_items + 1)
            for blk in range(2):
                own.done(f(fin[:, blk, :], acc[:, blk, :], ACT.Square, accum_out=fss[:, blk:blk + 1]))
            own.wait()
            f(frs, fss, ACT.Sqrt, scale=1.0 / D, bias=eps[:, 0:1]).then_inc(sem("final_std"), 1)

        @block.vector
        def _(dve):
            v = nc.vector
            own = Own(dve, "dve_own")
            link, done = own.link, own.done
            done(v.memset(eps[:, 0:1], NORM_EPS))
            done(v.memset(eps[:, 1:2], RWKV_GN_EPS))
            own.wait()
            v.memset(eps[:, 2:3], 1.0).then_inc(sem("dve_eps"), 1)
            dve.wait_ge(sem("params_loaded"), 32)
            v.tensor_scalar(om, par[:, MU:], -1.0, 1.0, ALU.mult, ALU.add).then_inc(sem("one_minus"), 1)
            dve.wait_ge(sem("h_std"), 1)
            link(v.reciprocal(rs1, rs1))
            for k in range(KC):
                v.scalar_tensor_tensor(uT[:, k, :], hT[:, k, :], pcol("norm_mix_g", k), rs1, ALU.mult, ALU.mult
                                       ).then_inc(sem("u_ready"), 1)
            for z in (gq, gk, gv, rb, rv):
                done(v.memset(z[:, :, 0:PAD], 0.0))
            v.memset(ra[:, :, 0:PAD], 0.0).then_inc(sem("pads_cleared"), 1)
            smalls = ((rwT, 64, "mu_w", 0), (raT, 64, "mu_a", 0), (sg[:, 0, :], 128, "mu_g", 0), (sg[:, 1, :], 32, "mu_g", 1))
            for n, (dst, rows, mu, m) in enumerate(smalls):
                dve.wait_ge(sem("small_part"), n + 1)
                v.scalar_tensor_tensor(dst[0:rows, 1:], bank(2 + n, T)[0:rows, 0:T - 1], pcol(mu, m, rows),
                                       dst[0:rows, 1:], ALU.mult, ALU.add).then_inc(sem("small_evacuated"), 1)
            for h in range(GH):
                dve.wait_ge(sem("gate_read"), h + 1)
                v.tensor_scalar(g_min[:, h, :], bank(h, T), pcol("b_gla_a", h), 0.0, ALU.add, ALU.min
                                ).then_inc(sem("gate_min_read"), 1)
            dve.wait_ge(sem("gate_log"), 1)
            dve.wait_ge(sem("gate_min_read"), GH)
            own.wait()
            link(v.tensor_tensor(gq[:, :, PAD:], g_min, g_abs, ALU.subtract))
            for h in range(GH):
                done(v.tensor_tensor_scan(gk[:, h, :], scan_mask, gq[:, h, :], 0.0, ALU.mult, ALU.add))
            own.wait()

            def chunks_of(x, n):
                return x.rearrange("p n (c t) -> p (n c) t", t=CHUNK)

            def spread(x, n):
                return chunks_of(x, n)[:, :, CHUNK // 2 - 1:CHUNK // 2].broadcast_to((P, n * NCHUNK, CHUNK))

            def boundary(dst, x, n):
                by = x.rearrange("p n (c t) -> p n c t", t=CHUNK)
                link(v.tensor_tensor(dst.rearrange("p n (c o) -> p n c o", o=1), by[:, :, :, CHUNK - 1:CHUNK],
                                     by[:, :, :, CHUNK // 2 - 1:CHUNK // 2], ALU.subtract))
                link(v.tensor_tensor(dst[:, :, 0:NCHUNK - 1].rearrange("p n (c o) -> p n c o", o=1),
                                     dst[:, :, 0:NCHUNK - 1].rearrange("p n (c o) -> p n c o", o=1),
                                     by[:, :, 1:, CHUNK // 2 - 1:CHUNK // 2], ALU.add))

            boundary(coefg, gk, GH)
            v.tensor_tensor(chunks_of(gq, GH), chunks_of(gk, GH), spread(gk, GH), ALU.subtract).then_inc(sem("g_log_decay"), 1)
            dve.wait_ge(sem("lora_evacuated"), 2 * KC)
            for m in range(KC):
                done(v.tensor_tensor_scan(rr[:, m, :], scan_mask, ra[:, m, :], 0.0, ALU.mult, ALU.add))
            own.wait()
            boundary(coefr, rr, KC)
            link(v.tensor_tensor(chunks_of(rk, KC), chunks_of(rr, KC), spread(rr, KC), ALU.subtract))
            v.tensor_tensor(ra, rk, ra, ALU.subtract).then_inc(sem("r_log_decay"), 1)
            for m in range(KC):
                done(v.tensor_scalar(rv[:, m, PAD:], rb[:, m, PAD:], pcol("k_a", m), omcol("k_a", m), ALU.mult, ALU.add))
            own.wait()
            dve.wait_ge(sem("g_decay"), 3)
            done(v.memset(gq[:, :, 0:PAD], 0.0))
            done(v.memset(gk[:, :, 0:PAD], 0.0))
            own.wait()
            with dve.Fori(0, 2) as i:
                for odd in range(2):
                    dve.wait_ge(sem("gla_projected"), 6 * i + 3 * odd + 2)
                    h = 2 * i + odd
                    q = gq[:, ds(h, 1), PAD:].rearrange("p a t -> p (a t)")
                    k = gk[:, ds(h, 1), PAD:].rearrange("p a t -> p (a t)")
                    v.scalar_tensor_tensor(q, bank(4 * odd, T), GDK ** -0.5, q, ALU.mult, ALU.mult)
                    v.tensor_tensor(k, bank(4 * odd + 1, T), k, ALU.mult).then_inc(sem("gla_qk_evacuated"), 1)
            dve.wait_ge(sem("r_decay"), 4)
            link(v.tensor_tensor(rb, rb, rk, ALU.mult))
            link(v.tensor_tensor(rk, rv, rk, ALU.mult))
            done(v.memset(ra[:, :, 0:PAD], 0.0))
            done(v.memset(rr[:, :, 0:PAD], 0.0))
            own.wait()
            v.memset(state, 0.0).then_inc(sem("rv_free"), 1)
            with dve.Fori(0, KC // 2) as i:
                own.enter(i, 8)
                for odd in range(2):
                    m = 2 * i + odd
                    rt, kt = rk_tmp[odd]
                    row = lambda x: x[:, ds(m, 1), PAD:].rearrange("p a t -> p (a t)")
                    dve.wait_ge(sem("rkv_part"), 6 * i + 3 * odd + 1)
                    link(v.scalar_tensor_tensor(rt[:, 1:], bank(4 * odd, T)[:, 0:T - 1], par[:, ds(m + PARAMS["mu_r"], 1)],
                                                rt[:, 1:], ALU.mult, ALU.add))
                    done(v.tensor_tensor(row(rr), row(rr), rt, ALU.mult))
                    dve.wait_ge(sem("rkv_part"), 6 * i + 3 * odd + 2)
                    v.scalar_tensor_tensor(kt[:, 1:], bank(4 * odd + 1, T)[:, 0:T - 1], par[:, ds(m + PARAMS["mu_k"], 1)],
                                           kt[:, 1:], ALU.mult, ALU.add).then_inc(sem("key_lerped"), 1)
                    dve.wait_ge(sem("key_lerped"), 2 * i + odd + 1)
                    done(v.tensor_tensor(row(rk), row(rk), kt, ALU.mult))
                    link(v.scalar_tensor_tensor(row(rb), kt, par[:, ds(m + PARAMS["k_k"], 1)], row(rb), ALU.mult, ALU.mult))
                    v.scalar_tensor_tensor(row(ra), kt, par[:, ds(m + PARAMS["k_k"], 1)], row(ra), ALU.mult, ALU.mult)
                    dve.wait_ge(sem("rkv_part"), 6 * i + 3 * odd + 3)
                    dve.wait_ge(sem("key_squared"), 2 * i + odd + 1)
                    v.scalar_tensor_tensor(row(rv)[:, 1:], bank(4 * odd + 2, T)[:, 0:T - 1],
                                           par[:, ds(m + PARAMS["mu_v"], 1)], row(rv)[:, 1:], ALU.mult, ALU.add
                                           ).then_inc(sem("rkv_evacuated"), 1)
            own.leave(KC // 2)
            dve.wait_ge(sem("key_norm_read"), 1)
            dve.wait_ge(sem("rkv_evacuated"), KC)
            link(v.tensor_scalar(hT, hT, 1e-12, None, ALU.max))
            link(v.reciprocal(hT, hT))
            link(v.tensor_tensor(rb[:, :, PAD:], rb[:, :, PAD:], hT, ALU.mult))
            link(v.scalar_tensor_tensor(ra[:, :, PAD:], ra[:, :, PAD:], -1.0, hT, ALU.mult, ALU.mult))
            v.memset(g_state, 0.0).then_inc(sem("factors_done"), 1)

            dve.wait_ge(sem("factors_done"), 1)
            with dve.Fori(0, NCHUNK) as c:
                own.enter(c, 3)
                cols = ds(CHUNK * c, CHUNK)
                dve.wait_ge(sem("state_product"), c)
                v.tensor_copy(c_ar[:, :, 0:CHUNK], ra[:, :, cols])
                v.tensor_copy(c_ar[:, :, CHUNK:], rr[:, :, cols])
                v.tensor_copy(c_b, rb[:, :, cols]).then_inc(sem("staged_dve"), 1)
                mask = causal.rearrange("p (a b) -> p a b", a=1).broadcast_to((P, KC, 2 * CHUNK))
                dve.wait_ge(sem("scores_b"), c + 1)
                v.tensor_tensor(c_mb, bank(0, KC, 2 * CHUNK), mask, ALU.mult).then_inc(sem("mask_b_done"), 1)
                dve.wait_ge(sem("mask_b_done"), c + 1)
                link(v.tensor_tensor(invT, c_mb[:, :, 0:CHUNK], levels[:, 0:1, :].broadcast_to((P, KC, CHUNK)), ALU.mult))
                v.tensor_tensor(invT, invT, half_ident.rearrange("p (a b) -> p a b", a=1).broadcast_to((P, KC, CHUNK)),
                                ALU.add).then_inc(sem("invT_ready"), 1)
                dve.wait_ge(sem("scores_k"), c + 1)
                v.tensor_tensor(c_mk, bank(2, KC, 2 * CHUNK), mask, ALU.mult).then_inc(sem("mask_k_done"), 1)
                for l in range(1, LEVELS):
                    if l == 3:
                        dve.wait_ge(sem("g_increment"), c + 1)
                        link(v.tensor_tensor(g_state, bank(0, GH, GDV), g_state, ALU.add))
                        v.tensor_tensor(g_state, g_state, coefg[:, :, ds(c, 1)].broadcast_to((P, GH, GDV)), ALU.mult
                                        ).then_inc(sem("g_state_ready"), 1)
                    if l < LEVELS - 1:
                        dve.wait_ge(sem("inv_step"), (LEVELS - 2) * c + l)
                        if l == 1:
                            dve.wait_ge(sem("inv_first"), c + 1)
                        v.tensor_tensor(inv, bank(4, KC, CHUNK), inv, ALU.add).then_inc(sem("inv_ready"), 1)
                    dve.wait_ge(sem("invT_step"), (LEVELS - 1) * c + l)
                    v.tensor_tensor(invT, bank(5, KC, CHUNK), invT, ALU.add).then_inc(sem("invT_ready"), 1)
                dve.wait_ge(sem("state_product"), c + 1)
                link(v.tensor_tensor(state, bank(5, KC, CHUNK), state, ALU.add))
                v.tensor_tensor(state, state, coefr[:, :, ds(c, 1)].broadcast_to((P, KC, CHUNK)), ALU.mult
                                ).then_inc(sem("state_ready"), 1)
            own.leave(NCHUNK)

            real = slice(CHUNK, TP)
            dve.wait_ge(sem("y_stored"), NCHUNK)
            link(v.tensor_tensor(rr[:, :, real], rr[:, :, real], rk[:, :, real], ALU.mult))
            for m in range(KC):
                ins = v.tensor_scalar(rr[:, m, real], rr[:, m, real], pcol("r_k", m), None, ALU.mult)
                if m < KC - 1:
                    done(ins)
            ins.then_inc(sem("bonus_in"), 1)
            dve.wait_ge(sem("product"), product("bonus_sum", 1))
            v.tensor_tensor(rv[:, :, real], bank(0, KC, SEQ), rv[:, :, real], ALU.mult).then_inc(sem("bonus_done"), 1)
            dve.wait_ge(sem("product"), product("y_sum", 1))
            v.scalar_tensor_tensor(ra[:, :, real], bank(4, KC, SEQ), -1.0 / HEAD, ra[:, :, real], ALU.mult, ALU.add
                                   ).then_inc(sem("y_centred"), 1)
            dve.wait_ge(sem("y_std"), 1)
            dve.wait_ge(sem("y_centred"), 1)
            link(v.reciprocal(rk[:, :, real], rk[:, :, real]))
            v.tensor_tensor(ra[:, :, real], ra[:, :, real], rk[:, :, real], ALU.mult).then_inc(sem("y_normed"), 1)
            dve.wait_ge(sem("g_std"), 1)
            link(v.reciprocal(g_std, g_std))
            for u in range(KC):
                done(v.scalar_tensor_tensor(gv[:, u, real], gv[:, u, real], pcol("gla_norm_g", u % 2), g_std[:, u // 2, :],
                                            ALU.mult, ALU.mult))
            dve.wait_ge(sem("r_sigmoid"), 1)
            link(v.tensor_tensor(late[:, 0:KC, :], late[:, 0:KC, :], sq_g, ALU.mult))
            v.tensor_tensor(gv[:, :, real], gv[:, :, real], late[:, 0:KC, :], ALU.mult).then_inc(sem("g_branch"), 1)
            dve.wait_ge(sem("y_affine"), 1)
            dve.wait_ge(sem("bonus_done"), 1)
            link(v.tensor_tensor(ra[:, :, real], ra[:, :, real], rv[:, :, real], ALU.add))
            dve.wait_ge(sem("product"), product("out_gate", 1))
            v.tensor_tensor(ra[:, :, real], bank(0, KC, SEQ), ra[:, :, real], ALU.mult).then_inc(sem("r_branch"), 1)
            dve.wait_ge(sem("gates_ready"), 1)
            for odd, j, first in ((0, 0, 6), (1, 3, 5)):
                us = slice(4 * odd, 4 * odd + 4)
                dve.wait_ge(sem(f"slot{j}_free"), first)
                done(v.tensor_tensor(rr[:, us, real], bank(4 + 2 * odd, 4, SEQ), late[:, KC + 4 * odd:KC + 4 * odd + 4, :], ALU.mult))
            for odd, j, first in ((0, 0, 7), (1, 3, 6)):
                us = slice(4 * odd, 4 * odd + 4)
                dve.wait_ge(sem(f"slot{j}_free"), first)
                link(v.tensor_tensor(rk[:, us, real], bank(2 * odd, 4, SEQ), late[:, 2 * KC + 4 * odd:2 * KC + 4 * odd + 4, :], ALU.mult))
                ins = v.tensor_tensor(rr[:, us, real], rr[:, us, real], rk[:, us, real], ALU.add)
                if odd == 0:
                    done(ins)
            ins.then_inc(sem("mixed"), 1)
            dve.wait_ge(sem("h_loaded"), 32)
            for odd, j, first in ((0, 0, 8), (1, 3, 7)):
                us = slice(4 * odd, 4 * odd + 4)
                dve.wait_ge(sem(f"slot{j}_free"), first)
                v.tensor_tensor(h2T[:, us, :], bank(4 + 2 * odd, 4, SEQ), h2T[:, us, :], ALU.add).then_inc(sem("h2_ready"), 1)
            v.memset(b_gu, 0.0).then_inc(sem("b_gu_cleared"), 1)
            dve.wait_ge(sem("h2_std"), 1)
            link(v.reciprocal(rs2, rs2))
            dve.wait_ge(sem("h2_ready"), 2)
            for k in range(KC):
                v.scalar_tensor_tensor(u2T[:, k, :], h2T[:, k, :], pcol("norm_ffn_g", k), rs2, ALU.mult, ALU.mult
                                       ).then_inc(sem("u2_ready"), 1)
            dve.wait_ge(sem("product"), product("logits", 1))
            link(v.tensor_copy(logits, bank(1, 2, NE)))
            for blk in range(2):
                done(v.max(top[:, blk, :], logits[:, blk, :]))
            own.wait()
            for blk in range(2):
                ins = v.max_index(top_i.bitcast(u32)[:, blk, :], top[:, blk, :], logits[:, blk, :])
                if blk == 0:
                    done(ins)
            ins.then_inc(sem("top_ready"), 1)
            dve.wait_ge(sem("top_ready"), 1)
            own.wait()
            link(v.tensor_copy(top_f, top_i.bitcast(u32)))
            dve.wait_ge(sem("probs_ready"), 2)
            link(v.reciprocal(psums, psums))
            for blk in range(2):
                done(v.tensor_scalar(probs[:, blk, :], probs[:, blk, :], psums[:, blk:blk + 1], None, ALU.mult))
            own.wait()
            dve.wait_ge(sem("moe_loaded"), 96)
            for blk in range(2):
                for k in range(TOPK):
                    dst = (comb if k == 0 else one_hot)
                    dst = comb[:, blk, :] if k == 0 else one_hot
                    link(v.tensor_scalar(dst, ids[:, 0:NE], top_f[:, blk, k:k + 1], probs[:, blk, k:k + 1],
                                         ALU.is_equal, ALU.mult))
                    if k:
                        link(v.tensor_tensor(comb[:, blk, :], comb[:, blk, :], one_hot, ALU.add))
            v.tensor_scalar(chosen, comb, 0.0, None, ALU.is_gt).then_inc(sem("chosen_ready"), 1)
            dve.wait_ge(sem("chosen_ready"), 1)
            dve.wait_ge(sem("product"), product("counted", 1))
            link(v.scalar_tensor_tensor(pos, bank(0, 3, NE)[:, 0:2, :], 1.0, chosen, ALU.add, ALU.mult))
            done(v.tensor_scalar(pos, pos, -1.0, None, ALU.add))
            link(v.tensor_copy(count, bank(0, 3, NE)[:, 2, :]))
            link(v.tensor_scalar(extra, count, float(SLOTS), None, ALU.is_gt))
            for b in range(2, BLOCKS):
                link(v.tensor_scalar(cmp_e, count, float(SLOTS * b), None, ALU.is_gt))
                link(v.tensor_tensor(extra, extra, cmp_e, ALU.add))
            link(v.tensor_tensor_scan(ends, ones[:, 0:NE], extra, 0.0, ALU.mult, ALU.add))
            link(v.tensor_scalar(cmp_e, ends, row_id[:, 0:1], None, ALU.is_le))
            done(v.reduce_sum(item_eb[:, 0:1], cmp_e, AX.X))
            link(v.tensor_tensor(cmp_x, cmp_e, extra, ALU.mult))
            link(v.reduce_sum(item_eb[:, 1:2], cmp_x, AX.X))
            link(v.scalar_tensor_tensor(item_eb[:, 1:2], item_eb[:, 1:2], -1.0, row_id[:, 0:1], ALU.mult, ALU.add))
            link(v.tensor_scalar(item_eb[:, 1:2], item_eb[:, 1:2], 1.0, float(BLOCKS - 1), ALU.add, ALU.min))
            link(v.tensor_scalar(item_eb[:, 0:1], item_eb[:, 0:1], float(NE - 1), None, ALU.min))
            link(v.tensor_scalar(bc_e, ones, item_eb[:, 0:1], None, ALU.mult))
            v.tensor_scalar(bc_b, ones, item_eb[:, 1:2], None, ALU.mult).then_inc(sem("extra_items"), 1)
            done(v.memset(item_b[:, 0:NE], 0.0))
            done(v.tensor_copy(item_e[:, 0:NE], ids[:, 0:NE]))
            link(v.tensor_scalar(nitems[:, 1:2], ends[:, NE - 1:NE], float(NE), None, ALU.add))
            done(v.tensor_copy(nitems.bitcast(i32)[:, 0:1], nitems[:, 1:2]))
            dve.wait_ge(sem("product"), product("items_spread", 1))
            done(v.tensor_copy(item_e[:, NE:], bank(3, 2, P)[:, 0, :]))
            link(v.tensor_scalar(item_b[:, NE:], bank(3, 2, P)[:, 1, :], float(2 * SLOTS), None, ALU.mult))
            link(v.tensor_copy(item_ei.bitcast(i32), item_e))
            v.tensor_copy(item_bi.bitcast(i32), item_b).then_inc(sem("items_ready"), 1)
            dve.wait_ge(sem("items_ready"), 1)
            done(v.memset(scatT, 0.0))
            v.memset(ye, 0.0).then_inc(sem("items_kept"), 1)
            dve.wait_ge(sem("product"), product("dn_bias", 1))
            dve.wait_ge(sem("h2_kept"), 2)
            link(v.tensor_tensor(acc.rearrange("p a d -> p (a d)"), bank(4, 2 * D), acc.rearrange("p a d -> p (a d)"), ALU.add))

            def item(w):
                e = dve.value_load(item_ei.bitcast(i32)[0:1, ds(w, 1)], min_val=0, max_val=NE - 1)
                first = dve.value_load(item_bi.bitcast(i32)[0:1, ds(w, 1)], min_val=0, max_val=(BLOCKS - 1) * 2 * SLOTS)
                return e, first

            def select_tokens(e, first):
                for blk in range(2):
                    ins = v.tensor_scalar(gat[:, blk, :], slot_ids[:, ds(first, SLOTS)], pos[:, blk, ds(e, 1)], None,
                                          ALU.is_equal)
                ins.then_inc(sem("gather_ready"), 1)

            def select_results(w, e, first):
                for blk in range(2):
                    v.tensor_scalar(scat[:, blk, :], slot_ids[:, ds(first, 2 * SLOTS)], pos[:, blk, ds(e, 1)],
                                    comb[:, blk, ds(e, 1)], ALU.is_equal, ALU.mult)
                v.tensor_scalar(sel, row_id[:, 0:1].broadcast_to((P, SLOTS)), item_e[:, ds(w, 1)], None, ALU.is_equal
                                ).then_inc(sem("select_ready"), 1)

            done(v.memset(h_up, 0.0))
            own.wait()
            v.memset(h_gate, 0.0).then_inc(sem("bias_added"), 1)
            e, first = item(0)
            select_tokens(e, first)
            select_results(0, e, first)
            v.memset(h_sig[:, 0:1], 0.0).then_inc(sem("loop_buffers"), 1)
            n_items = dve.value_load(nitems.bitcast(i32)[0:1, 0:1], min_val=NE, max_val=ITEMS)

            def add_scattered(n):
                dve.wait_ge(sem("scattered"), n)
                for q in range(4):
                    part = acc.rearrange("p a (h d) -> p (a h) d", h=2)[:, q, :]
                    ins = v.tensor_tensor(part, bank(4 + q, 512), part, ALU.add)
                ins.then_inc(sem("acc_added"), 1)

            with dve.Fori(0, n_items) as w:
                own.enter(w, 2)
                e, first = item(w + 1)
                dve.wait_ge(sem("gathered"), w + 1)
                select_tokens(e, first)
                dve.wait_ge(sem("slot3_free"), w + 8)
                dve.wait_ge(sem("gate_sigmoid"), w)
                dve.wait_ge(sem("act_turned"), w)
                v.tensor_scalar(h_gate, bank(0, 512), LIMIT, None, ALU.min).then_inc(sem("gate_clamped"), 1)
                link(v.tensor_scalar(h_up, bank(1, 512), LIMIT, -LIMIT, ALU.min, ALU.max))
                dve.wait_ge(sem("gate_clamped"), w + 1)
                link(v.scalar_tensor_tensor(h_up, h_up, 1.0, h_gate, ALU.add, ALU.mult))
                dve.wait_ge(sem("gate_sigmoid"), w + 1)
                v.tensor_tensor(h_up, h_up, h_sig, ALU.mult).then_inc(sem("act_ready"), 1)
                add_scattered(w + 1)
                dve.wait_ge(sem("scat_turned"), w + 1)
                select_results(w + 1, e, first)
            own.leave(0)
            add_scattered(n_items + 1)
            dve.wait_ge(sem("final_std"), 1)
            v.reciprocal(frs, frs).then_inc(sem("final_rstd"), 1)
            dve.wait_ge(sem("final_rstd"), 1)
            for blk in range(2):
                v.scalar_tensor_tensor(fin[:, blk, :], acc[:, blk, :], frs[:, blk:blk + 1], g_fin, ALU.mult, ALU.mult
                                       ).then_inc(sem("final_ready"), 1)

        @block.gpsimd
        def _(pool):
            g = nc.gpsimd
            pool.wait_ge(sem("factors_done"), 1)
            with pool.Fori(0, NCHUNK) as c:
                cols = ds(CHUNK * c, CHUNK)
                pool.wait_ge(sem("g_increment"), c)
                g.tensor_copy(g_v, gv[:, :, cols])
                g.tensor_copy(g_k, gk[:, :, cols])
                g.tensor_copy(g_q, gq[:, :, cols]).then_inc(sem("staged_pool"), 1)
                for l in range(1, LEVELS):
                    if l == 3:
                        pool.wait_ge(sem("g_scores_read"), c + 1)
                        apart(pool, "pool_passed")
                        g.affine_select(out=g_a[0:64, :, :], in_=g_a[0:64, :, :], compare_op=ALU.is_ge, fill=0.0, base=0,
                                        pattern=[[0, GH], [1, CHUNK]], channel_multiplier=-1).then_inc(sem("g_a_ready"), 1)
                    if l == 1:
                        pool.wait_ge(sem("mask_b_done"), c + 1)
                        pool.wait_ge(sem("level_product"), (LEVELS - 1) * c)
                    elif l >= 3:
                        pool.wait_ge(sem("level_product"), (LEVELS - 1) * c + l - 2)
                    g.tensor_tensor(c_nt[l % 2], c_mb[:, :, 0:CHUNK], levels[:, l:l + 1, :].broadcast_to((P, KC, CHUNK)),
                                    ALU.mult).then_inc(sem("level_ready"), 1)


def kernel(**inputs):
    import concourse.bacc as _bacc
    from concourse import mybir as _mybir
    from concourse.bass_utils import run_bass_kernel_spmd as _run

    x = {k: np.asarray(v) for k, v in inputs.items()}
    f = {k: (v[0] if k not in ("x", "meta_tokens", "norm_final_g") else v) for k, v in x.items()}

    def kmajor(w):
        return np.ascontiguousarray(w.reshape(KC, P, -1).transpose(1, 0, 2))

    w_in = f["w_in"]
    names = ("gq", "gk", "gv", "gr", "ga", "rr", "rk", "rv", "rw", "ra", "rg", "gate_gla", "gate_rwkv")
    sizes = (512, 512, 1024, 1024, 16, 1024, 1024, 1024, 64, 64, 160, 1024, 1024)
    ends = np.cumsum(sizes)
    W = {n: w_in[:, e - s:e] for n, s, e in zip(names, sizes, ends)}

    def units(v):
        v = np.asarray(v).reshape(-1)
        if v.size % P:
            v = np.concatenate([v, np.zeros(-v.size % P, v.dtype)])
        return v.reshape(-1, P).T

    consts, moe_consts = constants()
    mid = [W[n][:, 512 * j:512 * j + 512] for n in ("gr", "gate_gla", "gate_rwkv") for j in range(2)]
    mid += [f[n][:, 512 * j:512 * j + 512] for n in ("w_gla_o", "w_rwkv_o", "w_out") for j in range(2)]
    arrays = {
        "hT": kmajor(np.concatenate([x["meta_tokens"], x["x"][0]], 0).T),
        "consts": consts,
        "moe_consts": moe_consts,
        "params": np.ascontiguousarray(np.concatenate([units(f[n]) for n in PARAMS], 1)),
        "w_small": kmajor(np.concatenate([W[n] for n in ("ga", "rw", "ra", "rg")], 1)),
        "w_gla_a2": f["w_gla_a2"], "w_decay2": f["w_decay2"], "w_a2": f["w_a2"], "w_gate2": f["w_gate2"],
        "w_gla": np.stack([kmajor(np.concatenate([W["gq"][:, P * h:P * h + P], W["gk"][:, P * h:P * h + P],
                                                  W["gv"][:, GDV * h:GDV * h + GDV]], 1)) for h in range(GH)]),
        "w_rwkv": np.stack([kmajor(np.concatenate([W[n][:, P * m:P * m + P] for n in ("rr", "rk", "rv")], 1))
                            for m in range(KC)]),
        "w_mid": np.stack([kmajor(w) for w in mid]),
        "w_router": kmajor(f["w_router"]),
        "b_router": f["b_router"].reshape(1, NE),
        "w_gu": f["w_exp_gu"], "b_gu": f["b_exp_gu"], "w_dn": f["w_exp_down"], "b_dn": f["b_exp_down"],
        "norm_final_g": f["norm_final_g"].reshape(1, D),
    }
    nc = _bacc.Bacc("TRN2", target_bir_lowering=False, num_devices=1)
    ins, aps = {}, {}
    for name, a in arrays.items():
        a = np.ascontiguousarray(a)
        ins[f"in_{name}"] = a
        aps[name] = nc.dram_tensor(f"in_{name}", a.shape, _mybir.dt.from_np(a.dtype), kind="ExternalInput").ap()
    aps["out"] = nc.dram_tensor("out_0", (SEQ, D), _mybir.dt.float32, kind="ExternalOutput").ap()
    block_kernel(nc, aps)
    r = _run(nc, [ins], core_ids=[0])
    return r.results[0]["out_0"].reshape(1, SEQ, D)
```

```python
import concourse.bass as bass
from concourse import mybir
from contextlib import ExitStack
import numpy as np

P = 128
D = 1024
SEQ = 256
N_META = 16
T = SEQ + N_META
KC = D // P
CHUNK = 64
PAD = -N_META % CHUNK
NCHUNK = (T + PAD) // CHUNK
TP = NCHUNK * CHUNK
GH, GDK, GDV = 4, 128, 256
HEAD = 64
NORM_EPS = 1e-5
RWKV_GN_EPS = 64e-5
GATE_NORM = 16.0
DECAY_SCALE = float(np.exp(-0.5))
NE = 32
TOPK = 4
FE = 1024
LIMIT = 7.0
ALPHA = 1.702
SLOTS = 64
BLOCKS = SEQ // SLOTS
ITEMS = NE + SEQ * TOPK // SLOTS + 1
PIECE = 4096
RING = 6
TILE = 32
LEVELS = 5

PARAMS = {}
_at = 0
for _name, _n in (("norm_mix_g", 8), ("b_gla_a", 4), ("gla_norm_g", 2), ("b_decay", 8), ("b_a", 8),
                  ("k_k", 8), ("r_k", 8), ("ln_x_g", 8), ("ln_x_b", 8), ("norm_ffn_g", 8),
                  ("mu_r", 8), ("mu_k", 8), ("mu_v", 8), ("mu_wa", 1), ("mu_g", 2), ("k_a", 8)):
    PARAMS[_name] = _at
    _at += _n
NPARAM = _at
MU = PARAMS["mu_r"]

CONSTS = {}
_at = 0
for _name, _n in (("ident", P), ("ones", P), ("half_ones", P), ("half_ident", CHUNK), ("causal", 2 * CHUNK),
                  ("levels", LEVELS * TILE), ("tile_ident", TILE), ("parity", 2), ("scan", TP)):
    CONSTS[_name] = _at
    _at += _n
NCONST = _at
MOE_CONSTS = {}
_at = 0
for _name, _n in (("before", P), ("slot_ids", BLOCKS * 2 * SLOTS), ("row_id", 1), ("ids", P)):
    MOE_CONSTS[_name] = _at
    _at += _n
NMOE_CONST = _at


def constants():
    p = np.arange(P)[:, None]
    s, t = p % TILE, np.arange(TILE)[None, :]
    levels = []
    for l in range(LEVELS):
        b = 1 << l
        levels.append((t // (2 * b) == s // (2 * b)) & (t // b % 2 == 1) & (s // b % 2 == 0))
    tile_ident, parity = s == t, p // TILE % 2 == np.arange(2)[None, :]
    s, t = p % CHUNK, np.arange(CHUNK)[None, :]
    scan = np.broadcast_to(np.arange(TP)[None, :] % CHUNK != 0, (P, TP))
    parts = [np.eye(P), np.ones((P, P)), p // HEAD == np.arange(P)[None, :] // HEAD, s == t,
             np.concatenate([s < t, s <= t], 1), *levels, tile_ident, parity, scan]
    slots = np.tile(np.arange(SLOTS)[None, :], (P, 2))
    moe = [p < np.arange(P)[None, :], *[slots + SLOTS * b for b in range(BLOCKS)], p,
           np.broadcast_to(np.arange(P)[None, :], (P, P))]
    return (np.concatenate([np.asarray(x, np.float32) for x in parts], 1),
            np.concatenate([np.asarray(x, np.float32) for x in moe], 1))


def block_kernel(nc, A):
    f32, i32, u32 = mybir.dt.float32, mybir.dt.int32, mybir.dt.uint32
    ALU, ACT, AX = mybir.AluOpType, mybir.ActivationFunctionType, mybir.AxisListType
    ds = bass.ds

    with ExitStack() as ctx:
        ctx.enter_context(nc.allow_non_contiguous_dma("rows of a piece"))
        FLOATS = 53000
        arena = ctx.enter_context(nc.sbuf_tensor("arena", [P, FLOATS], f32))
        ps = ctx.enter_context(nc.psum_tensor("ps", [P, 8 * 512], f32))
        sems = {}

        def sem(name):
            if name not in sems:
                sems[name] = ctx.enter_context(nc.semaphore(name))
            return sems[name]

        def at(off, *shape):
            n = int(np.prod(shape))
            assert off + n <= FLOATS
            v = arena[:, off:off + n]
            if len(shape) == 2:
                v = v.rearrange("p (a b) -> p a b", a=shape[0])
            elif len(shape) == 3:
                v = v.rearrange("p (a b c) -> p a b c", a=shape[0], b=shape[1])
            return v

        def bank(b, *shape):
            n = int(np.prod(shape))
            v = ps[:, 512 * b:512 * b + n]
            if len(shape) == 2:
                v = v.rearrange("p (a b) -> p a b", a=shape[0])
            elif len(shape) == 3:
                v = v.rearrange("p (a b c) -> p a b c", a=shape[0], b=shape[1])
            return v

        used = [0]

        def take(n):
            used[0] += n
            return used[0] - n

        ring = [take(PIECE) for _ in range(RING)]
        o_h, o_u = take(KC * T), take(KC * T)
        o_late = take(GH * TP)
        o_gk = take(GH * TP)
        o_rb = take(KC * TP)
        take(3 * KC * SEQ - (2 * GH + KC) * TP)
        o_gv, o_ra, o_rk, o_rr, o_rv = (take(KC * TP) for _ in range(5))
        o_const, o_par, o_om = take(NCONST), take(NPARAM), take(NPARAM - MU)
        o_coefg, o_coefr, o_sg = take(GH * NCHUNK), take(KC * NCHUNK), take(2 * T)
        eps = at(take(4), 4)
        o_x = take(FLOATS - used[0])

        hT, uT = at(o_h, KC, T), at(o_u, KC, T)
        gq, gk, gv = at(o_late, GH, TP), at(o_gk, GH, TP), at(o_gv, KC, TP)
        ra, rb, rk, rr, rv = (at(o, KC, TP) for o in (o_ra, o_rb, o_rk, o_rr, o_rv))
        late_rows = at(o_late, 4 * SEQ // CHUNK, TP)

        def late(n):
            if isinstance(n, int) and n == NCHUNK:
                return at(o_late + 4 * SEQ // CHUNK * TP, 4 * SEQ // CHUNK, CHUNK)
            return late_rows[:, :, ds(CHUNK * n, CHUNK)]

        def in_rows(x):
            return x.rearrange("p u (b t) -> p u b t", t=CHUNK)

        def by_unit(n):
            return late(n).rearrange("p (u b) t -> p u b t", u=4)

        par = at(o_par, NPARAM)
        om = at(o_om, NPARAM - MU)

        def pcol(name, m=0, n=P):
            return par[0:n, PARAMS[name] + m:PARAMS[name] + m + 1]

        def omcol(name, m=0, n=P):
            c = PARAMS[name] - MU + m
            return om[0:n, c:c + 1]

        def const(name, n):
            return at(o_const + CONSTS[name], n)

        ident, ones, half_ones = const("ident", P), const("ones", P), const("half_ones", P)
        half_ident = const("half_ident", CHUNK)
        causal = const("causal", 2 * CHUNK)
        scan_mask = const("scan", TP)
        levels = at(o_const + CONSTS["levels"], LEVELS, TILE)
        tile_ident, parity = const("tile_ident", TILE), const("parity", 2)
        coefg, coefr = at(o_coefg, GH, NCHUNK), at(o_coefr, KC, NCHUNK)
        sg = at(o_sg, 2, T)

        def piece(j, n, w):
            return at(ring[j], n, w)

        o_t = ring[4]
        w_wa2, w_gla_a2 = at(o_t, D), at(o_t + 2 * D, GH * GDK)
        waT, gaT = at(o_t + 2560, T), at(o_t + 2560 + T, T)
        GA = slice(32, 48)
        g_abs, g_min = at(o_t + 3376, GH, T), at(o_t + 4464, GH, T)
        key_sq, key_rn = ([at(o_h + (2 * j + i) * T, T) for i in range(2)] for j in range(2))
        rk_tmp = [[at(o_t + 5552 + (2 * j + i) * T, T) for j in range(2)] for i in range(2)]
        o_s = ring[3]
        home = (tuple(o_s + 1024 * i for i in range(3)) + tuple(o_s + 3072 + 512 * i for i in range(4)),
                tuple(ring[0] + 1024 * i for i in range(3)) + (ring[0] + 3072, ring[0] + 3584, o_s + 5120, o_s + 5632))
        c_ar, c_mb, c_mk = ([at(home[s][i], KC, 2 * CHUNK) for s in range(2)] for i in range(3))
        t_b, t_k, t_v, invT = ([at(home[s][i], KC, CHUNK) for s in range(2)] for i in range(3, 7))
        c_b, c_k, c_v = (at(o_s + 6144 + 512 * i, KC, CHUNK) for i in range(3))
        c_r, c_sa = (at(o_s + 7680 + 512 * i, KC, CHUNK) for i in range(2))
        low, tile, tileT, prod = (at(o_s + 8704 + 256 * i, KC, TILE) for i in range(4))
        low_at = at(o_s + 9728, LEVELS - 1, KC, TILE)
        g_v = at(o_s + 10752, KC, CHUNK)
        g_q, g_k, g_a = (at(o_s + 11264 + 256 * i, GH, CHUNK) for i in range(3))
        tg_k = at(o_x, GH * GDK)
        state = at(o_x + 512, KC, CHUNK)
        tg_v, g_state = at(o_h, GH * GDV), at(o_h + 1024, GH, GDV)
        w_gate2 = at(o_x, 2, D)
        sq = at(o_h, KC, SEQ)
        r_sig = at(o_h, 2 * 4 * SEQ // CHUNK, CHUNK)
        g_std = at(o_x + 2 * D, GH, SEQ)
        rv_sq, rs1 = at(o_rv, KC, T), at(o_rk, T)
        h2T, u2T, rs2 = hT[:, :, N_META:], at(o_u, KC, SEQ), at(o_x + 2 * D, SEQ)

        mused = [o_gv]

        def mtake(n):
            mused[0] += n
            assert mused[0] <= o_gv + 5 * KC * TP
            return mused[0] - n

        o_mc = mtake(NMOE_CONST)
        w_r = at(mtake(KC * NE), KC, NE)
        b_r = at(mtake(NE), NE)
        b_dn = at(mtake(D), D)
        assert mused[0] <= o_ra
        mused[0] = o_ra
        u2 = at(mtake(2 * D), 2, D)
        acc = at(mtake(2 * D), 2, D)
        b_gu = at(mtake(2 * FE), 2 * FE)
        g_fin = at(mtake(D), D)
        before = at(o_mc + MOE_CONSTS["before"], P)
        slot_ids = at(o_mc + MOE_CONSTS["slot_ids"], BLOCKS * 2 * SLOTS)
        row_id = at(o_mc + MOE_CONSTS["row_id"], 1)
        ids = at(o_mc + MOE_CONSTS["ids"], P)
        logits, chosen, comb, pos = (at(mtake(2 * NE), 2, NE) for _ in range(4))
        top = at(mtake(16), 2, 8)
        top_i = at(mtake(16), 2, 8)
        top_f = at(mtake(16), 2, 8)
        probs, negmax, psums = at(mtake(8), 2, 4), at(mtake(2), 2), at(mtake(2), 2)
        one_hot, weighted = (at(mtake(2 * TOPK * NE), 2, TOPK, NE) for _ in range(2))
        count, extra, ends, cmp_e, cmp_x = (at(mtake(NE), NE) for _ in range(5))
        item_eb = at(mtake(2), 2)
        bc_e, bc_b = at(mtake(P), P), at(mtake(P), P)
        item_e = at(mtake(NE + P), NE + P)
        item_b = at(mtake(NE + P), NE + P)
        item_ei = at(mtake(NE + P), NE + P)
        item_bi = at(mtake(NE + P), NE + P)
        nitems = at(mtake(2), 2)
        combT = at(mtake(2 * P), 2, P)
        sel = at(mtake(SLOTS), SLOTS)
        gat = at(mtake(2 * SLOTS), 2, SLOTS)
        scat = at(mtake(4 * SLOTS), 2, 2 * SLOTS)
        lused = [o_late]

        def ltake(n):
            lused[0] += n
            assert lused[0] <= o_late + 3 * KC * SEQ
            return lused[0] - n

        scatT = at(ltake(2 * P), 2, P)
        xg = at(ltake(512), 512)
        xT = at(ltake(512), 4, 2, SLOTS)
        h_gate, h_sig, h_up = (at(ltake(512), 512) for _ in range(3))
        actT = at(ltake(512), 4, 2, SLOTS)
        ye = at(ltake(512), 512)
        fin = at(ltake(2 * D), 2, D)
        fss, frs = at(ltake(2), 2), at(ltake(2), 2)

        class Own:

            def __init__(self, eng, name):
                self.eng, self.sem, self.base, self.n = eng, sem(name), 0, 0

            def done(self, ins):
                ins.then_inc(self.sem, 1)
                self.n += 1

            def wait(self):
                self.eng.wait_ge(self.sem, self.base + self.n)

            def link(self, ins):
                self.done(ins)
                self.wait()

            def enter(self, i, per):
                self.start, self.n, self.per = self.n, 0, per
                self.base = self.start + i * per

            def leave(self, trips):
                assert self.n == self.per, (self.n, self.per)
                self.base, self.n = 0, self.start + trips * self.per

        PRODUCTS = {"h_sumsq": 1, "small_projected": 2, "lora_projected": 8, "gate_projected": 4, "g_sumsq": 1, "y_sum": 1, "y_sumsq": 1, "bonus_sum": 1, "out_gate": 1, "h2_sumsq": 1, "logits": 1, "u2_turned": 2, "h2_turned": 2, "counted": 1, "items_spread": 1, "comb_turned": 1, "dn_bias": 1}

        def product(name, n=1):
            names = list(PRODUCTS)
            return sum(PRODUCTS[x] for x in names[:names.index(name)]) + n

        def credit(eng, *names):
            for name in names:
                eng.sem_inc(sem(name), 1)

        def after(eng, name, n):
            eng.wait_ge(sem(name), n + 1)

        def apart(eng, name):
            eng.sem_inc(sem(name), 1)

        block = ctx.enter_context(nc.Block())
        A_ = A

        @block.sync
        def _(sp):
            sp.dma_start(hT[:, :, :], A_["hT"]).then_inc(sem("h_loaded"), 16)
            sp.dma_start(at(o_const, NCONST), A_["consts"]).then_inc(sem("params_loaded"), 16)
            sp.dma_start(par, A_["params"]).then_inc(sem("params_loaded"), 16)
            sp.dma_start(piece(0, KC, 304), A_["w_small"]).then_inc(sem("slot0"), 16)
            sp.dma_start(w_wa2, A_["w_wa2"]).then_inc(sem("lora_loaded"), 16)
            sp.dma_start(w_gla_a2[GA, :], A_["w_gla_a2"]).then_inc(sem("lora_loaded"), 16)
            sp.dma_start(piece(1, KC, 512), A_["w_gla"][0]).then_inc(sem("slot1"), 16)
            sp.dma_start(piece(2, KC, 512), A_["w_gla"][1]).then_inc(sem("slot2"), 16)
            sp.dma_start(piece(3, KC, 384), A_["w_rwkv"][1]).then_inc(sem("slot3"), 16)
            sp.wait_ge(sem("slot0_free"), 1)
            sp.dma_start(piece(0, KC, 384), A_["w_rwkv"][0]).then_inc(sem("slot0"), 16)
            for h in (2, 3):
                j = 1 + h % 2
                sp.wait_ge(sem(f"slot{j}_free"), 1)
                sp.dma_start(piece(j, KC, 512), A_["w_gla"][h]).then_inc(sem(f"slot{j}"), 16)
            with sp.Fori(1, KC // 2) as i:
                for odd, j, first in ((0, 0, 1), (1, 3, 0)):
                    sp.wait_ge(sem(f"slot{j}_free"), first + i)
                    sp.dma_start(piece(j, KC, 384), A_["w_rwkv"][ds(2 * i + odd, 1)].rearrange("a p k n -> (a p) k n")
                                 ).then_inc(sem(f"slot{j}"), 16)
            with sp.Fori(0, 3) as i:
                for odd in range(2):
                    j = 1 + odd
                    sp.wait_ge(sem(f"slot{j}_free"), 2 + i)
                    sp.dma_start(piece(j, KC, 512), A_["w_mid"][ds(2 * i + odd, 1)].rearrange("a p k n -> (a p) k n")
                                 ).then_inc(sem(f"slot{j}"), 16)
            sp.wait_ge(sem("state_product"), NCHUNK - 1)
            sp.dma_start(piece(0, KC, 512), A_["w_mid"][6]).then_inc(sem("slot0"), 16)
            after(sp, "y_stored", NCHUNK)
            sp.dma_start(piece(3, KC, 512), A_["w_mid"][7]).then_inc(sem("slot3"), 16)
            FREE = {0: 8, 1: 5, 2: 5, 3: 7, 4: 0, 5: 0}

            def first_load(j):
                if FREE[j]:
                    sp.wait_ge(sem(f"slot{j}_free"), FREE[j])
                if j < 4:
                    src = A_["w_gu"][0, 256 * j:256 * j + 256, :].rearrange("(k p) n -> p k n", p=P)
                    sp.dma_start(piece(j, 2, 2048), src).then_inc(sem(f"slot{j}"), 16)
                else:
                    src = A_["w_dn"][0, 512 * (j - 4):512 * (j - 4) + 512, :].rearrange("(k p) n -> p k n", p=P)
                    sp.dma_start(piece(j, 4, 1024), src).then_inc(sem(f"slot{j}"), 16)

            for j in (4, 5, 1, 2):
                first_load(j)
            with sp.Fori(1, 3) as i:
                for odd, j, first in ((0, 0, 5), (1, 3, 4)):
                    sp.wait_ge(sem(f"slot{j}_free"), first + i)
                    sp.dma_start(piece(j, KC, 512), A_["w_mid"][ds(6 + 2 * i + odd, 1)].rearrange("a p k n -> (a p) k n")
                                 ).then_inc(sem(f"slot{j}"), 16)
            for j in (0, 3):
                first_load(j)
            sp.wait_ge(sem("items_ready"), 1)
            n_items = sp.value_load(nitems.bitcast(i32)[0:1, 0:1], min_val=NE, max_val=ITEMS)
            with sp.Fori(1, n_items) as w:
                e = sp.value_load(item_ei.bitcast(i32)[0:1, ds(w, 1)], min_val=0, max_val=NE - 1)
                for j in range(RING):
                    sp.wait_ge(sem(f"slot{j}_free"), w + FREE[j])
                    if j < 4:
                        src = A_["w_gu"][ds(e, 1), 256 * j:256 * j + 256, :].rearrange("a (k p) n -> (a p) k n", p=P)
                        sp.dma_start(piece(j, 2, 2048), src).then_inc(sem(f"slot{j}"), 16)
                    else:
                        src = A_["w_dn"][ds(e, 1), 512 * (j - 4):512 * (j - 4) + 512, :].rearrange(
                            "a (k p) n -> (a p) k n", p=P)
                        sp.dma_start(piece(j, 4, 1024), src).then_inc(sem(f"slot{j}"), 16)
            sp.wait_ge(sem("final_ready"), 2)
            sp.dma_start(A_["out"].rearrange("(a p) d -> p a d", p=P), fin[:, :, :]).then_inc(sem("stored"), 16)
            sp.wait_ge(sem("stored"), 16)

        @block.tensor
        def _(pe):
            mm, tr = nc.tensor.matmul, nc.tensor.transpose
            credit(pe, "act_turned")

            def project(dst, lhs, rhs):
                for k in range(KC):
                    last = mm(dst, lhs(k), rhs(k), start=(k == 0), stop=(k == KC - 1))
                return last

            pe.wait_ge(sem("params_loaded"), 32)
            pe.wait_ge(sem("h_squared"), 1)
            project(bank(0, T), lambda k: ones, lambda k: rv_sq[:, k, :]).then_inc(sem("product"), 1)
            pe.wait_ge(sem("slot0"), 16)
            small = piece(0, KC, 304)
            for k in range(KC):
                pe.wait_ge(sem("u_ready"), k + 1)
                last = mm(bank(1, T), small[:, k, 0:128], uT[:, k, :], start=(k == 0), stop=(k == KC - 1))
            last.then_inc(sem("product"), 1)
            project(bank(2, T), lambda k: small[:, k, 128:256], lambda k: uT[:, k, :]).then_inc(sem("product"), 1)
            project(bank(3, T)[0:48, :], lambda k: small[:, k, 256:304], lambda k: uT[:, k, :]).then_inc(sem("slot0_free"), 1)
            pe.wait_ge(sem("lora_loaded"), 32)
            pe.wait_ge(sem("wa_ready"), 1)
            for m in range(KC):
                b = 4 + 2 * (m % 2)
                if m >= 2:
                    pe.wait_ge(sem("lora_evacuated"), 2 * (m - 1))
                mm(bank(b, T), w_wa2[0:64, P * m:P * m + P], waT[0:64, :], start=True, stop=True)
                mm(bank(b + 1, T), w_wa2[64:128, P * m:P * m + P], waT[64:128, :], start=True, stop=True
                   ).then_inc(sem("product"), 1)
            pe.wait_ge(sem("ga_ready"), 1)
            pe.wait_ge(sem("small_evacuated"), 3)
            for h in range(GH):
                mm(bank(h, T), w_gla_a2[GA, P * h:P * h + P], gaT[GA, :], start=True, stop=True
                   ).then_inc(sem("product"), 1)
            pe.wait_ge(sem("gate_read"), GH)
            pe.wait_ge(sem("gate_min_read"), GH)
            pe.wait_ge(sem("lora_evacuated"), 2 * KC)
            with pe.Fori(0, 2) as i:
                for odd in range(2):
                    w = piece(1 + odd, KC, 512)
                    pe.wait_ge(sem(f"slot{1 + odd}"), 16 * i + 16)
                    after(pe, "gla_v_evacuated", 2 * i)
                    after(pe, "gla_qk_evacuated", 2 * i)
                    for b in range(4):
                        last = project(bank(4 * odd + b, T), lambda k: w[:, k, P * b:P * b + P], lambda k: uT[:, k, :])
                        last.then_inc(sem("gla_projected" if b < 3 else f"slot{1 + odd}_free"), 1)
            after(pe, "gla_v_evacuated", GH)
            after(pe, "gla_qk_evacuated", GH)
            with pe.Fori(0, KC // 2) as i:
                for odd, j in ((0, 0), (1, 3)):
                    w = piece(j, KC, 384)
                    pe.wait_ge(sem(f"slot{j}"), 16 * i + (32 if j == 0 else 16))
                    after(pe, "rkv_evacuated", 2 * i)
                    for b in range(3):
                        last = project(bank(4 * odd + b, T), lambda k: w[:, k, P * b:P * b + P], lambda k: uT[:, k, :])
                        last.then_inc(sem("rkv_projected" if b < 2 else f"slot{j}_free"), 1)
                    pe.wait_ge(sem("key_squared"), 2 * i + odd + 1)
                    mm(bank(4 * odd + 3, T), half_ones, key_sq[odd], start=True, stop=True
                       ).then_inc(sem("key_sumsq"), 1)
            after(pe, "rkv_evacuated", KC)

            halves = (slice(0, 64), slice(64, 128))
            pairs = [(m, h) for m in range(KC) for h in halves]
            tiles = [(m, slice(TILE * q, TILE * q + TILE)) for m in range(KC) for q in range(P // TILE)]

            now = slice(N_META, T)
            real = slice(CHUNK, TP)

            def late_half(n, j, q, h):
                w = piece(j, KC, 512)
                u = h // 2
                if h == 0:
                    pe.wait_ge(sem(f"slot{j}"), 16 * q + 48)
                    apart(pe, "pe_passed")
                for k in range(4 * (h % 2), 4 * (h % 2) + 4):
                    last = mm(bank(0, 4, SEQ)[:, u, :], w[:, k, P * u:P * u + P], uT[:, k, now],
                              start=(k == 0), stop=(k == KC - 1))
                if h == 3:
                    last.then_inc(sem("late_projected"), 1)
                if h == 7:
                    last.then_inc(sem(f"slot{j}_free"), 1)

            def fill(u):
                late_half(NCHUNK, 2, 2, 2 * u)
                late_half(NCHUNK, 2, 2, 2 * u + 1)

            def chunk_products(n, sn, c, sc, piece_at=None):
                prep, turn = n is not None, c is not None

                def since(name, k):
                    if not (isinstance(k, int) and k == 0):
                        pe.wait_ge(sem(name), k)

                def turned(b, src):
                    for m, h in pairs:
                        last = mm(bank(b, KC, CHUNK)[h, m, :], src[h, m, :], half_ident[h, :], start=True, stop=True)
                    last.then_inc(sem("turned"), 1)

                def level(l, second):
                    if second:
                        pe.wait_ge(sem("prod_ready"), LEVELS * n + l)
                    else:
                        pe.wait_ge(sem("inv_ready"), LEVELS * n + l)
                    apart(pe, "pe_passed")
                    for m, q in tiles:
                        if second:
                            last = mm(bank(5, KC, TILE)[q, m, :], prod[q, m, :], tileT[q, m, :], start=True, stop=True)
                        else:
                            last = mm(bank(4, KC, TILE)[q, m, :], low_at[q, l - 1, m, :], tile[q, m, :], start=True, stop=True)
                    last.then_inc(sem("step_product" if second else "level_product"), 1)

                if turn:
                    pe.wait_ge(sem("turned_read"), 3 * c + 3)
                    pe.wait_ge(sem("mask_k_done"), c + 1)
                    pe.wait_ge(sem("state_ready"), c + 1)
                    after(pe, "y_stored", c)
                    apart(pe, "pe_passed")
                    for m, h in pairs:
                        mm(bank(6, KC, CHUNK)[h, m, :], c_ar[sc][h, m, 0:CHUNK], state[h, m, :], start=True, stop=False)
                        last = mm(bank(6, KC, CHUNK)[h, m, :], c_mk[sc][h, m, 0:CHUNK], t_v[sc][h, m, :], start=False, stop=True)
                    last.then_inc(sem("rhs_product"), 1)
                if not prep:
                    pe.wait_ge(sem("g_state_ready"), NCHUNK)
                    fill(0)
                    pe.wait_ge(sem("g_squared"), 1)
                    pe.wait_ge(sem("g_out_stored"), NCHUNK)
                    for h in range(GH):
                        for w in range(2):
                            last = mm(bank(2, GH, SEQ)[:, h, :], ones, sq[:, 2 * h + w, :], start=(w == 0), stop=(w == 1))
                    last.then_inc(sem("product"), 1)
                if prep:
                    pe.wait_ge(sem("staged_dve"), n + 1)
                    pe.wait_ge(sem("staged_act"), n + 1)
                    since("g_state_ready", n)
                    apart(pe, "pe_passed")
                    for m, h in pairs:
                        last = mm(bank(0, KC, 2 * CHUNK)[h, m, :], c_b[h, m, :], c_ar[sn][h, m, :], start=True, stop=True)
                    last.then_inc(sem("scores_b"), 1)
                    since("tg_k_ready", n)
                    since("g_out_stored", n)
                    apart(pe, "pe_passed")
                    for m, h in pairs:
                        last = mm(bank(2, KC, 2 * CHUNK)[h, m, :], c_k[h, m, :], c_ar[sn][h, m, :], start=True, stop=True)
                    last.then_inc(sem("scores_k"), 1)
                    since("prod_ready", LEVELS * n)
                    since("inverse_ready", n)
                    apart(pe, "pe_passed")
                    turned(4, c_b)
                    turned(5, c_k)
                if turn:
                    pe.wait_ge(sem("inverse_ready"), c + 1)
                    pe.wait_ge(sem("rhs_ready"), c + 1)
                    apart(pe, "pe_passed")
                    for m, h in pairs:
                        last = mm(bank(7, KC, CHUNK)[h, m, :], invT[sc][h, m, :], c_r[h, m, :], start=True, stop=True)
                    last.then_inc(sem("sa_product"), 1)
                if not prep:
                    fill(1)
                if prep:
                    pe.wait_ge(sem("turned_read"), 3 * n + 1)
                    apart(pe, "pe_passed")
                    turned(4, c_v)
                    pe.wait_ge(sem("staged_pool"), n + 1)
                    pe.wait_ge(sem("mask_b_done"), n + 1)
                    apart(pe, "pe_passed")
                    for u in range(KC):
                        last = tr(bank(0, KC, P)[0:64, u, :], g_v[:, u, :], ident)
                    last.then_inc(sem("g_v_turned"), 1)
                    pe.wait_ge(sem("level_ready"), n + 1)
                    pe.wait_ge(sem("turned_read"), 3 * n + 3)
                    level(1, False)
                if turn:
                    pe.wait_ge(sem("sa_ready"), c + 1)
                    apart(pe, "pe_passed")
                    for m, h in pairs:
                        mm(bank(6, KC, CHUNK)[h, m, :], state[h, m, :], c_ar[sc][h, m, CHUNK:], start=True, stop=False)
                        mm(bank(6, KC, CHUNK)[h, m, :], c_sa[h, m, :], c_mb[sc][h, m, CHUNK:], start=False, stop=False)
                        last = mm(bank(6, KC, CHUNK)[h, m, :], t_v[sc][h, m, :], c_mk[sc][h, m, CHUNK:], start=False, stop=True)
                    last.then_inc(sem("y_product"), 1)
                if not prep:
                    fill(2)
                    fill(3)
                if prep:
                    level(1, True)
                if turn and prep:
                    for m, h in pairs:
                        mm(bank(7, KC, CHUNK)[h, m, :], t_b[sc][h, m, :], c_sa[h, m, :], start=True, stop=False)
                        last = mm(bank(7, KC, CHUNK)[h, m, :], t_k[sc][h, m, :], t_v[sc][h, m, :], start=False, stop=True)
                    last.then_inc(sem("state_product"), 1)
                if prep:
                    pe.wait_ge(sem("mask_k_done"), n + 1)
                    apart(pe, "pe_passed")
                    for h in range(GH):
                        last = tr(bank(2, GH, P)[0:64, h, :], g_k[:, h, :], ident)
                    last.then_inc(sem("g_k_turned"), 1)
                    for h in range(GH):
                        last = mm(bank(3, GH, CHUNK)[0:64, h, :], g_k[:, h, :], g_q[:, h, :], start=True, stop=True)
                    last.then_inc(sem("g_scores"), 1)
                    pe.wait_ge(sem("tg_v_ready"), n + 1)
                    late_half(n, *piece_at, 0)
                    level(2, False)
                    late_half(n, *piece_at, 1)
                    level(2, True)
                    late_half(n, *piece_at, 2)
                    level(3, False)
                    late_half(n, *piece_at, 3)
                    level(3, True)
                    late_half(n, *piece_at, 4)
                    pe.wait_ge(sem("g_a_ready"), n + 1)
                    since("g_state_ready", n)
                    apart(pe, "pe_passed")
                    for u in range(KC):
                        mm(bank(3, KC, CHUNK)[:, u, :], tg_v[0:64, P * u:P * u + P], g_a[0:64, u // 2, :],
                           start=True, stop=False)
                        last = mm(bank(3, KC, CHUNK)[:, u, :], g_state[:, u // 2, P * (u % 2):P * (u % 2) + P],
                                  g_q[:, u // 2, :], start=False, stop=True)
                    last.then_inc(sem("g_out"), 1)
                    level(4, False)
                    late_half(n, *piece_at, 5)
                    level(4, True)
                    late_half(n, *piece_at, 6)
                    even, odds = (0, 2), (1, 3)
                    pe.wait_ge(sem("inv_ready"), LEVELS * n + LEVELS)
                    apart(pe, "pe_passed")
                    for m in range(KC):
                        for q in even:
                            a, b = slice(TILE * q, TILE * q + TILE), slice(TILE * q + TILE, TILE * q + 2 * TILE)
                            last = mm(bank(4, KC, TILE)[b, m, :], c_mb[sn][a, m, TILE:CHUNK], tile[a, m, :], start=True, stop=True)
                    last.then_inc(sem("level_product"), 1)
                    late_half(n, *piece_at, 7)
                    pe.wait_ge(sem("prod_ready"), LEVELS * n + LEVELS)
                    apart(pe, "pe_passed")
                    for m in range(KC):
                        for q in even:
                            a, b = slice(TILE * q, TILE * q + TILE), slice(TILE * q + TILE, TILE * q + 2 * TILE)
                            last = mm(bank(5, KC, TILE)[a, m, :], prod[b, m, :], tileT[b, m, :], start=True, stop=True)
                    last.then_inc(sem("step_product"), 1)

                    pe.wait_ge(sem("late_evacuated"), 2 * n + 3)
                    pe.wait_ge(sem("tg_k_ready"), n + 1)
                    apart(pe, "pe_passed")
                    for h in range(GH):
                        last = mm(bank(0, GH, GDV)[:, h, :], tg_k[0:64, P * h:P * h + P],
                                  tg_v[0:64, GDV * h:GDV * h + GDV], start=True, stop=True)
                    last.then_inc(sem("g_increment"), 1)

            chunk_products(0, 0, None, None, (1, 0))
            with pe.Fori(0, NCHUNK // 2) as i:
                for odd in range(2):
                    chunk_products(2 * i + odd + 1, 1 - odd, 2 * i + odd, odd, (2 - odd, i + odd))
            chunk_products(None, None, NCHUNK - 1, 0)

            def by_head(src, name):
                for m in range(KC):
                    last = mm(bank(4, KC, SEQ)[:, m, :], half_ones, src[:, m, :], start=True, stop=True)
                last.then_inc(sem("product"), 1)

            def out_unit(odd, u, b0, src):
                w = piece(3 * odd, KC, 512)
                return project(bank(b0, 4, SEQ)[:, u, :], lambda k: w[:, k, P * u:P * u + P], lambda k: src[:, k, real])

            after(pe, "y_stored", NCHUNK)
            by_head(ra[:, :, real], "y_sum")
            pe.wait_ge(sem("g_branch"), 1)
            pe.wait_ge(sem("slot0"), 16 * 6)
            out_unit(0, 0, 2, gv)
            out_unit(0, 1, 2, gv)
            pe.wait_ge(sem("y_centred"), 1)
            pe.wait_ge(sem("y_squared"), 1)
            by_head(sq, "y_sumsq")
            out_unit(0, 2, 2, gv)
            out_unit(0, 3, 2, gv).then_inc(sem("slot0_free"), 1)
            pe.wait_ge(sem("slot3"), 16 * 5)
            after(pe, "late_evacuated", 12)
            out_unit(1, 0, 0, gv)
            pe.wait_ge(sem("y_std"), 1)
            pe.wait_ge(sem("bonus_in"), 1)
            by_head(rr[:, :, real], "bonus_sum")
            out_unit(1, 1, 0, gv)
            pe.wait_ge(sem("gate2_loaded"), 32)
            pe.wait_ge(sem("bonus_done"), 1)
            for m in range(KC):
                mm(bank(4, KC, SEQ)[:, m, :], w_gate2[:, 0, P * m:P * m + P], sg[:, 0, now], start=True, stop=False)
                last = mm(bank(4, KC, SEQ)[:, m, :], w_gate2[0:32, 1, P * m:P * m + P], sg[0:32, 1, now],
                          start=False, stop=True)
            last.then_inc(sem("product"), 1)
            out_unit(1, 2, 0, gv)
            out_unit(1, 3, 0, gv).then_inc(sem("slot3_free"), 1)
            def sum_h2(half):
                pe.wait_ge(sem("h2_squared"), half + 1)
                for k in range(4 * half, 4 * half + 4):
                    last = mm(bank(4, SEQ), ones, rv[:, k, real], start=(k == 0), stop=(k == KC - 1))
                return last

            for n, (src, ready) in ((1, (ra, "r_branch")), (2, (rr, "mixed"))):
                pe.wait_ge(sem(ready), 1)
                for odd, j, first in ((0, 0, 6), (1, 3, 5)):
                    pe.wait_ge(sem(f"slot{j}"), 16 * (first + n))
                    for u in range(4):
                        last = out_unit(odd, u, (0, 4, 0)[n] + 2 * odd, src)
                        if (n, odd, u) == (2, 1, 1):
                            sum_h2(0)
                    last.then_inc(sem(f"slot{j}_free"), 1)
            sum_h2(1).then_inc(sem("product"), 1)
            pe.wait_ge(sem("u2_ready"), KC)
            pe.wait_ge(sem("router_loaded"), 48)
            for blk in range(2):
                for k in range(KC):
                    mm(bank(1, 2, NE)[:, blk, :], u2T[:, k, P * blk:P * blk + P], w_r[:, k, :],
                       start=(k == 0), stop=False)
                last = mm(bank(1, 2, NE)[:, blk, :], ones[0:1, :], b_r[0:1, :], start=False, stop=True)
            last.then_inc(sem("product"), 1)
            for blk in range(2):
                for k in range(KC):
                    last = tr(bank(4 + 2 * blk, KC, P)[:, k, :], u2T[:, k, P * blk:P * blk + P], ident)
                last.then_inc(sem("product"), 1)
            pe.wait_ge(sem("mixed"), 1)
            for blk in range(2):
                if blk:
                    pe.wait_ge(sem("u2_kept"), 1)
                for k in range(KC):
                    last = tr(bank(2 + 2 * blk, KC, P)[:, k, :], h2T[:, k, P * blk:P * blk + P], ident)
                last.then_inc(sem("product"), 1)
            pe.wait_ge(sem("chosen_ready"), 1)
            mm(bank(0, 3, NE)[:, 0, :], before, chosen[:, 0, :], start=True, stop=True)
            mm(bank(0, 3, NE)[:, 1, :], ones, chosen[:, 0, :], start=True, stop=False)
            mm(bank(0, 3, NE)[:, 1, :], before, chosen[:, 1, :], start=False, stop=True)
            mm(bank(0, 3, NE)[:, 2, :], ones, chosen[:, 0, :], start=True, stop=False)
            mm(bank(0, 3, NE)[:, 2, :], ones, chosen[:, 1, :], start=False, stop=True).then_inc(sem("product"), 1)

            def gather(n):
                pe.wait_ge(sem("gather_ready"), n)
                for blk in range(2):
                    for half in range(2):
                        last = mm(bank(2, 512)[64 * half:64 * half + 64, :], gat[:, blk, :],
                                  u2[:, blk, 512 * half:512 * half + 512], start=(blk == 0), stop=(blk == 1))
                last.then_inc(sem("gathered"), 1)

            def turn_x(n):
                pe.wait_ge(sem("xg_ready"), n)
                for q in range(4):
                    last = tr(bank(3, 4, P)[:, q, :], xg[:, P * q:P * q + P], ident)
                last.then_inc(sem("x_turned"), 1)

            def scatter():
                for blk in range(2):
                    for half in range(2):
                        h = slice(64 * half, 64 * half + 64)
                        last = mm(bank(4 + 2 * blk + half, 512), scatT[h, blk, :], ye[h, :], start=True, stop=True)
                last.then_inc(sem("scattered"), 1)

            pe.wait_ge(sem("h2_kept"), 1)
            gather(1)
            turn_x(1)
            pe.wait_ge(sem("extra_items"), 1)
            mm(bank(0, 2, P)[:, 0, :], bc_e, ident, start=True, stop=True)
            mm(bank(0, 2, P)[:, 1, :], bc_b, ident, start=True, stop=True).then_inc(sem("product"), 1)
            pe.wait_ge(sem("comb_ready"), 1)
            for blk in range(2):
                last = tr(bank(1, 2, P)[0:NE, blk, :], comb[:, blk, :], ident)
            last.then_inc(sem("product"), 1)
            pe.wait_ge(sem("combT_ready"), 1)
            pe.wait_ge(sem("h2_kept"), 2)
            pe.wait_ge(sem("u2_kept"), 2)
            pe.wait_ge(sem("moe_loaded"), 48)
            for blk in range(2):
                for half in range(2):
                    last = mm(bank(4 + 2 * blk + half, 512), combT[0:NE, blk, :], b_dn[0:NE, 512 * half:512 * half + 512],
                              start=True, stop=True)
            last.then_inc(sem("product"), 1)
            pe.wait_ge(sem("loop_buffers"), 1)
            n_items = pe.value_load(nitems.bitcast(i32)[0:1, 0:1], min_val=NE, max_val=ITEMS)
            with pe.Fori(0, n_items) as w:
                pe.wait_ge(sem("x_ready"), w + 1)
                pe.wait_ge(sem("select_ready"), w + 1)
                after(pe, "act_ready", w)
                for b in range(2):
                    for half in range(2):
                        mm(bank(b, 512)[64 * half:64 * half + 64, :], sel, b_gu[:, FE * b + 512 * half:FE * b + 512 * half + 512],
                           start=True, stop=False)
                for k in range(KC):
                    j, first = k // 2, (8, 5, 5, 7)[k // 2]
                    if k % 2 == 0:
                        pe.wait_ge(sem(f"slot{j}"), 16 * w + 16 * (first + 1))
                    wk = piece(j, 2, 2048)
                    for b in range(2):
                        for half in range(2):
                            last = mm(bank(b, 512)[64 * half:64 * half + 64, :], xT[:, k % 4, k // 4, :],
                                      wk[:, k % 2, FE * b + 512 * half:FE * b + 512 * half + 512],
                                      start=False, stop=(k == KC - 1))
                    if k % 2:
                        last.then_inc(sem(f"slot{j}_free"), 1)
                after(pe, "ye_ready", w)
                after(pe, "scatT_ready", w)
                after(pe, "acc_added", w)
                scatter()
                gather(w + 2)
                turn_x(w + 2)
                after(pe, "acc_added", w + 1)
                for blk in range(2):
                    last = tr(bank(4, 2, P)[:, blk, :], scat[:, blk, :], ident)
                last.then_inc(sem("scat_turned"), 1)
                after(pe, "act_ready", w + 1)
                for q in range(4):
                    last = tr(bank(2, 4, P)[:, q, :], h_up[:, P * q:P * q + P], ident)
                last.then_inc(sem("act_turned"), 1)
                pe.wait_ge(sem("actT_ready"), w + 1)
                pe.wait_ge(sem("x_ready"), w + 2)
                for k in range(KC):
                    j = 4 + k // 4
                    if k % 4 == 0:
                        pe.wait_ge(sem(f"slot{j}"), 16 * w + 16)
                    wk = piece(j, 4, 1024)
                    for half in range(2):
                        last = mm(bank(3, 512)[64 * half:64 * half + 64, :], actT[:, k % 4, k // 4, :],
                                  wk[:, k % 4, 512 * half:512 * half + 512], start=(k == 0), stop=(k == KC - 1))
                    if k % 4 == 3:
                        last.then_inc(sem(f"slot{j}_free"), 1)
            after(pe, "ye_ready", n_items)
            after(pe, "scatT_ready", n_items)
            after(pe, "acc_added", n_items)
            scatter()

        @block.scalar
        def _(act):
            own = Own(act, "act_own")
            f = nc.scalar.activation
            credit(act, "gla_v_evacuated", "late_evacuated", "y_stored", "gate_sigmoid", "ye_ready", "scatT_ready")
            act.wait_ge(sem("h_loaded"), 16)
            f(rv_sq, hT, ACT.Square).then_inc(sem("h_squared"), 1)
            act.wait_ge(sem("dve_eps"), 1)
            f(eps[:, 3:4], eps[:, 0:1], ACT.Sqrt)
            act.wait_ge(sem("product"), product("h_sumsq", 1))
            f(rs1, bank(0, T), ACT.Sqrt, scale=1.0 / D, bias=eps[:, 0:1]).then_inc(sem("h_std"), 1)
            act.wait_ge(sem("one_minus"), 1)
            smalls = ((waT, 128, "mu_wa", 0), (sg[:, 0, :], 128, "mu_g", 0), (sg[:, 1, :], 32, "mu_g", 1))
            for n, (dst, rows, mu, m) in enumerate(smalls):
                if n < 2:
                    act.wait_ge(sem("product"), product("small_projected", n + 1))
                else:
                    act.wait_ge(sem("slot0_free"), 1)
                f(dst[0:rows, :], bank(1 + n, T)[0:rows, :], ACT.Copy, scale=omcol(mu, m, rows)).then_inc(sem("small_part"), 1)
                if n == 0:
                    act.wait_ge(sem("small_evacuated"), 1)
                    f(waT[0:64, :], waT[0:64, :], ACT.Tanh).then_inc(sem("wa_ready"), 1)
            f(gaT[GA, :], bank(3, T)[GA, :], ACT.Copy).then_inc(sem("ga_ready"), 1)
            act.wait_ge(sem("small_evacuated"), 3)
            own.done(f(sg[:, 0, :], sg[:, 0, :], ACT.Sigmoid))
            own.done(f(sg[0:32, 1, :], sg[0:32, 1, :], ACT.Sigmoid))
            act.wait_ge(sem("pads_cleared"), 1)
            for m in range(KC):
                act.wait_ge(sem("product"), product("lora_projected", m + 1))
                b = 4 + 2 * (m % 2)
                f(ra[:, m, PAD:], bank(b, T), ACT.Sigmoid, bias=pcol("b_decay", m)).then_inc(sem("lora_evacuated"), 1)
                f(rb[:, m, PAD:], bank(b + 1, T), ACT.Sigmoid, bias=pcol("b_a", m)).then_inc(sem("lora_evacuated"), 1)
            for h in range(GH):
                act.wait_ge(sem("product"), product("gate_projected", h + 1))
                f(g_abs[:, h, :], bank(h, T), ACT.Abs, bias=pcol("b_gla_a", h)).then_inc(sem("gate_read"), 1)
            act.wait_ge(sem("gate_read"), GH)
            own.link(f(g_abs, g_abs, ACT.Exp, scale=-1.0))
            f(g_abs, g_abs, ACT.Ln, bias=eps[:, 2:3]).then_inc(sem("gate_log"), 1)
            act.wait_ge(sem("g_log_decay"), 1)
            f(gk, gq, ACT.Exp, scale=-1.0 / GATE_NORM).then_inc(sem("g_decay"), 1)
            act.wait_ge(sem("g_decay"), 1)
            f(gq, gq, ACT.Exp, scale=1.0 / GATE_NORM).then_inc(sem("g_decay"), 1)
            f(coefg, coefg, ACT.Exp, scale=1.0 / GATE_NORM).then_inc(sem("g_decay"), 1)
            act.wait_ge(sem("r_log_decay"), 1)
            f(rr, rk, ACT.Exp, scale=-DECAY_SCALE).then_inc(sem("r_decay"), 1)
            act.wait_ge(sem("r_decay"), 1)
            f(rk, rk, ACT.Exp, scale=DECAY_SCALE).then_inc(sem("r_decay"), 1)
            f(ra, ra, ACT.Exp, scale=-DECAY_SCALE).then_inc(sem("r_decay"), 1)
            f(coefr, coefr, ACT.Exp, scale=-DECAY_SCALE).then_inc(sem("r_decay"), 1)
            with act.Fori(0, 2) as i:
                for odd in range(2):
                    act.wait_ge(sem(f"slot{1 + odd}_free"), i + 1)
                    apart(act, "act_passed")
                    for u in range(2):
                        ins = f(gv[:, ds(4 * i + 2 * odd + u, 1), PAD:].rearrange("p a t -> p (a t)"),
                                bank(4 * odd + 2 + u, T), ACT.Copy)
                    ins.then_inc(sem("gla_v_evacuated"), 1)
            act.wait_ge(sem("rv_free"), 1)
            with act.Fori(0, KC // 2) as i:
                for odd, j in ((0, 0), (1, 3)):
                    m = 2 * i + odd
                    rt, kt = rk_tmp[odd]
                    row = lambda x: x[:, ds(m, 1), PAD:].rearrange("p a t -> p (a t)")
                    act.wait_ge(sem("rkv_projected"), 4 * i + 2 * odd + 1)
                    after(act, "rkv_evacuated", 2 * i)
                    apart(act, "act_passed")
                    f(kt, bank(4 * odd, T), ACT.Copy, scale=om[:, ds(m + PARAMS["mu_k"] - MU, 1)]).then_inc(sem("rkv_part"), 1)
                    act.wait_ge(sem("rkv_projected"), 4 * i + 2 * odd + 2)
                    apart(act, "act_passed")
                    f(rt, bank(4 * odd + 1, T), ACT.Copy, scale=om[:, ds(m + PARAMS["mu_r"] - MU, 1)]).then_inc(sem("rkv_part"), 1)
                    act.wait_ge(sem("key_lerped"), 2 * i + odd + 1)
                    apart(act, "act_passed")
                    f(key_sq[odd], kt, ACT.Square, scale=par[:, ds(m + PARAMS["k_k"], 1)]).then_inc(sem("key_squared"), 1)
                    act.wait_ge(sem(f"slot{j}_free"), i + (2 if j == 0 else 1))
                    apart(act, "act_passed")
                    f(row(rv), bank(4 * odd + 2, T), ACT.Copy, scale=om[:, ds(m + PARAMS["mu_v"] - MU, 1)]
                      ).then_inc(sem("rkv_part"), 1)
                    act.wait_ge(sem("key_sumsq"), 2 * i + odd + 1)
                    f(key_rn[odd], bank(4 * odd + 3, T), ACT.Sqrt).then_inc(sem("key_norm"), 1)

            def chunk_copies(n, sn, c, sc, piece_at=None):
                prep, turn = n is not None, c is not None

                def copy(dst, src, needed, k, ready):
                    act.wait_ge(sem(needed), k)
                    apart(act, "act_passed")
                    f(dst, src, ACT.Copy).then_inc(sem(ready), 1)

                def keep_late(n, b):
                    f(late(n)[:, 8 * b:8 * b + 8, :], bank(b, 8, CHUNK), ACT.Copy).then_inc(sem("late_evacuated"), 1)

                if prep:
                    cols = ds(CHUNK * n, CHUNK)
                    f(c_k, rk[:, :, cols], ACT.Copy)
                    f(c_v, rv[:, :, cols], ACT.Copy).then_inc(sem("staged_act"), 1)
                if turn:
                    copy(c_r, bank(6, KC, CHUNK), "rhs_product", c + 1, "rhs_ready")
                if not prep:
                    act.wait_ge(sem("g_state_ready"), NCHUNK)
                    f(sq, gv[:, :, real], ACT.Square).then_inc(sem("g_squared"), 1)
                if prep:
                    copy(t_b[sn], bank(4, KC, CHUNK), "turned", 3 * n + 1, "turned_read")
                    copy(t_k[sn], bank(5, KC, CHUNK), "turned", 3 * n + 2, "turned_read")
                if turn:
                    copy(c_sa, bank(7, KC, CHUNK), "sa_product", c + 1, "sa_ready")
                if not prep:
                    act.wait_ge(sem("product"), product("g_sumsq", 1))
                    f(g_std, bank(2, GH, SEQ), ACT.Sqrt, scale=1.0 / GDV, bias=eps[:, 0:1]).then_inc(sem("g_std"), 1)
                    act.wait_ge(sem("late_projected"), NCHUNK + 1)
                    keep_late(NCHUNK, 0)
                    act.wait_ge(sem("late_evacuated"), 5)
                    f(r_sig[:, 0:16, :], late(0), ACT.Sigmoid)
                    f(r_sig[:, 16:32, :], late(1), ACT.Sigmoid).then_inc(sem("r_sigmoid"), 1)
                if prep:
                    copy(t_v[sn], bank(4, KC, CHUNK), "turned", 3 * n + 3, "turned_read")
                    copy(tg_v[0:64, :], bank(0, GH * GDV)[0:64, :], "g_v_turned", n + 1, "tg_v_ready")
                    copy(prod, bank(4, KC, TILE), "level_product", LEVELS * n + 1, "prod_ready")
                if turn:
                    copy(ra[:, :, ds(CHUNK * c, CHUNK)], bank(6, KC, CHUNK), "y_product", c + 1, "y_stored")
                if prep:
                    copy(tg_k[0:64, :], bank(2, GH * GDK)[0:64, :], "g_k_turned", n + 1, "tg_k_ready")
                    copy(g_a[0:64, :, :], bank(3, GH, CHUNK)[0:64, :, :], "g_scores", n + 1, "g_scores_read")
                    copy(prod, bank(4, KC, TILE), "level_product", LEVELS * n + 2, "prod_ready")
                    copy(prod, bank(4, KC, TILE), "level_product", LEVELS * n + 3, "prod_ready")
                    act.wait_ge(sem("late_projected"), n + 1)
                    apart(act, "act_passed")
                    keep_late(n, 0)
                    copy(gv[:, :, cols], bank(3, KC, CHUNK), "g_out", n + 1, "g_out_stored")
                    copy(prod, bank(4, KC, TILE), "level_product", LEVELS * n + 4, "prod_ready")
                    act.wait_ge(sem("level_product"), LEVELS * n + LEVELS)
                    for q in (1, 3):
                        rows = slice(TILE * q, TILE * q + TILE)
                        ins = f(prod[rows, :, :], bank(4, KC, TILE)[rows, :, :], ACT.Copy)
                    ins.then_inc(sem("prod_ready"), 1)
                    j, q = piece_at
                    act.wait_ge(sem(f"slot{j}_free"), q + 3)
                    apart(act, "act_passed")
                    keep_late(n, 1)

            real = slice(CHUNK, TP)
            act.wait_ge(sem("factors_done"), 1)
            chunk_copies(0, 0, None, None, (1, 0))
            with act.Fori(0, NCHUNK // 2) as i:
                for odd in range(2):
                    chunk_copies(2 * i + odd + 1, 1 - odd, 2 * i + odd, odd, (2 - odd, i + odd))
            chunk_copies(None, None, NCHUNK - 1, 0)
            act.wait_ge(sem("slot2_free"), 5)
            f(late(NCHUNK)[:, 8:16, :], bank(1, 8, CHUNK), ACT.Copy).then_inc(sem("late_evacuated"), 1)

            act.wait_ge(sem("state_ready"), NCHUNK)
            act.dma_start(w_gate2[:, 0, :], A_["w_gate2"][0:128, :]).then_inc(sem("gate2_loaded"), 16)
            act.dma_start(w_gate2[0:32, 1, :], A_["w_gate2"][128:160, :]).then_inc(sem("gate2_loaded"), 16)
            act.wait_ge(sem("y_centred"), 1)
            f(sq, ra[:, :, real], ACT.Square).then_inc(sem("y_squared"), 1)
            act.wait_ge(sem("late_evacuated"), 13)
            f(late(2), late(2), ACT.Sigmoid)
            f(late(3), late(3), ACT.Sigmoid).then_inc(sem("gates_ready"), 1)
            act.wait_ge(sem("product"), product("y_sumsq", 1))
            f(rk[:, :, real], bank(4, KC, SEQ), ACT.Sqrt, scale=1.0 / HEAD, bias=eps[:, 1:2]).then_inc(sem("y_std"), 1)
            act.dma_start(hT[:, :, :], A_["hT"]).then_inc(sem("h_loaded"), 16)
            f(late(4), late(4), ACT.Sigmoid)
            f(late(5), late(5), ACT.Sigmoid).then_inc(sem("gates_ready"), 1)
            act.wait_ge(sem("y_normed"), 1)
            for m in range(KC):
                ins = f(ra[:, m, real], ra[:, m, real], ACT.Identity, scale=pcol("ln_x_g", m), bias=pcol("ln_x_b", m))
            ins.then_inc(sem("y_affine"), 1)
            act.wait_ge(sem("slot3_free"), 5)
            act.dma_start(w_r[:, :, :], A_["w_router"]).then_inc(sem("router_loaded"), 16)
            act.dma_start(b_r[0:1, :], A_["b_router"]).then_inc(sem("router_loaded"), 16)
            act.dma_start(at(o_mc, NMOE_CONST), A_["moe_consts"]).then_inc(sem("router_loaded"), 16)
            act.dma_start(b_dn[0:NE, :], A_["b_dn"]).then_inc(sem("moe_loaded"), 16)
            for half in range(2):
                us = slice(4 * half, 4 * half + 4)
                act.wait_ge(sem("h2_ready"), half + 1)
                f(rv[:, us, real], h2T[:, us, :], ACT.Square).then_inc(sem("h2_squared"), 1)
            act.wait_ge(sem("product"), product("h2_sumsq", 1))
            f(rs2, bank(4, SEQ), ACT.Sqrt, scale=1.0 / D, bias=eps[:, 0:1]).then_inc(sem("h2_std"), 1)
            act.wait_ge(sem("product"), product("h2_sumsq", 1))
            act.wait_ge(sem("b_gu_cleared"), 1)
            act.dma_start(b_gu[0:NE, :], A_["b_gu"]).then_inc(sem("moe_loaded"), 16)
            act.dma_start(g_fin[:, :], A_["norm_final_g"].broadcast_to((P, D))).then_inc(sem("moe_loaded"), 16)
            act.wait_ge(sem("top_ready"), 1)
            for blk in range(2):
                own.link(f(negmax[:, blk:blk + 1], top[:, blk, 0:1], ACT.Copy, scale=-1.0))
                ins = f(probs[:, blk, :], top[:, blk, 0:TOPK], ACT.Exp, bias=negmax[:, blk:blk + 1],
                        accum_out=psums[:, blk:blk + 1])
                ins.then_inc(sem("probs_ready"), 1)
            for blk in range(2):
                act.wait_ge(sem("product"), product("u2_turned", blk + 1))
                f(u2[:, blk, :], bank(4 + 2 * blk, D), ACT.Copy).then_inc(sem("u2_kept"), 1)
            for blk in range(2):
                act.wait_ge(sem("product"), product("h2_turned", blk + 1))
                f(acc[:, blk, :], bank(2 + 2 * blk, D), ACT.Copy).then_inc(sem("h2_kept"), 1)

            def keep_x(n):
                act.wait_ge(sem("gathered"), n)
                f(xg, bank(2, 512), ACT.Copy).then_inc(sem("xg_ready"), 1)
                act.wait_ge(sem("x_turned"), n)
                f(xT.rearrange("p a b c -> p (a b c)"), bank(3, 512), ACT.Copy).then_inc(sem("x_ready"), 1)

            keep_x(1)
            act.wait_ge(sem("product"), product("comb_turned", 1))
            f(combT[0:NE, :, :], bank(1, 2, P)[0:NE, :, :], ACT.Copy).then_inc(sem("combT_ready"), 1)
            act.wait_ge(sem("items_ready"), 1)
            n_items = act.value_load(nitems.bitcast(i32)[0:1, 0:1], min_val=NE, max_val=ITEMS)
            with act.Fori(0, n_items) as w:
                act.wait_ge(sem("gate_clamped"), w + 1)
                f(h_sig, h_gate, ACT.Sigmoid, scale=ALPHA).then_inc(sem("gate_sigmoid"), 1)
                keep_x(w + 2)
                act.wait_ge(sem("scat_turned"), w + 1)
                f(scatT.rearrange("p a b -> p (a b)"), bank(4, 2 * P), ACT.Copy).then_inc(sem("scatT_ready"), 1)
                after(act, "act_turned", w + 1)
                f(actT.rearrange("p a b c -> p (a b c)"), bank(2, 512), ACT.Copy).then_inc(sem("actT_ready"), 1)
                act.wait_ge(sem("slot5_free"), w + 1)
                f(ye, bank(3, 512), ACT.Copy).then_inc(sem("ye_ready"), 1)
            after(act, "acc_added", n_items + 1)
            for blk in range(2):
                own.done(f(fin[:, blk, :], acc[:, blk, :], ACT.Square, accum_out=fss[:, blk:blk + 1]))
            own.wait()
            f(frs, fss, ACT.Sqrt, scale=1.0 / D, bias=eps[:, 0:1]).then_inc(sem("final_std"), 1)

        @block.vector
        def _(dve):
            v = nc.vector
            own = Own(dve, "dve_own")
            link, done = own.link, own.done
            credit(dve, "gla_qk_evacuated", "rkv_evacuated", "act_ready")
            done(v.memset(eps[:, 0:1], NORM_EPS))
            done(v.memset(eps[:, 1:2], RWKV_GN_EPS))
            own.wait()
            v.memset(eps[:, 2:3], 1.0).then_inc(sem("dve_eps"), 1)
            dve.wait_ge(sem("params_loaded"), 32)
            v.tensor_scalar(om, par[:, MU:], -1.0, 1.0, ALU.mult, ALU.add).then_inc(sem("one_minus"), 1)
            dve.wait_ge(sem("h_std"), 1)
            link(v.reciprocal(rs1, rs1))
            for k in range(KC):
                v.scalar_tensor_tensor(uT[:, k, :], hT[:, k, :], pcol("norm_mix_g", k), rs1, ALU.mult, ALU.mult
                                       ).then_inc(sem("u_ready"), 1)
            for z in (gq, gk, gv, rb, rv):
                done(v.memset(z[:, :, 0:PAD], 0.0))
            v.memset(ra[:, :, 0:PAD], 0.0).then_inc(sem("pads_cleared"), 1)
            smalls = ((waT, 128, "mu_wa", 0), (sg[:, 0, :], 128, "mu_g", 0), (sg[:, 1, :], 32, "mu_g", 1))
            for n, (dst, rows, mu, m) in enumerate(smalls):
                dve.wait_ge(sem("small_part"), n + 1)
                v.scalar_tensor_tensor(dst[0:rows, 1:], bank(1 + n, T)[0:rows, 0:T - 1], pcol(mu, m, rows),
                                       dst[0:rows, 1:], ALU.mult, ALU.add).then_inc(sem("small_evacuated"), 1)
            for h in range(GH):
                dve.wait_ge(sem("gate_read"), h + 1)
                v.tensor_scalar(g_min[:, h, :], bank(h, T), pcol("b_gla_a", h), 0.0, ALU.add, ALU.min
                                ).then_inc(sem("gate_min_read"), 1)
            dve.wait_ge(sem("gate_log"), 1)
            dve.wait_ge(sem("gate_min_read"), GH)
            own.wait()
            link(v.tensor_tensor(gq[:, :, PAD:], g_min, g_abs, ALU.subtract))
            for h in range(GH):
                done(v.tensor_tensor_scan(gk[:, h, :], scan_mask, gq[:, h, :], 0.0, ALU.mult, ALU.add))
            own.wait()

            def chunks_of(x, n):
                return x.rearrange("p n (c t) -> p (n c) t", t=CHUNK)

            def spread(x, n):
                return chunks_of(x, n)[:, :, CHUNK // 2 - 1:CHUNK // 2].broadcast_to((P, n * NCHUNK, CHUNK))

            def boundary(dst, x, n):
                by = x.rearrange("p n (c t) -> p n c t", t=CHUNK)
                link(v.tensor_tensor(dst.rearrange("p n (c o) -> p n c o", o=1), by[:, :, :, CHUNK - 1:CHUNK],
                                     by[:, :, :, CHUNK // 2 - 1:CHUNK // 2], ALU.subtract))
                link(v.tensor_tensor(dst[:, :, 0:NCHUNK - 1].rearrange("p n (c o) -> p n c o", o=1),
                                     dst[:, :, 0:NCHUNK - 1].rearrange("p n (c o) -> p n c o", o=1),
                                     by[:, :, 1:, CHUNK // 2 - 1:CHUNK // 2], ALU.add))

            boundary(coefg, gk, GH)
            v.tensor_tensor(chunks_of(gq, GH), chunks_of(gk, GH), spread(gk, GH), ALU.subtract).then_inc(sem("g_log_decay"), 1)
            dve.wait_ge(sem("lora_evacuated"), 2 * KC)
            for m in range(KC):
                done(v.tensor_tensor_scan(rr[:, m, :], scan_mask, ra[:, m, :], 0.0, ALU.mult, ALU.add))
            own.wait()
            boundary(coefr, rr, KC)
            link(v.tensor_tensor(chunks_of(rk, KC), chunks_of(rr, KC), spread(rr, KC), ALU.subtract))
            v.tensor_tensor(ra, rk, ra, ALU.subtract).then_inc(sem("r_log_decay"), 1)
            for m in range(KC):
                done(v.tensor_scalar(rv[:, m, PAD:], rb[:, m, PAD:], pcol("k_a", m), omcol("k_a", m), ALU.mult, ALU.add))
            own.wait()
            dve.wait_ge(sem("g_decay"), 3)
            done(v.memset(gq[:, :, 0:PAD], 0.0))
            done(v.memset(gk[:, :, 0:PAD], 0.0))
            own.wait()
            with dve.Fori(0, 2) as i:
                for odd in range(2):
                    dve.wait_ge(sem("gla_projected"), 6 * i + 3 * odd + 2)
                    h = 2 * i + odd
                    q = gq[:, ds(h, 1), PAD:].rearrange("p a t -> p (a t)")
                    k = gk[:, ds(h, 1), PAD:].rearrange("p a t -> p (a t)")
                    v.scalar_tensor_tensor(q, bank(4 * odd, T), GDK ** -0.5, q, ALU.mult, ALU.mult)
                    v.tensor_tensor(k, bank(4 * odd + 1, T), k, ALU.mult).then_inc(sem("gla_qk_evacuated"), 1)
            dve.wait_ge(sem("r_decay"), 4)
            link(v.tensor_tensor(rb, rb, rk, ALU.mult))
            link(v.tensor_tensor(rk, rv, rk, ALU.mult))
            done(v.memset(ra[:, :, 0:PAD], 0.0))
            v.memset(rr[:, :, 0:PAD], 0.0).then_inc(sem("rv_free"), 1)
            dve.wait_ge(sem("rv_free"), 1)
            own.wait()
            with dve.Fori(0, KC // 2) as i:
                own.enter(i, 18)
                for odd in range(2):
                    m = 2 * i + odd
                    rt, kt = rk_tmp[odd]
                    row = lambda x: x[:, ds(m, 1), PAD:].rearrange("p a t -> p (a t)")
                    k_k = par[:, ds(m + PARAMS["k_k"], 1)]
                    dve.wait_ge(sem("rkv_part"), 6 * i + 3 * odd + 1)
                    v.scalar_tensor_tensor(kt[:, 1:], bank(4 * odd, T)[:, 0:T - 1], par[:, ds(m + PARAMS["mu_k"], 1)],
                                           kt[:, 1:], ALU.mult, ALU.add).then_inc(sem("key_lerped"), 1)
                    dve.wait_ge(sem("key_lerped"), 2 * i + odd + 1)
                    done(v.tensor_tensor(row(rk), row(rk), kt, ALU.mult))
                    done(v.scalar_tensor_tensor(row(rb), kt, k_k, row(rb), ALU.mult, ALU.mult))
                    done(v.scalar_tensor_tensor(row(ra), kt, k_k, row(ra), ALU.mult, ALU.mult))
                    dve.wait_ge(sem("rkv_part"), 6 * i + 3 * odd + 2)
                    link(v.scalar_tensor_tensor(rt[:, 1:], bank(4 * odd + 1, T)[:, 0:T - 1], par[:, ds(m + PARAMS["mu_r"], 1)],
                                                rt[:, 1:], ALU.mult, ALU.add))
                    done(v.tensor_tensor(row(rr), row(rr), rt, ALU.mult))
                    dve.wait_ge(sem("rkv_part"), 6 * i + 3 * odd + 3)
                    done(v.scalar_tensor_tensor(row(rv)[:, 1:], bank(4 * odd + 2, T)[:, 0:T - 1],
                                                par[:, ds(m + PARAMS["mu_v"], 1)], row(rv)[:, 1:], ALU.mult, ALU.add))
                    dve.wait_ge(sem("key_norm"), 2 * i + odd + 1)
                    rn = key_rn[odd]
                    link(v.tensor_scalar(rn, rn, 1e-12, None, ALU.max))
                    link(v.reciprocal(rn, rn))
                    done(v.tensor_tensor(row(rb), row(rb), rn, ALU.mult))
                    v.scalar_tensor_tensor(row(ra), row(ra), -1.0, rn, ALU.mult, ALU.mult).then_inc(sem("rkv_evacuated"), 1)
            own.leave(KC // 2)
            after(dve, "rkv_evacuated", KC)
            own.wait()
            v.memset(g_state, 0.0)
            v.memset(invT[0], 0.0)
            v.memset(state, 0.0).then_inc(sem("state_ready"), 1)
            v.memset(invT[1], 0.0).then_inc(sem("factors_done"), 1)

            dve.wait_ge(sem("factors_done"), 1)
            mask = causal.rearrange("p (a b) -> p a b", a=1).broadcast_to((P, KC, 2 * CHUNK))

            def over_units(x):
                return x.broadcast_to((P, KC, TILE))

            def chunk_steps(n, sn, c, sc):
                prep, turn = n is not None, c is not None
                if prep:
                    cols = ds(CHUNK * n, CHUNK)
                    v.tensor_copy(c_ar[sn][:, :, 0:CHUNK], ra[:, :, cols])
                    v.tensor_copy(c_ar[sn][:, :, CHUNK:], rr[:, :, cols])
                    v.tensor_copy(c_b, rb[:, :, cols]).then_inc(sem("staged_dve"), 1)
                    dve.wait_ge(sem("scores_b"), n + 1)
                    v.tensor_tensor(c_mb[sn], bank(0, KC, 2 * CHUNK), mask, ALU.mult).then_inc(sem("mask_b_done"), 1)
                    dve.wait_ge(sem("mask_b_done"), n + 1)
                    link(v.tensor_scalar(low, c_mb[sn][:, :, 0:TILE], parity[:, 0:1], None, ALU.mult))
                    v.scalar_tensor_tensor(low, c_mb[sn][:, :, TILE:CHUNK], parity[:, 1:2], low, ALU.mult, ALU.add
                                           ).then_inc(sem("low_ready"), 1)
                    dve.wait_ge(sem("low_ready"), n + 1)
                    link(v.tensor_tensor(tileT, low, over_units(levels[:, 0:1, :]), ALU.mult))
                    link(v.tensor_tensor(tileT, tileT, over_units(tile_ident.rearrange("p (a b) -> p a b", a=1)), ALU.add))
                    v.transpose(tile.rearrange("p a b -> p (a b)"), tileT.rearrange("p a b -> p (a b)")
                                ).then_inc(sem("inv_ready"), 1)
                    dve.wait_ge(sem("scores_k"), n + 1)
                    v.tensor_tensor(c_mk[sn], bank(2, KC, 2 * CHUNK), mask, ALU.mult).then_inc(sem("mask_k_done"), 1)
                    for l in (1, 2):
                        double(n, l)
                if turn and prep:
                    dve.wait_ge(sem("state_product"), c + 1)
                    link(v.tensor_tensor(state, bank(7, KC, CHUNK), state, ALU.add))
                    v.tensor_tensor(state, state, coefr[:, :, ds(c, 1)].broadcast_to((P, KC, CHUNK)), ALU.mult
                                    ).then_inc(sem("state_ready"), 1)
                if prep:
                    double(n, 3)
                    double(n, 4)
                    for q in range(4):
                        rows, half = slice(TILE * q, TILE * q + TILE), slice(TILE * (q % 2), TILE * (q % 2) + TILE)
                        done(v.tensor_copy(invT[sn][rows, :, half], tileT[rows, :, :]))
                    dve.wait_ge(sem("step_product"), LEVELS * n + LEVELS)
                    for q in (0, 2):
                        rows = slice(TILE * q, TILE * q + TILE)
                        ins = v.tensor_copy(invT[sn][rows, :, TILE:CHUNK], bank(5, KC, TILE)[rows, :, :])
                    ins.then_inc(sem("inverse_ready"), 1)
                    dve.wait_ge(sem("g_increment"), n + 1)
                    link(v.tensor_tensor(g_state, bank(0, GH, GDV), g_state, ALU.add))
                    v.tensor_tensor(g_state, g_state, coefg[:, :, ds(n, 1)].broadcast_to((P, GH, GDV)), ALU.mult
                                    ).then_inc(sem("g_state_ready"), 1)

            def double(n, l):
                dve.wait_ge(sem("step_product"), LEVELS * n + l)
                link(v.tensor_tensor(tileT, bank(5, KC, TILE), tileT, ALU.add))
                v.transpose(tile.rearrange("p a b -> p (a b)"), tileT.rearrange("p a b -> p (a b)")
                            ).then_inc(sem("inv_ready"), 1)

            chunk_steps(0, 0, None, None)
            with dve.Fori(0, NCHUNK // 2) as i:
                own.enter(i, 26)
                for odd in range(2):
                    chunk_steps(2 * i + odd + 1, 1 - odd, 2 * i + odd, odd)
            own.leave(NCHUNK // 2)

            real = slice(CHUNK, TP)
            dve.wait_ge(sem("staged_act"), NCHUNK)
            dve.wait_ge(sem("staged_dve"), NCHUNK)
            link(v.tensor_tensor(rr[:, :, real], rr[:, :, real], rk[:, :, real], ALU.mult))
            for m in range(KC):
                ins = v.tensor_scalar(rr[:, m, real], rr[:, m, real], pcol("r_k", m), None, ALU.mult)
                if m < KC - 1:
                    done(ins)
            ins.then_inc(sem("bonus_in"), 1)
            dve.wait_ge(sem("g_std"), 1)
            link(v.reciprocal(g_std, g_std))
            for u in range(KC):
                done(v.scalar_tensor_tensor(gv[:, u, real], gv[:, u, real], pcol("gla_norm_g", u % 2), g_std[:, u // 2, :],
                                            ALU.mult, ALU.mult))
            dve.wait_ge(sem("r_sigmoid"), 1)
            for n in range(2):
                done(v.tensor_tensor(late(n), late(n), r_sig[:, 16 * n:16 * n + 16, :], ALU.mult))
            own.wait()
            for n in range(2):
                out = in_rows(gv[:, 4 * n:4 * n + 4, real])
                ins = v.tensor_tensor(out, out, by_unit(n), ALU.mult)
                if n == 0:
                    done(ins)
            ins.then_inc(sem("g_branch"), 1)
            dve.wait_ge(sem("product"), product("y_sum", 1))
            v.scalar_tensor_tensor(ra[:, :, real], bank(4, KC, SEQ), -1.0 / HEAD, ra[:, :, real], ALU.mult, ALU.add
                                   ).then_inc(sem("y_centred"), 1)
            dve.wait_ge(sem("y_std"), 1)
            dve.wait_ge(sem("y_centred"), 1)
            link(v.reciprocal(rk[:, :, real], rk[:, :, real]))
            v.tensor_tensor(ra[:, :, real], ra[:, :, real], rk[:, :, real], ALU.mult).then_inc(sem("y_normed"), 1)
            dve.wait_ge(sem("product"), product("bonus_sum", 1))
            v.tensor_tensor(rv[:, :, real], bank(4, KC, SEQ), rv[:, :, real], ALU.mult).then_inc(sem("bonus_done"), 1)
            dve.wait_ge(sem("y_affine"), 1)
            dve.wait_ge(sem("bonus_done"), 1)
            link(v.tensor_tensor(ra[:, :, real], ra[:, :, real], rv[:, :, real], ALU.add))
            dve.wait_ge(sem("product"), product("out_gate", 1))
            v.tensor_tensor(ra[:, :, real], bank(4, KC, SEQ), ra[:, :, real], ALU.mult).then_inc(sem("r_branch"), 1)
            dve.wait_ge(sem("gates_ready"), 2)
            for odd, j, first in ((0, 0, 6), (1, 3, 5)):
                us = slice(4 * odd, 4 * odd + 4)
                dve.wait_ge(sem(f"slot{j}_free"), first)
                done(v.tensor_tensor(in_rows(rr[:, us, real]), in_rows(bank(2 - 2 * odd, 4, SEQ)), by_unit(2 + odd), ALU.mult))
            for odd, j, first in ((0, 0, 7), (1, 3, 6)):
                us = slice(4 * odd, 4 * odd + 4)
                dve.wait_ge(sem(f"slot{j}_free"), first)
                link(v.tensor_tensor(in_rows(rk[:, us, real]), in_rows(bank(4 + 2 * odd, 4, SEQ)), by_unit(4 + odd), ALU.mult))
                ins = v.tensor_tensor(rr[:, us, real], rr[:, us, real], rk[:, us, real], ALU.add)
                if odd == 0:
                    done(ins)
            ins.then_inc(sem("mixed"), 1)
            dve.wait_ge(sem("h_loaded"), 32)
            for odd, j, first in ((0, 0, 8), (1, 3, 7)):
                us = slice(4 * odd, 4 * odd + 4)
                dve.wait_ge(sem(f"slot{j}_free"), first)
                v.tensor_tensor(h2T[:, us, :], bank(2 * odd, 4, SEQ), h2T[:, us, :], ALU.add).then_inc(sem("h2_ready"), 1)
            v.memset(b_gu, 0.0).then_inc(sem("b_gu_cleared"), 1)
            dve.wait_ge(sem("h2_std"), 1)
            link(v.reciprocal(rs2, rs2))
            dve.wait_ge(sem("h2_ready"), 2)
            for k in range(KC):
                v.scalar_tensor_tensor(u2T[:, k, :], h2T[:, k, :], pcol("norm_ffn_g", k), rs2, ALU.mult, ALU.mult
                                       ).then_inc(sem("u2_ready"), 1)
            for x in (h_up, h_gate, scatT, ye, item_b[:, 0:NE]):
                done(v.memset(x, 0.0))
            dve.wait_ge(sem("router_loaded"), 48)
            done(v.tensor_copy(item_e[:, 0:NE], ids[:, 0:NE]))
            dve.wait_ge(sem("product"), product("logits", 1))
            link(v.tensor_copy(logits, bank(1, 2, NE)))
            for blk in range(2):
                done(v.max(top[:, blk, :], logits[:, blk, :]))
            own.wait()
            for blk in range(2):
                ins = v.max_index(top_i.bitcast(u32)[:, blk, :], top[:, blk, :], logits[:, blk, :])
                if blk == 0:
                    done(ins)
            ins.then_inc(sem("top_ready"), 1)
            dve.wait_ge(sem("top_ready"), 1)
            own.wait()
            link(v.tensor_copy(top_f, top_i.bitcast(u32)))
            for blk in range(2):
                for k in range(TOPK):
                    done(v.tensor_scalar(one_hot[:, blk, k, :], ids[:, 0:NE], top_f[:, blk, k:k + 1], None, ALU.is_equal))
            own.wait()
            link(v.tensor_tensor(weighted[:, :, 0:2, :], one_hot[:, :, 0:2, :], one_hot[:, :, 2:4, :], ALU.add))
            v.tensor_tensor(chosen.rearrange("p a (b e) -> p a b e", b=1), weighted[:, :, 0:1, :], weighted[:, :, 1:2, :],
                            ALU.add).then_inc(sem("chosen_ready"), 1)
            dve.wait_ge(sem("chosen_ready"), 1)
            dve.wait_ge(sem("product"), product("counted", 1))
            link(v.scalar_tensor_tensor(pos, bank(0, 3, NE)[:, 0:2, :], 1.0, chosen, ALU.add, ALU.mult))
            done(v.tensor_scalar(pos, pos, -1.0, None, ALU.add))
            link(v.tensor_copy(count, bank(0, 3, NE)[:, 2, :]))
            for blk in range(2):
                ins = v.tensor_scalar(gat[:, blk, :], slot_ids[:, 0:SLOTS], pos[:, blk, 0:1], None, ALU.is_equal)
                if blk == 0:
                    done(ins)
            ins.then_inc(sem("gather_ready"), 1)
            link(v.tensor_scalar(extra, count, float(SLOTS), None, ALU.is_gt))
            for b in range(2, BLOCKS):
                link(v.tensor_scalar(cmp_e, count, float(SLOTS * b), None, ALU.is_gt))
                link(v.tensor_tensor(extra, extra, cmp_e, ALU.add))
            link(v.tensor_tensor_scan(ends, ones[:, 0:NE], extra, 0.0, ALU.mult, ALU.add))
            link(v.tensor_scalar(cmp_e, ends, row_id[:, 0:1], None, ALU.is_le))
            done(v.reduce_sum(item_eb[:, 0:1], cmp_e, AX.X))
            link(v.tensor_tensor(cmp_x, cmp_e, extra, ALU.mult))
            link(v.reduce_sum(item_eb[:, 1:2], cmp_x, AX.X))
            link(v.scalar_tensor_tensor(item_eb[:, 1:2], item_eb[:, 1:2], -1.0, row_id[:, 0:1], ALU.mult, ALU.add))
            link(v.tensor_scalar(item_eb[:, 1:2], item_eb[:, 1:2], 1.0, float(BLOCKS - 1), ALU.add, ALU.min))
            link(v.tensor_scalar(item_eb[:, 0:1], item_eb[:, 0:1], float(NE - 1), None, ALU.min))
            link(v.tensor_scalar(bc_e, ones, item_eb[:, 0:1], None, ALU.mult))
            v.tensor_scalar(bc_b, ones, item_eb[:, 1:2], None, ALU.mult).then_inc(sem("extra_items"), 1)
            link(v.tensor_scalar(nitems[:, 1:2], ends[:, NE - 1:NE], float(NE), None, ALU.add))
            done(v.tensor_copy(nitems.bitcast(i32)[:, 0:1], nitems[:, 1:2]))
            dve.wait_ge(sem("product"), product("items_spread", 1))
            done(v.tensor_copy(item_e[:, NE:], bank(0, 2, P)[:, 0, :]))
            link(v.tensor_scalar(item_b[:, NE:], bank(0, 2, P)[:, 1, :], float(2 * SLOTS), None, ALU.mult))
            link(v.tensor_copy(item_ei.bitcast(i32), item_e))
            v.tensor_copy(item_bi.bitcast(i32), item_b).then_inc(sem("items_ready"), 1)
            dve.wait_ge(sem("probs_ready"), 2)
            link(v.reciprocal(psums, psums))
            for blk in range(2):
                done(v.tensor_scalar(probs[:, blk, :], probs[:, blk, :], psums[:, blk:blk + 1], None, ALU.mult))
            own.wait()
            for blk in range(2):
                for k in range(TOPK):
                    done(v.tensor_scalar(weighted[:, blk, k, :], one_hot[:, blk, k, :], probs[:, blk, k:k + 1], None, ALU.mult))
            own.wait()
            link(v.tensor_tensor(one_hot[:, :, 0:2, :], weighted[:, :, 0:2, :], weighted[:, :, 2:4, :], ALU.add))
            v.tensor_tensor(comb.rearrange("p a (b e) -> p a b e", b=1), one_hot[:, :, 0:1, :], one_hot[:, :, 1:2, :],
                            ALU.add).then_inc(sem("comb_ready"), 1)
            dve.wait_ge(sem("comb_ready"), 1)
            dve.wait_ge(sem("items_ready"), 1)

            def item(w):
                e = dve.value_load(item_ei.bitcast(i32)[0:1, ds(w, 1)], min_val=0, max_val=NE - 1)
                first = dve.value_load(item_bi.bitcast(i32)[0:1, ds(w, 1)], min_val=0, max_val=(BLOCKS - 1) * 2 * SLOTS)
                return e, first

            def select_tokens(e, first):
                for blk in range(2):
                    ins = v.tensor_scalar(gat[:, blk, :], slot_ids[:, ds(first, SLOTS)], pos[:, blk, ds(e, 1)], None,
                                          ALU.is_equal)
                ins.then_inc(sem("gather_ready"), 1)

            def select_results(w, e, first):
                for blk in range(2):
                    v.tensor_scalar(scat[:, blk, :], slot_ids[:, ds(first, 2 * SLOTS)], pos[:, blk, ds(e, 1)],
                                    comb[:, blk, ds(e, 1)], ALU.is_equal, ALU.mult)
                v.tensor_scalar(sel, row_id[:, 0:1].broadcast_to((P, SLOTS)), item_e[:, ds(w, 1)], None, ALU.is_equal
                                ).then_inc(sem("select_ready"), 1)

            e, first = item(0)
            select_results(0, e, first)
            v.memset(h_sig[:, 0:1], 0.0).then_inc(sem("loop_buffers"), 1)
            dve.wait_ge(sem("product"), product("dn_bias", 1))
            dve.wait_ge(sem("h2_kept"), 2)
            v.tensor_tensor(acc.rearrange("p a d -> p (a d)"), bank(4, 2 * D), acc.rearrange("p a d -> p (a d)"), ALU.add
                            ).then_inc(sem("acc_added"), 1)
            dve.wait_ge(sem("acc_added"), 1)
            n_items = dve.value_load(nitems.bitcast(i32)[0:1, 0:1], min_val=NE, max_val=ITEMS)

            def add_scattered(n):
                dve.wait_ge(sem("scattered"), n)
                for q in range(4):
                    part = acc.rearrange("p a (h d) -> p (a h) d", h=2)[:, q, :]
                    ins = v.tensor_tensor(part, bank(4 + q, 512), part, ALU.add)
                ins.then_inc(sem("acc_added"), 1)

            with dve.Fori(0, n_items) as w:
                own.enter(w, 2)
                e, first = item(w + 1)
                dve.wait_ge(sem("gathered"), w + 1)
                select_tokens(e, first)
                dve.wait_ge(sem("slot3_free"), w + 8)
                after(dve, "gate_sigmoid", w)
                after(dve, "act_turned", w)
                v.tensor_scalar(h_gate, bank(0, 512), LIMIT, None, ALU.min).then_inc(sem("gate_clamped"), 1)
                link(v.tensor_scalar(h_up, bank(1, 512), LIMIT, -LIMIT, ALU.min, ALU.max))
                dve.wait_ge(sem("gate_clamped"), w + 1)
                link(v.scalar_tensor_tensor(h_up, h_up, 1.0, h_gate, ALU.add, ALU.mult))
                after(dve, "gate_sigmoid", w + 1)
                v.tensor_tensor(h_up, h_up, h_sig, ALU.mult).then_inc(sem("act_ready"), 1)
                add_scattered(w + 1)
                dve.wait_ge(sem("scat_turned"), w + 1)
                select_results(w + 1, e, first)
            own.leave(0)
            add_scattered(n_items + 1)
            dve.wait_ge(sem("final_std"), 1)
            v.reciprocal(frs, frs).then_inc(sem("final_rstd"), 1)
            dve.wait_ge(sem("final_rstd"), 1)
            for blk in range(2):
                v.scalar_tensor_tensor(fin[:, blk, :], acc[:, blk, :], frs[:, blk:blk + 1], g_fin, ALU.mult, ALU.mult
                                       ).then_inc(sem("final_ready"), 1)

        @block.gpsimd
        def _(pool):
            g = nc.gpsimd
            pool.wait_ge(sem("factors_done"), 1)

            def chunk_extras(n):
                cols = ds(CHUNK * n, CHUNK)
                if not isinstance(n, int):
                    pool.wait_ge(sem("g_increment"), n)
                g.tensor_copy(g_v, gv[:, :, cols])
                g.tensor_copy(g_k, gk[:, :, cols])
                g.tensor_copy(g_q, gq[:, :, cols]).then_inc(sem("staged_pool"), 1)
                pool.wait_ge(sem("low_ready"), n + 1)
                for l in range(1, LEVELS):
                    ins = g.tensor_tensor(low_at[:, l - 1, :, :], low, levels[:, l:l + 1, :].broadcast_to((P, KC, TILE)),
                                          ALU.mult)
                ins.then_inc(sem("level_ready"), 1)
                pool.wait_ge(sem("g_scores_read"), n + 1)
                apart(pool, "pool_passed")
                g.affine_select(out=g_a[0:64, :, :], in_=g_a[0:64, :, :], compare_op=ALU.is_ge, fill=0.0, base=0,
                                pattern=[[0, GH], [1, CHUNK]], channel_multiplier=-1).then_inc(sem("g_a_ready"), 1)

            chunk_extras(0)
            with pool.Fori(1, NCHUNK) as n:
                chunk_extras(n)


def kernel(**inputs):
    import concourse.bacc as _bacc
    from concourse import mybir as _mybir
    from concourse.bass_utils import run_bass_kernel_spmd as _run

    x = {k: np.asarray(v) for k, v in inputs.items()}
    f = {k: (v[0] if k not in ("x", "meta_tokens", "norm_final_g") else v) for k, v in x.items()}

    def kmajor(w):
        return np.ascontiguousarray(w.reshape(KC, P, -1).transpose(1, 0, 2))

    w_in = f["w_in"]
    names = ("gq", "gk", "gv", "gr", "ga", "rr", "rk", "rv", "rw", "ra", "rg", "gate_gla", "gate_rwkv")
    sizes = (512, 512, 1024, 1024, 16, 1024, 1024, 1024, 64, 64, 160, 1024, 1024)
    ends = np.cumsum(sizes)
    W = {n: w_in[:, e - s:e] for n, s, e in zip(names, sizes, ends)}

    def units(v):
        v = np.asarray(v).reshape(-1)
        if v.size % P:
            v = np.concatenate([v, np.zeros(-v.size % P, v.dtype)])
        return v.reshape(-1, P).T

    consts, moe_consts = constants()
    mid = [W[n][:, 512 * j:512 * j + 512] for n in ("gr", "gate_gla", "gate_rwkv") for j in range(2)]
    mid += [f[n][:, 512 * j:512 * j + 512] for n in ("w_gla_o", "w_rwkv_o", "w_out") for j in range(2)]
    f["mu_wa"] = np.concatenate([f["mu_w"], f["mu_a"]], -1)
    arrays = {
        "hT": kmajor(np.concatenate([x["meta_tokens"], x["x"][0]], 0).T),
        "consts": consts,
        "moe_consts": moe_consts,
        "params": np.ascontiguousarray(np.concatenate([units(f[n]) for n in PARAMS], 1)),
        "w_small": kmajor(np.concatenate([W[n] for n in ("rw", "ra", "rg", "ga")], 1)),
        "w_gla_a2": f["w_gla_a2"], "w_wa2": np.concatenate([f["w_decay2"], f["w_a2"]], 0), "w_gate2": f["w_gate2"],
        "w_gla": np.stack([kmajor(np.concatenate([W["gq"][:, P * h:P * h + P], W["gk"][:, P * h:P * h + P],
                                                  W["gv"][:, GDV * h:GDV * h + GDV]], 1)) for h in range(GH)]),
        "w_rwkv": np.stack([kmajor(np.concatenate([W[n][:, P * m:P * m + P] for n in ("rk", "rr", "rv")], 1))
                            for m in range(KC)]),
        "w_mid": np.stack([kmajor(w) for w in mid]),
        "w_router": kmajor(f["w_router"]),
        "b_router": f["b_router"].reshape(1, NE),
        "w_gu": f["w_exp_gu"], "b_gu": f["b_exp_gu"], "w_dn": f["w_exp_down"], "b_dn": f["b_exp_down"],
        "norm_final_g": f["norm_final_g"].reshape(1, D),
    }
    nc = _bacc.Bacc("TRN2", target_bir_lowering=False, num_devices=1)
    ins, aps = {}, {}
    for name, a in arrays.items():
        a = np.ascontiguousarray(a)
        ins[f"in_{name}"] = a
        aps[name] = nc.dram_tensor(f"in_{name}", a.shape, _mybir.dt.from_np(a.dtype), kind="ExternalInput").ap()
    aps["out"] = nc.dram_tensor("out_0", (SEQ, D), _mybir.dt.float32, kind="ExternalOutput").ap()
    block_kernel(nc, aps)
    r = _run(nc, [ins], core_ids=[0])
    return r.results[0]["out_0"].reshape(1, SEQ, D)
```

```python
import concourse.bass as bass
from concourse import mybir
from contextlib import ExitStack
import numpy as np

P = 128
D = 1024
SEQ = 256
N_META = 16
T = SEQ + N_META
KC = D // P
CHUNK = 64
PAD = -N_META % CHUNK
NCHUNK = (T + PAD) // CHUNK
TP = NCHUNK * CHUNK
GH, GDK, GDV = 4, 128, 256
HEAD = 64
NORM_EPS = 1e-5
RWKV_GN_EPS = 64e-5
GATE_NORM = 16.0
DECAY_SCALE = float(np.exp(-0.5))
NE = 32
TOPK = 4
FE = 1024
LIMIT = 7.0
ALPHA = 1.702
SLOTS = 64
BLOCKS = SEQ // SLOTS
ITEMS = NE + SEQ * TOPK // SLOTS + 1
PIECE = 4096
RING = 6
TILE = 32
LEVELS = 5

PARAMS = {}
_at = 0
for _name, _n in (("norm_mix_g", 8), ("b_gla_a", 4), ("gla_norm_g", 2), ("b_decay", 8), ("b_a", 8),
                  ("k_k", 8), ("r_k", 8), ("ln_x_g", 8), ("ln_x_b", 8), ("norm_ffn_g", 8),
                  ("mu_r", 8), ("mu_k", 8), ("mu_v", 8), ("mu_wa", 1), ("mu_g", 2), ("k_a", 8)):
    PARAMS[_name] = _at
    _at += _n
NPARAM = _at
MU = PARAMS["mu_r"]

CONSTS = {}
_at = 0
for _name, _n in (("ident", P), ("ones", P), ("half_ones", P), ("causal", 2 * CHUNK),
                  ("levels", LEVELS * TILE), ("tile_ident", TILE), ("parity", 2), ("scan", TP)):
    CONSTS[_name] = _at
    _at += _n
NCONST = _at
MOE_CONSTS = {}
_at = 0
for _name, _n in (("before", P), ("slot_ids", BLOCKS * 2 * SLOTS), ("row_id", 1), ("ids", P)):
    MOE_CONSTS[_name] = _at
    _at += _n
NMOE_CONST = _at


def constants():
    p = np.arange(P)[:, None]
    s, t = p % TILE, np.arange(TILE)[None, :]
    levels = []
    for l in range(LEVELS):
        b = 1 << l
        levels.append((t // (2 * b) == s // (2 * b)) & (t // b % 2 == 1) & (s // b % 2 == 0))
    tile_ident, parity = s == t, p // TILE % 2 == np.arange(2)[None, :]
    s, t = p % CHUNK, np.arange(CHUNK)[None, :]
    scan = np.broadcast_to(np.arange(TP)[None, :] % CHUNK != 0, (P, TP))
    parts = [np.eye(P), np.ones((P, P)), p // HEAD == np.arange(P)[None, :] // HEAD,
             np.concatenate([s < t, s <= t], 1), *levels, tile_ident, parity, scan]
    slots = np.tile(np.arange(SLOTS)[None, :], (P, 2))
    moe = [p < np.arange(P)[None, :], *[slots + SLOTS * b for b in range(BLOCKS)], p,
           np.broadcast_to(np.arange(P)[None, :], (P, P))]
    return (np.concatenate([np.asarray(x, np.float32) for x in parts], 1),
            np.concatenate([np.asarray(x, np.float32) for x in moe], 1))


def block_kernel(nc, A):
    f32, i32, u32 = mybir.dt.float32, mybir.dt.int32, mybir.dt.uint32
    ALU, ACT, AX = mybir.AluOpType, mybir.ActivationFunctionType, mybir.AxisListType
    ds = bass.ds

    with ExitStack() as ctx:
        ctx.enter_context(nc.allow_non_contiguous_dma("rows of a piece"))
        FLOATS = 53000
        arena = ctx.enter_context(nc.sbuf_tensor("arena", [P, FLOATS], f32))
        ps = ctx.enter_context(nc.psum_tensor("ps", [P, 8 * 512], f32))
        sems = {}

        def sem(name):
            if name not in sems:
                sems[name] = ctx.enter_context(nc.semaphore(name))
            return sems[name]

        def at(off, *shape):
            n = int(np.prod(shape))
            assert off + n <= FLOATS
            v = arena[:, off:off + n]
            if len(shape) == 2:
                v = v.rearrange("p (a b) -> p a b", a=shape[0])
            elif len(shape) == 3:
                v = v.rearrange("p (a b c) -> p a b c", a=shape[0], b=shape[1])
            return v

        def bank(b, *shape):
            n = int(np.prod(shape))
            v = ps[:, 512 * b:512 * b + n]
            if len(shape) == 2:
                v = v.rearrange("p (a b) -> p a b", a=shape[0])
            elif len(shape) == 3:
                v = v.rearrange("p (a b c) -> p a b c", a=shape[0], b=shape[1])
            return v

        used = [0]

        def take(n):
            used[0] += n
            return used[0] - n

        ring = [take(PIECE) for _ in range(RING)]
        o_h, o_u = take(KC * T), take(KC * T)
        o_late = take(GH * TP)
        o_gk = take(GH * TP)
        o_rb = take(KC * TP)
        take(3 * KC * SEQ - (2 * GH + KC) * TP)
        o_gv, o_ra, o_rk, o_rr, o_rv = (take(KC * TP) for _ in range(5))
        o_const, o_par, o_om = take(NCONST), take(NPARAM), take(NPARAM - MU)
        o_coefg, o_coefr, o_sg = take(GH * NCHUNK), take(KC * NCHUNK), take(2 * T)
        eps = at(take(4), 4)
        o_x = take(FLOATS - used[0])

        hT, uT = at(o_h, KC, T), at(o_u, KC, T)
        gq, gk, gv = at(o_late, GH, TP), at(o_gk, GH, TP), at(o_gv, KC, TP)
        ra, rb, rk, rr, rv = (at(o, KC, TP) for o in (o_ra, o_rb, o_rk, o_rr, o_rv))
        late_rows = at(o_late, 4 * SEQ // CHUNK, TP)

        def late(n):
            if isinstance(n, int) and n == NCHUNK:
                return at(o_late + 4 * SEQ // CHUNK * TP, 4 * SEQ // CHUNK, CHUNK)
            return late_rows[:, :, ds(CHUNK * n, CHUNK)]

        def in_rows(x):
            return x.rearrange("p u (b t) -> p u b t", t=CHUNK)

        def by_unit(n):
            return late(n).rearrange("p (u b) t -> p u b t", u=4)

        par = at(o_par, NPARAM)
        om = at(o_om, NPARAM - MU)

        def pcol(name, m=0, n=P):
            return par[0:n, PARAMS[name] + m:PARAMS[name] + m + 1]

        def omcol(name, m=0, n=P):
            c = PARAMS[name] - MU + m
            return om[0:n, c:c + 1]

        def const(name, n):
            return at(o_const + CONSTS[name], n)

        ident, ones, half_ones = const("ident", P), const("ones", P), const("half_ones", P)
        causal = const("causal", 2 * CHUNK)
        scan_mask = const("scan", TP)
        levels = at(o_const + CONSTS["levels"], LEVELS, TILE)
        tile_ident, parity = const("tile_ident", TILE), const("parity", 2)
        coefg, coefr = at(o_coefg, GH, NCHUNK), at(o_coefr, KC, NCHUNK)
        sg = at(o_sg, 2, T)

        def piece(j, n, w):
            return at(ring[j], n, w)

        o_t = ring[4]
        w_wa2, w_gla_a2 = at(o_t, D), at(o_t + 2 * D, GH * GDK)
        waT, gaT = at(o_t + 2560, T), at(o_t + 2560 + T, T)
        GA = slice(32, 48)
        g_abs, g_min = at(o_t + 3376, GH, T), at(o_t + 4464, GH, T)
        key_sq, key_rn = ([at(o_x + 1024 + (2 * j + i) * T, T) for i in range(2)] for j in range(2))
        rk_tmp = [[at(o_t + 5552 + (2 * j + i) * T, T) for j in range(2)] for i in range(2)]
        o_s = ring[3]
        home = (tuple(o_s + 1024 * i for i in range(3)) + tuple(o_s + 3072 + 512 * i for i in range(4)),
                tuple(ring[0] + 1024 * i for i in range(3)) + (ring[0] + 3072, ring[0] + 3584, o_s + 5120, o_s + 5632))
        c_ar, c_mb, c_mk = ([at(home[s][i], KC, 2 * CHUNK) for s in range(2)] for i in range(3))
        t_b, t_k, t_v, invT = ([at(home[s][i], KC, CHUNK) for s in range(2)] for i in range(3, 7))
        c_b, c_k, c_v = (at(o_s + 6144 + 512 * i, KC, CHUNK) for i in range(3))
        c_r, c_sa = (at(o_s + 7680 + 512 * i, KC, CHUNK) for i in range(2))
        low, tile, tileT, prod = (at(o_s + 8704 + 256 * i, KC, TILE) for i in range(4))
        low_at = at(o_s + 9728, LEVELS - 1, KC, TILE)
        g_v = at(o_s + 10752, KC, CHUNK)
        g_q, g_k, g_a = (at(o_s + 11264 + 256 * i, GH, CHUNK) for i in range(3))
        tg_k = at(o_x, GH * GDK)
        crossed = at(o_x + 1024, KC, CHUNK)
        state = at(o_x + 512, KC, CHUNK)
        tg_v, g_state = at(o_h, GH * GDV), at(o_h + 1024, GH, GDV)
        w_gate2 = at(o_x, 2, D)
        sq = at(o_h, KC, SEQ)
        r_sig = at(o_h, 2 * 4 * SEQ // CHUNK, CHUNK)
        g_std = at(o_x + 2 * D, GH, SEQ)
        rv_sq, rs1 = at(o_rv, KC, T), at(o_rk, T)
        h2T = hT[:, :, N_META:]
        g_ffn = at(o_u, D)

        mused = [o_gv]

        def mtake(n):
            mused[0] += n
            assert mused[0] <= o_gv + 5 * KC * TP
            return mused[0] - n

        o_mc = mtake(NMOE_CONST)
        w_r = at(mtake(KC * NE), KC, NE)
        b_r = at(mtake(NE), NE)
        b_dn = at(mtake(D), D)
        assert mused[0] <= o_ra
        mused[0] = o_ra
        u2 = at(mtake(2 * D), 2, D)
        b_gu = at(mtake(2 * FE), 2 * FE)
        assert mused[0] <= o_rr
        acc = at(mtake(2 * D), 2, D)
        g_fin = at(mtake(D), D)
        before = at(o_mc + MOE_CONSTS["before"], P)
        slot_ids = at(o_mc + MOE_CONSTS["slot_ids"], BLOCKS * 2 * SLOTS)
        row_id = at(o_mc + MOE_CONSTS["row_id"], 1)
        ids = at(o_mc + MOE_CONSTS["ids"], P)
        logits, chosen, comb, pos = (at(mtake(2 * NE), 2, NE) for _ in range(4))
        rs2 = at(mtake(2), 2)
        top = at(mtake(16), 2, 8)
        top_i = at(mtake(16), 2, 8)
        top_f = at(mtake(16), 2, 8)
        probs, negmax, psums = at(mtake(8), 2, 4), at(mtake(2), 2), at(mtake(2), 2)
        one_hot, weighted = (at(mtake(2 * TOPK * NE), 2, TOPK, NE) for _ in range(2))
        count, extra, ends, cmp_e, cmp_x = (at(mtake(NE), NE) for _ in range(5))
        item_eb = at(mtake(2), 2)
        bc_e, bc_b = at(mtake(P), P), at(mtake(P), P)
        item_e = at(mtake(NE + P), NE + P)
        item_b = at(mtake(NE + P), NE + P)
        item_ei = at(mtake(NE + P), NE + P)
        item_bi = at(mtake(NE + P), NE + P)
        nitems = at(mtake(2), 2)
        sel = at(mtake(SLOTS), SLOTS)
        gat = at(mtake(2 * SLOTS), 2, SLOTS)
        scat = at(mtake(4 * SLOTS), 2, 2 * SLOTS)
        lused = [o_late]

        def ltake(n):
            lused[0] += n
            assert lused[0] <= o_late + 3 * KC * SEQ
            return lused[0] - n

        scatT = at(ltake(2 * P), 2, P)
        xg = at(ltake(512), 512)
        xT = at(ltake(512), 4, 2, SLOTS)
        h_gate, h_sig, h_up = (at(ltake(512), 512) for _ in range(3))
        actT = at(ltake(512), 4, 2, SLOTS)
        ye = at(ltake(512), 512)
        fin = at(ltake(2 * D), 2, D)
        fss, frs = at(ltake(2), 2), at(ltake(2), 2)

        class Own:

            def __init__(self, eng, name):
                self.eng, self.sem, self.base, self.n = eng, sem(name), 0, 0

            def done(self, ins):
                ins.then_inc(self.sem, 1)
                self.n += 1

            def wait(self):
                self.eng.wait_ge(self.sem, self.base + self.n)

            def link(self, ins):
                self.done(ins)
                self.wait()

            def enter(self, i, per):
                self.start, self.n, self.per = self.n, 0, per
                self.base = self.start + i * per

            def leave(self, trips):
                assert self.n == self.per, (self.n, self.per)
                self.base, self.n = 0, self.start + trips * self.per

        PRODUCTS = {"h_sumsq": 1, "small_projected": 2, "lora_projected": 8, "gate_projected": 4, "g_sumsq": 1, "y_sum": 1, "y_sumsq": 1, "bonus_sum": 1, "out_gate": 1, "logits": 1, "h2_sumsq": 1, "h2_turned": 2, "counted": 1, "items_spread": 1}

        def product(name, n=1):
            names = list(PRODUCTS)
            return sum(PRODUCTS[x] for x in names[:names.index(name)]) + n

        def credit(eng, *names):
            for name in names:
                eng.sem_inc(sem(name), 1)

        def after(eng, name, n):
            eng.wait_ge(sem(name), n + 1)

        SHORT = 3
        assert 2 ** (SHORT + 1) >= CHUNK - PAD

        def joins(n):
            return 0 if isinstance(n, int) and n == 0 else LEVELS * n - (LEVELS - SHORT)

        def inverses(n):
            return 0 if isinstance(n, int) and n == 0 else LEVELS * n - (LEVELS - SHORT - 1)

        def unit_before_last(eng, name, u):
            eng.wait_ge(sem(name), u + 1)

        def apart(eng, name):
            eng.sem_inc(sem(name), 1)

        block = ctx.enter_context(nc.Block())
        A_ = A

        @block.sync
        def _(sp):
            sp.dma_start(hT[:, :, :], A_["hT"]).then_inc(sem("h_loaded"), 16)
            sp.dma_start(at(o_const, NCONST), A_["consts"]).then_inc(sem("params_loaded"), 16)
            sp.dma_start(par, A_["params"]).then_inc(sem("params_loaded"), 16)
            sp.dma_start(piece(0, KC, 304), A_["w_small"]).then_inc(sem("slot0"), 16)
            sp.dma_start(w_wa2, A_["w_wa2"]).then_inc(sem("lora_loaded"), 16)
            sp.dma_start(w_gla_a2[GA, :], A_["w_gla_a2"]).then_inc(sem("lora_loaded"), 16)
            sp.dma_start(piece(1, KC, 512), A_["w_gla"][0]).then_inc(sem("slot1"), 16)
            sp.dma_start(piece(2, KC, 512), A_["w_gla"][1]).then_inc(sem("slot2"), 16)
            sp.dma_start(piece(3, KC, 384), A_["w_rwkv"][1]).then_inc(sem("slot3"), 16)
            sp.wait_ge(sem("slot0_free"), 1)
            sp.dma_start(piece(0, KC, 384), A_["w_rwkv"][0]).then_inc(sem("slot0"), 16)
            for h in (2, 3):
                j = 1 + h % 2
                sp.wait_ge(sem(f"slot{j}_free"), 1)
                sp.dma_start(piece(j, KC, 512), A_["w_gla"][h]).then_inc(sem(f"slot{j}"), 16)
            with sp.Fori(1, KC // 2) as i:
                for odd, j, first in ((0, 0, 1), (1, 3, 0)):
                    sp.wait_ge(sem(f"slot{j}_free"), first + i)
                    sp.dma_start(piece(j, KC, 384), A_["w_rwkv"][ds(2 * i + odd, 1)].rearrange("a p k n -> (a p) k n")
                                 ).then_inc(sem(f"slot{j}"), 16)
            with sp.Fori(0, 3) as i:
                for odd in range(2):
                    j = 1 + odd
                    sp.wait_ge(sem(f"slot{j}_free"), 2 + i)
                    sp.dma_start(piece(j, KC, 512), A_["w_mid"][ds(2 * i + odd, 1)].rearrange("a p k n -> (a p) k n")
                                 ).then_inc(sem(f"slot{j}"), 16)
            sp.wait_ge(sem("state_product"), NCHUNK - 1)
            sp.dma_start(piece(0, KC, 512), A_["w_mid"][6]).then_inc(sem("slot0"), 16)
            after(sp, "y_stored", NCHUNK)
            sp.dma_start(piece(3, KC, 512), A_["w_mid"][7]).then_inc(sem("slot3"), 16)
            FREE = {0: 8, 1: 5, 2: 5, 3: 7, 4: 0, 5: 0}

            def first_load(j):
                if FREE[j]:
                    sp.wait_ge(sem(f"slot{j}_free"), FREE[j])
                if j < 4:
                    src = A_["w_gu"][0, 256 * j:256 * j + 256, :].rearrange("(k p) n -> p k n", p=P)
                    sp.dma_start(piece(j, 2, 2048), src).then_inc(sem(f"slot{j}"), 16)
                else:
                    src = A_["w_dn"][0, 512 * (j - 4):512 * (j - 4) + 512, :].rearrange("(k p) n -> p k n", p=P)
                    sp.dma_start(piece(j, 4, 1024), src).then_inc(sem(f"slot{j}"), 16)

            for j in (4, 5, 1, 2):
                first_load(j)
            with sp.Fori(1, 3) as i:
                for odd, j, first in ((0, 0, 5), (1, 3, 4)):
                    sp.wait_ge(sem(f"slot{j}_free"), first + i)
                    sp.dma_start(piece(j, KC, 512), A_["w_mid"][ds(6 + 2 * i + odd, 1)].rearrange("a p k n -> (a p) k n")
                                 ).then_inc(sem(f"slot{j}"), 16)
            for j in (0, 3):
                first_load(j)
            sp.wait_ge(sem("items_ready"), 1)
            n_items = sp.value_load(nitems.bitcast(i32)[0:1, 0:1], min_val=NE, max_val=ITEMS)
            with sp.Fori(1, n_items) as w:
                e = sp.value_load(item_ei.bitcast(i32)[0:1, ds(w, 1)], min_val=0, max_val=NE - 1)
                for j in range(RING):
                    sp.wait_ge(sem(f"slot{j}_free"), w + FREE[j])
                    if j < 4:
                        src = A_["w_gu"][ds(e, 1), 256 * j:256 * j + 256, :].rearrange("a (k p) n -> (a p) k n", p=P)
                        sp.dma_start(piece(j, 2, 2048), src).then_inc(sem(f"slot{j}"), 16)
                    else:
                        src = A_["w_dn"][ds(e, 1), 512 * (j - 4):512 * (j - 4) + 512, :].rearrange(
                            "a (k p) n -> (a p) k n", p=P)
                        sp.dma_start(piece(j, 4, 1024), src).then_inc(sem(f"slot{j}"), 16)
            for blk in range(2):
                sp.wait_ge(sem("final_ready"), blk + 1)
                sp.dma_start(A_["out"][P * blk:P * blk + P, :], fin[:, blk, :]).then_inc(sem("stored"), 16)
            sp.wait_ge(sem("stored"), 32)

        @block.tensor
        def _(pe):
            mm, tr = nc.tensor.matmul, nc.tensor.transpose
            credit(pe, "act_turned")

            def project(dst, lhs, rhs):
                for k in range(KC):
                    last = mm(dst, lhs(k), rhs(k), start=(k == 0), stop=(k == KC - 1))
                return last

            pe.wait_ge(sem("params_loaded"), 32)
            pe.wait_ge(sem("h_squared"), 1)
            project(bank(0, T), lambda k: ones, lambda k: rv_sq[:, k, :]).then_inc(sem("product"), 1)
            pe.wait_ge(sem("slot0"), 16)
            small = piece(0, KC, 304)
            for k in range(KC):
                pe.wait_ge(sem("u_ready"), k + 1)
                last = mm(bank(1, T), small[:, k, 0:128], uT[:, k, :], start=(k == 0), stop=(k == KC - 1))
            last.then_inc(sem("product"), 1)
            project(bank(2, T), lambda k: small[:, k, 128:256], lambda k: uT[:, k, :]).then_inc(sem("product"), 1)
            project(bank(3, T)[0:48, :], lambda k: small[:, k, 256:304], lambda k: uT[:, k, :]).then_inc(sem("slot0_free"), 1)
            pe.wait_ge(sem("lora_loaded"), 32)
            pe.wait_ge(sem("wa_ready"), 1)
            for m in range(KC):
                b = 4 + 2 * (m % 2)
                if m >= 2:
                    pe.wait_ge(sem("lora_evacuated"), 2 * (m - 1))
                mm(bank(b, T), w_wa2[0:64, P * m:P * m + P], waT[0:64, :], start=True, stop=True)
                mm(bank(b + 1, T), w_wa2[64:128, P * m:P * m + P], waT[64:128, :], start=True, stop=True
                   ).then_inc(sem("product"), 1)
            pe.wait_ge(sem("ga_ready"), 1)
            pe.wait_ge(sem("small_evacuated"), 3)
            for h in range(GH):
                mm(bank(h, T), w_gla_a2[GA, P * h:P * h + P], gaT[GA, :], start=True, stop=True
                   ).then_inc(sem("product"), 1)
            pe.wait_ge(sem("gate_read"), GH)
            pe.wait_ge(sem("gate_min_read"), GH)
            pe.wait_ge(sem("lora_evacuated"), 2 * KC)
            with pe.Fori(0, 2) as i:
                for odd in range(2):
                    w = piece(1 + odd, KC, 512)
                    pe.wait_ge(sem(f"slot{1 + odd}"), 16 * i + 16)
                    unit_before_last(pe, "gla_v_evacuated", 2 * i + odd)
                    unit_before_last(pe, "gla_qk_evacuated", 2 * i + odd)
                    for b in range(4):
                        last = project(bank(4 * odd + b, T), lambda k: w[:, k, P * b:P * b + P], lambda k: uT[:, k, :])
                        last.then_inc(sem("gla_projected" if b < 3 else f"slot{1 + odd}_free"), 1)
            pe.wait_ge(sem("gla_v_evacuated"), GH + 2)
            pe.wait_ge(sem("gla_qk_evacuated"), GH + 2)
            with pe.Fori(0, KC // 2) as i:
                for odd, j in ((0, 0), (1, 3)):
                    w = piece(j, KC, 384)
                    pe.wait_ge(sem(f"slot{j}"), 16 * i + (32 if j == 0 else 16))
                    unit_before_last(pe, "rkv_evacuated", 2 * i + odd)
                    for b in range(3):
                        last = project(bank(4 * odd + b, T), lambda k: w[:, k, P * b:P * b + P], lambda k: uT[:, k, :])
                        last.then_inc(sem("rkv_projected" if b < 2 else f"slot{j}_free"), 1)
                    pe.wait_ge(sem("key_squared"), 2 * i + odd + 1)
                    mm(bank(4 * odd + 3, T), half_ones, key_sq[odd], start=True, stop=True
                       ).then_inc(sem("key_sumsq"), 1)
            pe.wait_ge(sem("rkv_evacuated"), KC + 2)

            halves = (slice(0, 64), slice(64, 128))
            pairs = [(m, h) for m in range(KC) for h in halves]
            tiles = [(m, slice(TILE * q, TILE * q + TILE)) for m in range(KC) for q in range(P // TILE)]

            now = slice(N_META, T)
            real = slice(CHUNK, TP)

            def late_half(n, j, q, h):
                w = piece(j, KC, 512)
                u = h // 2
                if h == 0:
                    pe.wait_ge(sem(f"slot{j}"), 16 * q + 48)
                    apart(pe, "pe_passed")
                for k in range(4 * (h % 2), 4 * (h % 2) + 4):
                    last = mm(bank(0, 4, SEQ)[:, u, :], w[:, k, P * u:P * u + P], uT[:, k, now],
                              start=(k == 0), stop=(k == KC - 1))
                if h == 3:
                    last.then_inc(sem("late_projected"), 1)
                if h == 7:
                    last.then_inc(sem(f"slot{j}_free"), 1)

            def fill(u):
                late_half(NCHUNK, 2, 2, 2 * u)
                late_half(NCHUNK, 2, 2, 2 * u + 1)

            def chunk_products(n, sn, c, sc, piece_at=None):
                prep, turn = n is not None, c is not None

                def since(name, k):
                    if not (isinstance(k, int) and k == 0):
                        pe.wait_ge(sem(name), k)

                def level(l, second):
                    if second:
                        pe.wait_ge(sem("prod_ready"), joins(n) + l)
                    else:
                        pe.wait_ge(sem("inv_ready"), inverses(n) + l)
                    apart(pe, "pe_passed")
                    for m, q in tiles:
                        if second:
                            last = mm(bank(5, KC, TILE)[q, m, :], prod[q, m, :], tileT[q, m, :], start=True, stop=True)
                        else:
                            last = mm(bank(4, KC, TILE)[q, m, :], low_at[q, l - 1, m, :], tile[q, m, :], start=True, stop=True)
                    last.then_inc(sem("step_product" if second else "level_product"), 1)

                if turn:
                    pe.wait_ge(sem("turned_ready"), c + 1)
                    pe.wait_ge(sem("mask_k_done"), c + 1)
                    pe.wait_ge(sem("state_ready"), c + 1)
                    after(pe, "y_stored", c)
                    apart(pe, "pe_passed")
                    for m, h in pairs:
                        mm(bank(6, KC, CHUNK)[h, m, :], c_ar[sc][h, m, 0:CHUNK], state[h, m, :], start=True, stop=False)
                        last = mm(bank(6, KC, CHUNK)[h, m, :], c_mk[sc][h, m, 0:CHUNK], t_v[sc][h, m, :], start=False, stop=True)
                    last.then_inc(sem("rhs_product"), 1)
                if not prep:
                    pe.wait_ge(sem("g_state_ready"), NCHUNK)
                    fill(0)
                    pe.wait_ge(sem("g_squared"), 1)
                    pe.wait_ge(sem("g_out_stored"), NCHUNK)
                    for h in range(GH):
                        for w in range(2):
                            last = mm(bank(2, GH, SEQ)[:, h, :], ones, sq[:, 2 * h + w, :], start=(w == 0), stop=(w == 1))
                    last.then_inc(sem("product"), 1)
                if prep:
                    pe.wait_ge(sem("staged_dve"), n + 1)
                    pe.wait_ge(sem("staged_act"), n + 1)
                    since("g_state_ready", n)
                    apart(pe, "pe_passed")
                    for m, h in pairs:
                        last = mm(bank(0, KC, 2 * CHUNK)[h, m, :], c_b[h, m, :], c_ar[sn][h, m, :], start=True, stop=True)
                    last.then_inc(sem("scores_b"), 1)
                    since("tg_k_ready", n)
                    since("g_out_stored", n)
                    apart(pe, "pe_passed")
                    for m, h in pairs:
                        last = mm(bank(2, KC, 2 * CHUNK)[h, m, :], c_k[h, m, :], c_ar[sn][h, m, :], start=True, stop=True)
                    last.then_inc(sem("scores_k"), 1)
                if turn:
                    pe.wait_ge(sem("inverse_ready"), c + 1)
                    pe.wait_ge(sem("rhs_ready"), c + 1)
                    apart(pe, "pe_passed")
                    for m, h in pairs:
                        last = mm(bank(7, KC, CHUNK)[h, m, :], invT[sc][h, m, :], c_r[h, m, :], start=True, stop=True)
                    last.then_inc(sem("sa_product"), 1)
                if not prep:
                    fill(1)
                if prep:
                    pe.wait_ge(sem("staged_pool"), n + 1)
                    pe.wait_ge(sem("mask_b_done"), n + 1)
                    apart(pe, "pe_passed")
                    for u in range(KC):
                        last = tr(bank(0, KC, P)[0:64, u, :], g_v[:, u, :], ident)
                    last.then_inc(sem("g_v_turned"), 1)
                    pe.wait_ge(sem("level_ready"), n + 1)
                    since("prod_ready", joins(n))
                    since("inverse_ready", n)
                    level(1, False)
                if turn:
                    pe.wait_ge(sem("sa_ready"), c + 1)
                    apart(pe, "pe_passed")
                    for m, h in pairs:
                        mm(bank(6, KC, CHUNK)[h, m, :], state[h, m, :], c_ar[sc][h, m, CHUNK:], start=True, stop=False)
                        mm(bank(6, KC, CHUNK)[h, m, :], c_sa[h, m, :], c_mb[sc][h, m, CHUNK:], start=False, stop=False)
                        last = mm(bank(6, KC, CHUNK)[h, m, :], t_v[sc][h, m, :], c_mk[sc][h, m, CHUNK:], start=False, stop=True)
                    last.then_inc(sem("y_product"), 1)
                if not prep:
                    fill(2)
                    fill(3)
                if prep:
                    level(1, True)
                if turn and prep:
                    for m, h in pairs:
                        mm(bank(7, KC, CHUNK)[h, m, :], t_b[sc][h, m, :], c_sa[h, m, :], start=True, stop=False)
                        last = mm(bank(7, KC, CHUNK)[h, m, :], t_k[sc][h, m, :], t_v[sc][h, m, :], start=False, stop=True)
                    last.then_inc(sem("state_product"), 1)
                if prep:
                    pe.wait_ge(sem("mask_k_done"), n + 1)
                    apart(pe, "pe_passed")
                    for h in range(GH):
                        last = tr(bank(2, GH, P)[0:64, h, :], g_k[:, h, :], ident)
                    last.then_inc(sem("g_k_turned"), 1)
                    for h in range(GH):
                        last = mm(bank(3, GH, CHUNK)[0:64, h, :], g_k[:, h, :], g_q[:, h, :], start=True, stop=True)
                    last.then_inc(sem("g_scores"), 1)
                    pe.wait_ge(sem("tg_v_ready"), n + 1)
                    late_half(n, *piece_at, 0)
                    level(2, False)
                    late_half(n, *piece_at, 1)
                    level(2, True)
                    late_half(n, *piece_at, 2)
                    level(3, False)
                    late_half(n, *piece_at, 3)
                    level(3, True)
                    late_half(n, *piece_at, 4)
                    pe.wait_ge(sem("g_a_ready"), n + 1)
                    since("g_state_ready", n)
                    apart(pe, "pe_passed")
                    for u in range(KC):
                        mm(bank(3, KC, CHUNK)[:, u, :], tg_v[0:64, P * u:P * u + P], g_a[0:64, u // 2, :],
                           start=True, stop=False)
                        last = mm(bank(3, KC, CHUNK)[:, u, :], g_state[:, u // 2, P * (u % 2):P * (u % 2) + P],
                                  g_q[:, u // 2, :], start=False, stop=True)
                    last.then_inc(sem("g_out"), 1)
                    if isinstance(n, int):
                        for h in (5, 6, 7):
                            late_half(n, *piece_at, h)
                    else:
                        level(4, False)
                        late_half(n, *piece_at, 5)
                        level(4, True)
                        late_half(n, *piece_at, 6)
                        even, odds = (0, 2), (1, 3)
                        pe.wait_ge(sem("inv_ready"), inverses(n) + LEVELS)
                        apart(pe, "pe_passed")
                        for m in range(KC):
                            for q in even:
                                a, b = slice(TILE * q, TILE * q + TILE), slice(TILE * q + TILE, TILE * q + 2 * TILE)
                                last = mm(bank(4, KC, TILE)[b, m, :], c_mb[sn][a, m, TILE:CHUNK], tile[a, m, :], start=True, stop=True)
                        last.then_inc(sem("level_product"), 1)
                        late_half(n, *piece_at, 7)
                        pe.wait_ge(sem("prod_ready"), joins(n) + LEVELS)
                        apart(pe, "pe_passed")
                        for m in range(KC):
                            for q in even:
                                a, b = slice(TILE * q, TILE * q + TILE), slice(TILE * q + TILE, TILE * q + 2 * TILE)
                                last = mm(bank(5, KC, TILE)[a, m, :], prod[b, m, :], tileT[b, m, :], start=True, stop=True)
                        last.then_inc(sem("step_product"), 1)

                    pe.wait_ge(sem("late_evacuated"), 2 * n + 3)
                    pe.wait_ge(sem("tg_k_ready"), n + 1)
                    apart(pe, "pe_passed")
                    for h in range(GH):
                        last = mm(bank(0, GH, GDV)[:, h, :], tg_k[0:64, P * h:P * h + P],
                                  tg_v[0:64, GDV * h:GDV * h + GDV], start=True, stop=True)
                    last.then_inc(sem("g_increment"), 1)

            chunk_products(0, 0, None, None, (1, 0))
            with pe.Fori(0, NCHUNK // 2) as i:
                for odd in range(2):
                    chunk_products(2 * i + odd + 1, 1 - odd, 2 * i + odd, odd, (2 - odd, i + odd))
            chunk_products(None, None, NCHUNK - 1, 0)

            def by_head(src, name):
                for m in range(KC):
                    last = mm(bank(4, KC, SEQ)[:, m, :], half_ones, src[:, m, :], start=True, stop=True)
                last.then_inc(sem("product"), 1)

            def out_unit(odd, u, b0, src):
                w = piece(3 * odd, KC, 512)
                return project(bank(b0, 4, SEQ)[:, u, :], lambda k: w[:, k, P * u:P * u + P], lambda k: src[:, k, real])

            after(pe, "y_stored", NCHUNK)
            by_head(ra[:, :, real], "y_sum")
            pe.wait_ge(sem("g_branch"), 1)
            pe.wait_ge(sem("slot0"), 16 * 6)
            out_unit(0, 0, 2, gv)
            out_unit(0, 1, 2, gv)
            pe.wait_ge(sem("y_centred"), 1)
            pe.wait_ge(sem("y_squared"), 1)
            by_head(sq, "y_sumsq")
            out_unit(0, 2, 2, gv)
            out_unit(0, 3, 2, gv).then_inc(sem("slot0_free"), 1)
            pe.wait_ge(sem("slot3"), 16 * 5)
            after(pe, "late_evacuated", 12)
            out_unit(1, 0, 0, gv)
            pe.wait_ge(sem("y_std"), 1)
            pe.wait_ge(sem("bonus_in"), 1)
            by_head(rr[:, :, real], "bonus_sum")
            out_unit(1, 1, 0, gv)
            pe.wait_ge(sem("gate2_loaded"), 32)
            pe.wait_ge(sem("bonus_done"), 1)
            for m in range(KC):
                mm(bank(4, KC, SEQ)[:, m, :], w_gate2[:, 0, P * m:P * m + P], sg[:, 0, now], start=True, stop=False)
                last = mm(bank(4, KC, SEQ)[:, m, :], w_gate2[0:32, 1, P * m:P * m + P], sg[0:32, 1, now],
                          start=False, stop=True)
            last.then_inc(sem("product"), 1)
            out_unit(1, 2, 0, gv)
            out_unit(1, 3, 0, gv).then_inc(sem("slot3_free"), 1)
            def route(half):
                ks = range(4 * half, 4 * half + 4)
                pe.wait_ge(sem("h2_ready"), half + 1)
                for blk in range(2):
                    for k in ks:
                        logits_ = mm(bank(4 + blk, NE), h2T[:, k, P * blk:P * blk + P], w_r[:, k, :],
                                     start=(k == 0), stop=(k == KC - 1))
                if half:
                    logits_.then_inc(sem("product"), 1)
                pe.wait_ge(sem("h2_squared"), half + 1)
                for blk in range(2):
                    for k in ks:
                        squares = mm(bank(6 + blk, 1), rv[:, k, CHUNK + P * blk:CHUNK + P * blk + P], ones[:, 0:1],
                                     start=(k == 0), stop=(k == KC - 1))
                if half:
                    squares.then_inc(sem("product"), 1)

            for n, (src, ready) in ((1, (ra, "r_branch")), (2, (rr, "mixed"))):
                pe.wait_ge(sem(ready), 1)
                for odd, j, first in ((0, 0, 6), (1, 3, 5)):
                    pe.wait_ge(sem(f"slot{j}"), 16 * (first + n))
                    for u in range(4):
                        last = out_unit(odd, u, (0, 4, 0)[n] + 2 * odd, src)
                        if (n, odd, u) == (2, 1, 1):
                            pe.wait_ge(sem("w_r_scaled"), 1)
                            route(0)
                    last.then_inc(sem(f"slot{j}_free"), 1)
            route(1)
            for blk in range(2):
                for k in range(KC):
                    last = tr(bank(2 * blk, KC, P)[:, k, :], h2T[:, k, P * blk:P * blk + P], ident)
                last.then_inc(sem("product"), 1)
            pe.wait_ge(sem("chosen_ready"), 1)
            mm(bank(4, 3, NE)[:, 0, :], before, chosen[:, 0, :], start=True, stop=True)
            mm(bank(4, 3, NE)[:, 1, :], ones, chosen[:, 0, :], start=True, stop=False)
            mm(bank(4, 3, NE)[:, 1, :], before, chosen[:, 1, :], start=False, stop=True)
            mm(bank(4, 3, NE)[:, 2, :], ones, chosen[:, 0, :], start=True, stop=False)
            mm(bank(4, 3, NE)[:, 2, :], ones, chosen[:, 1, :], start=False, stop=True).then_inc(sem("product"), 1)

            def gather(n):
                pe.wait_ge(sem("gather_ready"), n)
                for blk in range(2):
                    for half in range(2):
                        last = mm(bank(2, 512)[64 * half:64 * half + 64, :], gat[:, blk, :],
                                  u2[:, blk, 512 * half:512 * half + 512], start=(blk == 0), stop=(blk == 1))
                last.then_inc(sem("gathered"), 1)

            def turn_x(n):
                pe.wait_ge(sem("xg_ready"), n)
                for q in range(4):
                    last = tr(bank(2, 4, P)[:, q, :], xg[:, P * q:P * q + P], ident)
                last.then_inc(sem("x_turned"), 1)

            def scatter():
                for blk in range(2):
                    for half in range(2):
                        h = slice(64 * half, 64 * half + 64)
                        last = mm(bank(4 + 2 * blk + half, 512), scatT[h, blk, :], ye[h, :], start=True, stop=True)
                    last.then_inc(sem("scattered"), 1)

            def down(w, part):
                pe.wait_ge(sem(f"slot{4 + part}"), 16 * w + 16)
                wk = piece(4 + part, 4, 1024)
                for k in range(4):
                    for half in range(2):
                        last = mm(bank(0, 512)[64 * half:64 * half + 64, :], actT[:, k, part, :],
                                  wk[:, k, 512 * half:512 * half + 512], start=False, stop=(part == 1 and k == 3))
                last.then_inc(sem(f"slot{4 + part}_free"), 1)

            pe.wait_ge(sem("u2_ready"), 1)
            pe.wait_ge(sem("u2_ready_dve"), 1)
            pe.wait_ge(sem("h2_kept"), 2)
            gather(1)
            pe.wait_ge(sem("extra_items"), 1)
            mm(bank(0, 2, P)[:, 0, :], bc_e, ident, start=True, stop=True)
            mm(bank(0, 2, P)[:, 1, :], bc_b, ident, start=True, stop=True).then_inc(sem("product"), 1)
            turn_x(1)
            pe.wait_ge(sem("moe_loaded"), 48)
            pe.wait_ge(sem("loop_buffers"), 1)
            n_items = pe.value_load(nitems.bitcast(i32)[0:1, 0:1], min_val=NE, max_val=ITEMS)
            with pe.Fori(0, n_items) as w:
                pe.wait_ge(sem("x_ready"), w + 1)
                after(pe, "act_ready", w)
                for k in range(KC):
                    j, first = k // 2, (8, 5, 5, 7)[k // 2]
                    if k % 2 == 0:
                        pe.wait_ge(sem(f"slot{j}"), 16 * w + 16 * (first + 1))
                    wk = piece(j, 2, 2048)
                    for b in (1, 0):
                        if k == b == 0:
                            after(pe, "ye_ready", w)
                        for half in range(2):
                            last = mm(bank(b, 512)[64 * half:64 * half + 64, :], xT[:, k % 4, k // 4, :],
                                      wk[:, k % 2, FE * b + 512 * half:FE * b + 512 * half + 512],
                                      start=(k == 0), stop=(k == KC - 1))
                    if k % 2:
                        last.then_inc(sem(f"slot{j}_free"), 1)
                    if k == 1:
                        pe.wait_ge(sem("select_ready"), w + 1)
                        for b in range(2):
                            for half in range(2):
                                mm(bank(b, 512)[64 * half:64 * half + 64, :], sel,
                                   b_gu[:, FE * b + 512 * half:FE * b + 512 * half + 512], start=False, stop=False)
                after(pe, "scatT_ready", w)
                after(pe, "acc_added", w)
                scatter()
                after(pe, "act_ready", w + 1)
                for q in range(4):
                    last = tr(bank(3, 4, P)[:, q, :], h_up[:, P * q:P * q + P], ident)
                last.then_inc(sem("act_turned"), 1)
                gather(w + 2)
                pe.wait_ge(sem("actT_ready"), w + 1)
                for half in range(2):
                    last = mm(bank(0, 512)[64 * half:64 * half + 64, :], sel, b_dn[:, 512 * half:512 * half + 512],
                              start=True, stop=False)
                last.then_inc(sem("row_used"), 1)
                down(w, 0)
                turn_x(w + 2)
                after(pe, "acc_added", w + 1)
                pe.wait_ge(sem("scat_ready"), w + 1)
                for blk in range(2):
                    last = tr(bank(4, 2, P)[:, blk, :], scat[:, blk, :], ident)
                last.then_inc(sem("scat_turned"), 1)
                down(w, 1)
            after(pe, "ye_ready", n_items)
            after(pe, "scatT_ready", n_items)
            after(pe, "acc_added", n_items)
            scatter()

        @block.scalar
        def _(act):
            own = Own(act, "act_own")
            f = nc.scalar.activation
            credit(act, "gla_v_evacuated", "gla_v_evacuated", "late_evacuated", "y_stored", "gate_sigmoid", "ye_ready", "scatT_ready")
            act.wait_ge(sem("h_loaded"), 16)
            f(rv_sq, hT, ACT.Square).then_inc(sem("h_squared"), 1)
            act.wait_ge(sem("dve_eps"), 1)
            f(eps[:, 3:4], eps[:, 0:1], ACT.Sqrt)
            act.wait_ge(sem("product"), product("h_sumsq", 1))
            f(rs1, bank(0, T), ACT.Sqrt, scale=1.0 / D, bias=eps[:, 0:1]).then_inc(sem("h_std"), 1)
            act.wait_ge(sem("one_minus"), 1)
            smalls = ((waT, 128, "mu_wa", 0), (sg[:, 0, :], 128, "mu_g", 0), (sg[:, 1, :], 32, "mu_g", 1))
            for n, (dst, rows, mu, m) in enumerate(smalls):
                if n < 2:
                    act.wait_ge(sem("product"), product("small_projected", n + 1))
                else:
                    act.wait_ge(sem("slot0_free"), 1)
                f(dst[0:rows, :], bank(1 + n, T)[0:rows, :], ACT.Copy, scale=omcol(mu, m, rows)).then_inc(sem("small_part"), 1)
                if n == 0:
                    act.wait_ge(sem("small_evacuated"), 1)
                    f(waT[0:64, :], waT[0:64, :], ACT.Tanh).then_inc(sem("wa_ready"), 1)
            f(gaT[GA, :], bank(3, T)[GA, :], ACT.Copy).then_inc(sem("ga_ready"), 1)
            act.wait_ge(sem("small_evacuated"), 3)
            own.done(f(sg[:, 0, :], sg[:, 0, :], ACT.Sigmoid))
            own.done(f(sg[0:32, 1, :], sg[0:32, 1, :], ACT.Sigmoid))
            act.wait_ge(sem("pads_cleared"), 1)
            for m in range(KC):
                act.wait_ge(sem("product"), product("lora_projected", m + 1))
                b = 4 + 2 * (m % 2)
                f(ra[:, m, PAD:], bank(b, T), ACT.Sigmoid, bias=pcol("b_decay", m)).then_inc(sem("lora_evacuated"), 1)
                f(rb[:, m, PAD:], bank(b + 1, T), ACT.Sigmoid, bias=pcol("b_a", m)).then_inc(sem("lora_evacuated"), 1)
            for h in range(GH):
                act.wait_ge(sem("product"), product("gate_projected", h + 1))
                f(g_abs[:, h, :], bank(h, T), ACT.Abs, bias=pcol("b_gla_a", h)).then_inc(sem("gate_read"), 1)
            act.wait_ge(sem("gate_read"), GH)
            own.link(f(g_abs, g_abs, ACT.Exp, scale=-1.0))
            f(g_abs, g_abs, ACT.Ln, bias=eps[:, 2:3]).then_inc(sem("gate_log"), 1)
            act.wait_ge(sem("g_log_decay"), 1)
            f(gk, gq, ACT.Exp, scale=-1.0 / GATE_NORM).then_inc(sem("g_decay"), 1)
            act.wait_ge(sem("g_decay"), 1)
            f(gq, gq, ACT.Exp, scale=1.0 / GATE_NORM).then_inc(sem("g_decay"), 1)
            f(coefg, coefg, ACT.Exp, scale=1.0 / GATE_NORM).then_inc(sem("g_decay"), 1)
            act.wait_ge(sem("r_log_decay"), 1)
            f(rr, rk, ACT.Exp, scale=-DECAY_SCALE).then_inc(sem("r_decay"), 1)
            act.wait_ge(sem("r_decay"), 1)
            f(rk, rk, ACT.Exp, scale=DECAY_SCALE).then_inc(sem("r_decay"), 1)
            f(ra, ra, ACT.Exp, scale=-DECAY_SCALE).then_inc(sem("r_decay"), 1)
            f(coefr, coefr, ACT.Exp, scale=-DECAY_SCALE).then_inc(sem("r_decay"), 1)
            with act.Fori(0, 2) as i:
                for odd in range(2):
                    act.wait_ge(sem(f"slot{1 + odd}_free"), i + 1)
                    apart(act, "act_passed")
                    for u in range(2):
                        ins = f(gv[:, ds(4 * i + 2 * odd + u, 1), PAD:].rearrange("p a t -> p (a t)"),
                                bank(4 * odd + 2 + u, T), ACT.Copy)
                    ins.then_inc(sem("gla_v_evacuated"), 1)
            act.wait_ge(sem("rv_free"), 1)
            with act.Fori(0, KC // 2) as i:
                for odd, j in ((0, 0), (1, 3)):
                    m = 2 * i + odd
                    rt, kt = rk_tmp[odd]
                    row = lambda x: x[:, ds(m, 1), PAD:].rearrange("p a t -> p (a t)")
                    act.wait_ge(sem("rkv_projected"), 4 * i + 2 * odd + 1)
                    unit_before_last(act, "rkv_evacuated", 2 * i + odd)
                    apart(act, "act_passed")
                    f(kt, bank(4 * odd, T), ACT.Copy, scale=om[:, ds(m + PARAMS["mu_k"] - MU, 1)]).then_inc(sem("rkv_part"), 1)
                    act.wait_ge(sem("rkv_projected"), 4 * i + 2 * odd + 2)
                    apart(act, "act_passed")
                    f(rt, bank(4 * odd + 1, T), ACT.Copy, scale=om[:, ds(m + PARAMS["mu_r"] - MU, 1)]).then_inc(sem("rkv_part"), 1)
                    act.wait_ge(sem("key_lerped"), 2 * i + odd + 1)
                    apart(act, "act_passed")
                    f(key_sq[odd], kt, ACT.Square, scale=par[:, ds(m + PARAMS["k_k"], 1)]).then_inc(sem("key_squared"), 1)
                    act.wait_ge(sem(f"slot{j}_free"), i + (2 if j == 0 else 1))
                    apart(act, "act_passed")
                    f(row(rv), bank(4 * odd + 2, T), ACT.Copy, scale=om[:, ds(m + PARAMS["mu_v"] - MU, 1)]
                      ).then_inc(sem("rkv_part"), 1)
                    act.wait_ge(sem("key_sumsq"), 2 * i + odd + 1)
                    f(key_rn[odd], bank(4 * odd + 3, T), ACT.Sqrt).then_inc(sem("key_norm"), 1)

            def chunk_copies(n, sn, c, sc, piece_at=None):
                prep, turn = n is not None, c is not None

                def copy(dst, src, needed, k, ready):
                    act.wait_ge(sem(needed), k)
                    apart(act, "act_passed")
                    f(dst, src, ACT.Copy).then_inc(sem(ready), 1)

                def keep_late(n, b):
                    f(late(n)[:, 8 * b:8 * b + 8, :], bank(b, 8, CHUNK), ACT.Copy).then_inc(sem("late_evacuated"), 1)

                if prep:
                    if not isinstance(n, int):
                        act.wait_ge(sem("turned_ready"), n)
                    cols = ds(CHUNK * n, CHUNK)
                    f(c_k, rk[:, :, cols], ACT.Copy)
                    f(c_v, rv[:, :, cols], ACT.Copy).then_inc(sem("staged_act"), 1)
                if turn:
                    copy(c_r, bank(6, KC, CHUNK), "rhs_product", c + 1, "rhs_ready")
                if not prep:
                    act.wait_ge(sem("g_state_ready"), NCHUNK)
                    f(sq, gv[:, :, real], ACT.Square).then_inc(sem("g_squared"), 1)
                if turn:
                    copy(c_sa, bank(7, KC, CHUNK), "sa_product", c + 1, "sa_ready")
                if not prep:
                    act.wait_ge(sem("product"), product("g_sumsq", 1))
                    f(g_std, bank(2, GH, SEQ), ACT.Sqrt, scale=1.0 / GDV, bias=eps[:, 0:1]).then_inc(sem("g_std"), 1)
                    act.wait_ge(sem("late_projected"), NCHUNK + 1)
                    keep_late(NCHUNK, 0)
                    act.wait_ge(sem("late_evacuated"), 5)
                    f(r_sig[:, 0:16, :], late(0), ACT.Sigmoid)
                    f(r_sig[:, 16:32, :], late(1), ACT.Sigmoid).then_inc(sem("r_sigmoid"), 1)
                if prep:
                    copy(tg_v[0:64, :], bank(0, GH * GDV)[0:64, :], "g_v_turned", n + 1, "tg_v_ready")
                    copy(prod, bank(4, KC, TILE), "level_product", joins(n) + 1, "prod_ready")
                if turn:
                    copy(ra[:, :, ds(CHUNK * c, CHUNK)], bank(6, KC, CHUNK), "y_product", c + 1, "y_stored")
                if prep:
                    copy(tg_k[0:64, :], bank(2, GH * GDK)[0:64, :], "g_k_turned", n + 1, "tg_k_ready")
                    copy(g_a[0:64, :, :], bank(3, GH, CHUNK)[0:64, :, :], "g_scores", n + 1, "g_scores_read")
                    copy(prod, bank(4, KC, TILE), "level_product", joins(n) + 2, "prod_ready")
                    copy(prod, bank(4, KC, TILE), "level_product", joins(n) + 3, "prod_ready")
                    act.wait_ge(sem("late_projected"), n + 1)
                    apart(act, "act_passed")
                    keep_late(n, 0)
                    copy(gv[:, :, cols], bank(3, KC, CHUNK), "g_out", n + 1, "g_out_stored")
                    if not isinstance(n, int):
                        copy(prod, bank(4, KC, TILE), "level_product", joins(n) + 4, "prod_ready")
                        act.wait_ge(sem("level_product"), joins(n) + LEVELS)
                        for q in (1, 3):
                            rows = slice(TILE * q, TILE * q + TILE)
                            ins = f(prod[rows, :, :], bank(4, KC, TILE)[rows, :, :], ACT.Copy)
                        ins.then_inc(sem("prod_ready"), 1)
                    j, q = piece_at
                    act.wait_ge(sem(f"slot{j}_free"), q + 3)
                    apart(act, "act_passed")
                    keep_late(n, 1)

            real = slice(CHUNK, TP)
            act.wait_ge(sem("factors_done"), 1)
            chunk_copies(0, 0, None, None, (1, 0))
            with act.Fori(0, NCHUNK // 2) as i:
                for odd in range(2):
                    chunk_copies(2 * i + odd + 1, 1 - odd, 2 * i + odd, odd, (2 - odd, i + odd))
            chunk_copies(None, None, NCHUNK - 1, 0)
            act.wait_ge(sem("slot2_free"), 5)
            f(late(NCHUNK)[:, 8:16, :], bank(1, 8, CHUNK), ACT.Copy).then_inc(sem("late_evacuated"), 1)

            act.wait_ge(sem("state_ready"), NCHUNK)
            act.dma_start(w_gate2[:, 0, :], A_["w_gate2"][0:128, :]).then_inc(sem("gate2_loaded"), 16)
            act.dma_start(w_gate2[0:32, 1, :], A_["w_gate2"][128:160, :]).then_inc(sem("gate2_loaded"), 16)
            act.wait_ge(sem("y_centred"), 1)
            f(sq, ra[:, :, real], ACT.Square).then_inc(sem("y_squared"), 1)
            act.wait_ge(sem("late_evacuated"), 13)
            f(late(2), late(2), ACT.Sigmoid)
            f(late(3), late(3), ACT.Sigmoid).then_inc(sem("gates_ready"), 1)
            act.wait_ge(sem("product"), product("y_sumsq", 1))
            f(rk[:, :, real], bank(4, KC, SEQ), ACT.Sqrt, scale=1.0 / HEAD, bias=eps[:, 1:2]).then_inc(sem("y_std"), 1)
            act.dma_start(hT[:, :, :], A_["hT"]).then_inc(sem("h_loaded"), 16)
            f(late(4), late(4), ACT.Sigmoid)
            f(late(5), late(5), ACT.Sigmoid).then_inc(sem("gates_ready"), 1)
            act.wait_ge(sem("y_normed"), 1)
            for m in range(KC):
                ins = f(ra[:, m, real], ra[:, m, real], ACT.Identity, scale=pcol("ln_x_g", m), bias=pcol("ln_x_b", m))
            ins.then_inc(sem("y_affine"), 1)
            act.wait_ge(sem("slot3_free"), 5)
            act.dma_start(w_r[:, :, :], A_["w_router"]).then_inc(sem("router_loaded"), 16)
            act.dma_start(b_r, A_["b_router"].broadcast_to((P, NE))).then_inc(sem("router_loaded"), 16)
            act.dma_start(at(o_mc, NMOE_CONST), A_["moe_consts"]).then_inc(sem("router_loaded"), 16)
            act.wait_ge(sem("slot2_free"), 5)
            act.dma_start(g_ffn, A_["norm_ffn_g"].broadcast_to((P, D))).then_inc(sem("g_ffn_loaded"), 16)
            act.wait_ge(sem("biases_cleared"), 1)
            act.dma_start(b_dn[0:NE, :], A_["b_dn"]).then_inc(sem("moe_loaded"), 16)
            act.dma_start(b_gu[0:NE, :], A_["b_gu"]).then_inc(sem("moe_loaded"), 16)
            for half in range(2):
                us = slice(4 * half, 4 * half + 4)
                act.wait_ge(sem("h2_ready"), half + 1)
                f(rv[:, us, real], h2T[:, us, :], ACT.Square).then_inc(sem("h2_squared"), 1)
            act.wait_ge(sem("product"), product("h2_sumsq", 1))
            f(rs2, bank(6, 2, 512)[:, :, 0:1].rearrange("p a b -> p (a b)"), ACT.Sqrt, scale=1.0 / D, bias=eps[:, 0:1]
              ).then_inc(sem("h2_std"), 1)
            act.wait_ge(sem("product"), product("h2_sumsq", 1))
            act.dma_start(g_fin[:, :], A_["norm_final_g"].broadcast_to((P, D))).then_inc(sem("moe_loaded"), 16)
            act.wait_ge(sem("h2_rstd"), 1)
            act.wait_ge(sem("product"), product("h2_turned", 1))
            f(u2[:, 0, :], bank(0, D), ACT.Copy, scale=rs2[:, 0:1]).then_inc(sem("u2_scaled"), 1)
            for blk in range(2):
                if blk:
                    act.wait_ge(sem("u2_ready_dve"), 1)
                f(acc[:, blk, :], bank(2 * blk, D), ACT.Copy).then_inc(sem("h2_kept"), 1)
            act.wait_ge(sem("top_ready"), 1)
            for blk in range(2):
                own.link(f(negmax[:, blk:blk + 1], top[:, blk, 0:1], ACT.Copy, scale=-1.0))
                ins = f(probs[:, blk, :], top[:, blk, 0:TOPK], ACT.Exp, bias=negmax[:, blk:blk + 1],
                        accum_out=psums[:, blk:blk + 1])
                ins.then_inc(sem("probs_ready"), 1)

            def keep_x(n):
                act.wait_ge(sem("gathered"), n)
                f(xg, bank(2, 512), ACT.Copy).then_inc(sem("xg_ready"), 1)
                act.wait_ge(sem("x_turned"), n)
                f(xT.rearrange("p a b c -> p (a b c)"), bank(2, 512), ACT.Copy).then_inc(sem("x_ready"), 1)

            keep_x(1)
            act.wait_ge(sem("items_ready"), 1)
            n_items = act.value_load(nitems.bitcast(i32)[0:1, 0:1], min_val=NE, max_val=ITEMS)
            with act.Fori(0, n_items) as w:
                act.wait_ge(sem("gate_clamped"), w + 1)
                f(h_sig, h_gate, ACT.Sigmoid, scale=ALPHA).then_inc(sem("gate_sigmoid"), 1)
                after(act, "act_turned", w + 1)
                f(actT.rearrange("p a b c -> p (a b c)"), bank(3, 512), ACT.Copy).then_inc(sem("actT_ready"), 1)
                keep_x(w + 2)
                act.wait_ge(sem("scat_turned"), w + 1)
                f(scatT.rearrange("p a b -> p (a b)"), bank(4, 2 * P), ACT.Copy).then_inc(sem("scatT_ready"), 1)
                act.wait_ge(sem("slot5_free"), w + 1)
                f(ye, bank(0, 512), ACT.Copy).then_inc(sem("ye_ready"), 1)
            for blk in range(2):
                act.wait_ge(sem("acc_whole"), blk + 1)
                own.link(f(fin[:, blk, :], acc[:, blk, :], ACT.Square, accum_out=fss[:, blk:blk + 1]))
                f(frs[:, blk:blk + 1], fss[:, blk:blk + 1], ACT.Sqrt, scale=1.0 / D, bias=eps[:, 0:1]).then_inc(sem("final_std"), 1)

        @block.vector
        def _(dve):
            v = nc.vector
            own = Own(dve, "dve_own")
            link, done = own.link, own.done
            credit(dve, "gla_qk_evacuated", "gla_qk_evacuated", "rkv_evacuated", "rkv_evacuated", "act_ready", "acc_added")
            done(v.memset(eps[:, 0:1], NORM_EPS))
            done(v.memset(eps[:, 1:2], RWKV_GN_EPS))
            own.wait()
            v.memset(eps[:, 2:3], 1.0).then_inc(sem("dve_eps"), 1)
            dve.wait_ge(sem("params_loaded"), 32)
            v.tensor_scalar(om, par[:, MU:], -1.0, 1.0, ALU.mult, ALU.add).then_inc(sem("one_minus"), 1)
            dve.wait_ge(sem("h_std"), 1)
            link(v.reciprocal(rs1, rs1))
            for k in range(KC):
                v.scalar_tensor_tensor(uT[:, k, :], hT[:, k, :], pcol("norm_mix_g", k), rs1, ALU.mult, ALU.mult
                                       ).then_inc(sem("u_ready"), 1)
            for z in (gq, gk, gv, rb, rv):
                done(v.memset(z[:, :, 0:PAD], 0.0))
            v.memset(ra[:, :, 0:PAD], 0.0).then_inc(sem("pads_cleared"), 1)
            smalls = ((waT, 128, "mu_wa", 0), (sg[:, 0, :], 128, "mu_g", 0), (sg[:, 1, :], 32, "mu_g", 1))
            for n, (dst, rows, mu, m) in enumerate(smalls):
                dve.wait_ge(sem("small_part"), n + 1)
                v.scalar_tensor_tensor(dst[0:rows, 1:], bank(1 + n, T)[0:rows, 0:T - 1], pcol(mu, m, rows),
                                       dst[0:rows, 1:], ALU.mult, ALU.add).then_inc(sem("small_evacuated"), 1)
            for h in range(GH):
                dve.wait_ge(sem("gate_read"), h + 1)
                v.tensor_scalar(g_min[:, h, :], bank(h, T), pcol("b_gla_a", h), 0.0, ALU.add, ALU.min
                                ).then_inc(sem("gate_min_read"), 1)
            dve.wait_ge(sem("gate_log"), 1)
            dve.wait_ge(sem("gate_min_read"), GH)
            own.wait()
            link(v.tensor_tensor(gq[:, :, PAD:], g_min, g_abs, ALU.subtract))
            for h in range(GH):
                done(v.tensor_tensor_scan(gk[:, h, :], scan_mask, gq[:, h, :], 0.0, ALU.mult, ALU.add))
            own.wait()

            def chunks_of(x, n):
                return x.rearrange("p n (c t) -> p (n c) t", t=CHUNK)

            def spread(x, n):
                return chunks_of(x, n)[:, :, CHUNK // 2 - 1:CHUNK // 2].broadcast_to((P, n * NCHUNK, CHUNK))

            def boundary(dst, x, n):
                by = x.rearrange("p n (c t) -> p n c t", t=CHUNK)
                link(v.tensor_tensor(dst.rearrange("p n (c o) -> p n c o", o=1), by[:, :, :, CHUNK - 1:CHUNK],
                                     by[:, :, :, CHUNK // 2 - 1:CHUNK // 2], ALU.subtract))
                link(v.tensor_tensor(dst[:, :, 0:NCHUNK - 1].rearrange("p n (c o) -> p n c o", o=1),
                                     dst[:, :, 0:NCHUNK - 1].rearrange("p n (c o) -> p n c o", o=1),
                                     by[:, :, 1:, CHUNK // 2 - 1:CHUNK // 2], ALU.add))

            boundary(coefg, gk, GH)
            v.tensor_tensor(chunks_of(gq, GH), chunks_of(gk, GH), spread(gk, GH), ALU.subtract).then_inc(sem("g_log_decay"), 1)
            dve.wait_ge(sem("lora_evacuated"), 2 * KC)
            for m in range(KC):
                done(v.tensor_tensor_scan(rr[:, m, :], scan_mask, ra[:, m, :], 0.0, ALU.mult, ALU.add))
            own.wait()
            boundary(coefr, rr, KC)
            link(v.tensor_tensor(chunks_of(rk, KC), chunks_of(rr, KC), spread(rr, KC), ALU.subtract))
            v.tensor_tensor(ra, rk, ra, ALU.subtract).then_inc(sem("r_log_decay"), 1)
            for m in range(KC):
                done(v.tensor_scalar(rv[:, m, PAD:], rb[:, m, PAD:], pcol("k_a", m), omcol("k_a", m), ALU.mult, ALU.add))
            own.wait()
            dve.wait_ge(sem("g_decay"), 3)
            done(v.memset(gq[:, :, 0:PAD], 0.0))
            done(v.memset(gk[:, :, 0:PAD], 0.0))
            own.wait()
            with dve.Fori(0, 2) as i:
                for odd in range(2):
                    dve.wait_ge(sem("gla_projected"), 6 * i + 3 * odd + 2)
                    h = 2 * i + odd
                    q = gq[:, ds(h, 1), PAD:].rearrange("p a t -> p (a t)")
                    k = gk[:, ds(h, 1), PAD:].rearrange("p a t -> p (a t)")
                    v.scalar_tensor_tensor(q, bank(4 * odd, T), GDK ** -0.5, q, ALU.mult, ALU.mult)
                    v.tensor_tensor(k, bank(4 * odd + 1, T), k, ALU.mult).then_inc(sem("gla_qk_evacuated"), 1)
            dve.wait_ge(sem("r_decay"), 4)
            link(v.tensor_tensor(rb, rb, rk, ALU.mult))
            link(v.tensor_tensor(rk, rv, rk, ALU.mult))
            done(v.memset(ra[:, :, 0:PAD], 0.0))
            done(v.memset(g_state, 0.0))
            done(v.memset(invT[0], 0.0))
            done(v.memset(invT[1], 0.0))
            v.memset(state, 0.0).then_inc(sem("state_ready"), 1)
            v.memset(rr[:, :, 0:PAD], 0.0).then_inc(sem("rv_free"), 1)
            dve.wait_ge(sem("rv_free"), 1)
            own.wait()
            with dve.Fori(0, KC // 2) as i:
                own.enter(i, 18)
                for odd in range(2):
                    m = 2 * i + odd
                    rt, kt = rk_tmp[odd]
                    row = lambda x: x[:, ds(m, 1), PAD:].rearrange("p a t -> p (a t)")
                    k_k = par[:, ds(m + PARAMS["k_k"], 1)]
                    dve.wait_ge(sem("rkv_part"), 6 * i + 3 * odd + 1)
                    v.scalar_tensor_tensor(kt[:, 1:], bank(4 * odd, T)[:, 0:T - 1], par[:, ds(m + PARAMS["mu_k"], 1)],
                                           kt[:, 1:], ALU.mult, ALU.add).then_inc(sem("key_lerped"), 1)
                    dve.wait_ge(sem("key_lerped"), 2 * i + odd + 1)
                    done(v.tensor_tensor(row(rk), row(rk), kt, ALU.mult))
                    done(v.scalar_tensor_tensor(row(rb), kt, k_k, row(rb), ALU.mult, ALU.mult))
                    done(v.scalar_tensor_tensor(row(ra), kt, k_k, row(ra), ALU.mult, ALU.mult))
                    dve.wait_ge(sem("rkv_part"), 6 * i + 3 * odd + 2)
                    link(v.scalar_tensor_tensor(rt[:, 1:], bank(4 * odd + 1, T)[:, 0:T - 1], par[:, ds(m + PARAMS["mu_r"], 1)],
                                                rt[:, 1:], ALU.mult, ALU.add))
                    done(v.tensor_tensor(row(rr), row(rr), rt, ALU.mult))
                    dve.wait_ge(sem("rkv_part"), 6 * i + 3 * odd + 3)
                    done(v.scalar_tensor_tensor(row(rv)[:, 1:], bank(4 * odd + 2, T)[:, 0:T - 1],
                                                par[:, ds(m + PARAMS["mu_v"], 1)], row(rv)[:, 1:], ALU.mult, ALU.add))
                    dve.wait_ge(sem("key_norm"), 2 * i + odd + 1)
                    rn = key_rn[odd]
                    link(v.tensor_scalar(rn, rn, 1e-12, None, ALU.max))
                    link(v.reciprocal(rn, rn))
                    done(v.tensor_tensor(row(rb), row(rb), rn, ALU.mult))
                    v.scalar_tensor_tensor(row(ra), row(ra), -1.0, rn, ALU.mult, ALU.mult).then_inc(sem("rkv_evacuated"), 1)
            own.leave(KC // 2)
            dve.wait_ge(sem("rkv_evacuated"), KC + 2)
            own.wait()
            dve.sem_inc(sem("factors_done"), 1)

            dve.wait_ge(sem("factors_done"), 1)
            mask = causal.rearrange("p (a b) -> p a b", a=1).broadcast_to((P, KC, 2 * CHUNK))

            def over_units(x):
                return x.broadcast_to((P, KC, TILE))

            def turn_over(dst, src):
                done(v.transpose(dst, src))
                done(v.transpose(crossed, src))
                own.wait()
                for q in range(4):
                    to, left = q ^ 1, TILE * (q % 2)
                    right = TILE - left
                    ins = v.tensor_copy(dst[TILE * to:TILE * to + TILE, :, left:left + TILE],
                                        crossed[TILE * q:TILE * q + TILE, :, right:right + TILE])
                    if q < 3:
                        done(ins)
                return ins

            def chunk_steps(n, sn, c, sc):
                prep, turn = n is not None, c is not None
                if prep:
                    cols = ds(CHUNK * n, CHUNK)
                    if not isinstance(n, int):
                        dve.wait_ge(sem("turned_ready"), n)
                    v.tensor_copy(c_ar[sn][:, :, 0:CHUNK], ra[:, :, cols])
                    v.tensor_copy(c_ar[sn][:, :, CHUNK:], rr[:, :, cols])
                    v.tensor_copy(c_b, rb[:, :, cols]).then_inc(sem("staged_dve"), 1)
                    dve.wait_ge(sem("scores_b"), n + 1)
                    v.tensor_tensor(c_mb[sn], bank(0, KC, 2 * CHUNK), mask, ALU.mult).then_inc(sem("mask_b_done"), 1)
                    dve.wait_ge(sem("mask_b_done"), n + 1)
                    link(v.tensor_scalar(low, c_mb[sn][:, :, 0:TILE], parity[:, 0:1], None, ALU.mult))
                    v.scalar_tensor_tensor(low, c_mb[sn][:, :, TILE:CHUNK], parity[:, 1:2], low, ALU.mult, ALU.add
                                           ).then_inc(sem("low_ready"), 1)
                    dve.wait_ge(sem("low_ready"), n + 1)
                    link(v.tensor_tensor(tileT, low, over_units(levels[:, 0:1, :]), ALU.mult))
                    link(v.tensor_tensor(tileT, tileT, over_units(tile_ident.rearrange("p (a b) -> p a b", a=1)), ALU.add))
                    v.transpose(tile.rearrange("p a b -> p (a b)"), tileT.rearrange("p a b -> p (a b)")
                                ).then_inc(sem("inv_ready"), 1)
                    dve.wait_ge(sem("scores_k"), n + 1)
                    v.tensor_tensor(c_mk[sn], bank(2, KC, 2 * CHUNK), mask, ALU.mult).then_inc(sem("mask_k_done"), 1)
                    done(turn_over(t_b[sn], c_b))
                    double(n, 1)
                    dve.wait_ge(sem("staged_act"), n + 1)
                    done(turn_over(t_k[sn], c_k))
                    double(n, 2)
                if turn and prep:
                    dve.wait_ge(sem("state_product"), c + 1)
                    link(v.tensor_tensor(state, bank(7, KC, CHUNK), state, ALU.add))
                    v.tensor_tensor(state, state, coefr[:, :, ds(c, 1)].broadcast_to((P, KC, CHUNK)), ALU.mult
                                    ).then_inc(sem("state_ready"), 1)
                if prep:
                    turn_over(t_v[sn], c_v).then_inc(sem("turned_ready"), 1)
                    double(n, 3)
                    short = isinstance(n, int)
                    if not short:
                        double(n, 4)
                    for q in range(4):
                        rows, half = slice(TILE * q, TILE * q + TILE), slice(TILE * (q % 2), TILE * (q % 2) + TILE)
                        ins = v.tensor_copy(invT[sn][rows, :, half], tileT[rows, :, :])
                        if q < 3 or not short:
                            done(ins)
                    if not short:
                        dve.wait_ge(sem("step_product"), joins(n) + LEVELS)
                        for q in (0, 2):
                            rows = slice(TILE * q, TILE * q + TILE)
                            ins = v.tensor_copy(invT[sn][rows, :, TILE:CHUNK], bank(5, KC, TILE)[rows, :, :])
                    ins.then_inc(sem("inverse_ready"), 1)
                    dve.wait_ge(sem("g_increment"), n + 1)
                    link(v.tensor_tensor(g_state, bank(0, GH, GDV), g_state, ALU.add))
                    v.tensor_tensor(g_state, g_state, coefg[:, :, ds(n, 1)].broadcast_to((P, GH, GDV)), ALU.mult
                                    ).then_inc(sem("g_state_ready"), 1)

            def double(n, l):
                dve.wait_ge(sem("step_product"), joins(n) + l)
                link(v.tensor_tensor(tileT, bank(5, KC, TILE), tileT, ALU.add))
                v.transpose(tile.rearrange("p a b -> p (a b)"), tileT.rearrange("p a b -> p (a b)")
                            ).then_inc(sem("inv_ready"), 1)

            chunk_steps(0, 0, None, None)
            with dve.Fori(0, NCHUNK // 2) as i:
                own.enter(i, 60)
                for odd in range(2):
                    chunk_steps(2 * i + odd + 1, 1 - odd, 2 * i + odd, odd)
            own.leave(NCHUNK // 2)

            real = slice(CHUNK, TP)
            dve.wait_ge(sem("staged_act"), NCHUNK)
            dve.wait_ge(sem("staged_dve"), NCHUNK)
            link(v.tensor_tensor(rr[:, :, real], rr[:, :, real], rk[:, :, real], ALU.mult))
            for m in range(KC):
                ins = v.tensor_scalar(rr[:, m, real], rr[:, m, real], pcol("r_k", m), None, ALU.mult)
                if m < KC - 1:
                    done(ins)
            ins.then_inc(sem("bonus_in"), 1)
            dve.wait_ge(sem("g_std"), 1)
            link(v.reciprocal(g_std, g_std))
            for u in range(KC):
                done(v.scalar_tensor_tensor(gv[:, u, real], gv[:, u, real], pcol("gla_norm_g", u % 2), g_std[:, u // 2, :],
                                            ALU.mult, ALU.mult))
            dve.wait_ge(sem("r_sigmoid"), 1)
            for n in range(2):
                done(v.tensor_tensor(late(n), late(n), r_sig[:, 16 * n:16 * n + 16, :], ALU.mult))
            own.wait()
            for n in range(2):
                out = in_rows(gv[:, 4 * n:4 * n + 4, real])
                ins = v.tensor_tensor(out, out, by_unit(n), ALU.mult)
                if n == 0:
                    done(ins)
            ins.then_inc(sem("g_branch"), 1)
            dve.wait_ge(sem("product"), product("y_sum", 1))
            v.scalar_tensor_tensor(ra[:, :, real], bank(4, KC, SEQ), -1.0 / HEAD, ra[:, :, real], ALU.mult, ALU.add
                                   ).then_inc(sem("y_centred"), 1)
            dve.wait_ge(sem("y_std"), 1)
            dve.wait_ge(sem("y_centred"), 1)
            link(v.reciprocal(rk[:, :, real], rk[:, :, real]))
            v.tensor_tensor(ra[:, :, real], ra[:, :, real], rk[:, :, real], ALU.mult).then_inc(sem("y_normed"), 1)
            dve.wait_ge(sem("product"), product("bonus_sum", 1))
            v.tensor_tensor(rv[:, :, real], bank(4, KC, SEQ), rv[:, :, real], ALU.mult).then_inc(sem("bonus_done"), 1)
            dve.wait_ge(sem("y_affine"), 1)
            dve.wait_ge(sem("bonus_done"), 1)
            link(v.tensor_tensor(ra[:, :, real], ra[:, :, real], rv[:, :, real], ALU.add))
            dve.wait_ge(sem("product"), product("out_gate", 1))
            v.tensor_tensor(ra[:, :, real], bank(4, KC, SEQ), ra[:, :, real], ALU.mult).then_inc(sem("r_branch"), 1)
            dve.wait_ge(sem("gates_ready"), 2)
            for odd, j, first in ((0, 0, 6), (1, 3, 5)):
                us = slice(4 * odd, 4 * odd + 4)
                dve.wait_ge(sem(f"slot{j}_free"), first)
                done(v.tensor_tensor(in_rows(rr[:, us, real]), in_rows(bank(2 - 2 * odd, 4, SEQ)), by_unit(2 + odd), ALU.mult))
            for odd, j, first in ((0, 0, 7), (1, 3, 6)):
                us = slice(4 * odd, 4 * odd + 4)
                dve.wait_ge(sem(f"slot{j}_free"), first)
                link(v.tensor_tensor(in_rows(rk[:, us, real]), in_rows(bank(4 + 2 * odd, 4, SEQ)), by_unit(4 + odd), ALU.mult))
                ins = v.tensor_tensor(rr[:, us, real], rr[:, us, real], rk[:, us, real], ALU.add)
                if odd == 0:
                    done(ins)
            ins.then_inc(sem("mixed"), 1)
            dve.wait_ge(sem("mixed"), 1)
            done(v.memset(b_dn, 0.0))
            v.memset(b_gu, 0.0).then_inc(sem("biases_cleared"), 1)
            dve.wait_ge(sem("router_loaded"), 48)
            g_cols = par[:, PARAMS["norm_ffn_g"]:PARAMS["norm_ffn_g"] + KC].rearrange("p (k n) -> p k n", n=1)
            v.tensor_tensor(w_r, w_r, g_cols.broadcast_to((P, KC, NE)), ALU.mult).then_inc(sem("w_r_scaled"), 1)
            dve.wait_ge(sem("h_loaded"), 32)
            for odd, j, first in ((0, 0, 8), (1, 3, 7)):
                us = slice(4 * odd, 4 * odd + 4)
                dve.wait_ge(sem(f"slot{j}_free"), first)
                v.tensor_tensor(h2T[:, us, :], bank(2 * odd, 4, SEQ), h2T[:, us, :], ALU.add).then_inc(sem("h2_ready"), 1)
            for x in (h_up, h_gate, scatT, ye, item_b[:, 0:NE]):
                done(v.memset(x, 0.0))
            done(v.tensor_copy(item_e[:, 0:NE], ids[:, 0:NE]))
            dve.wait_ge(sem("h2_std"), 1)
            v.reciprocal(rs2, rs2).then_inc(sem("h2_rstd"), 1)
            dve.wait_ge(sem("h2_rstd"), 1)
            dve.wait_ge(sem("product"), product("logits", 1))
            for blk in range(2):
                done(v.scalar_tensor_tensor(logits[:, blk, :], bank(4 + blk, NE), rs2[:, blk:blk + 1], b_r, ALU.mult, ALU.add))
            own.wait()
            for blk in range(2):
                done(v.max(top[:, blk, :], logits[:, blk, :]))
            own.wait()
            for blk in range(2):
                ins = v.max_index(top_i.bitcast(u32)[:, blk, :], top[:, blk, :], logits[:, blk, :])
                if blk == 0:
                    done(ins)
            ins.then_inc(sem("top_ready"), 1)
            dve.wait_ge(sem("top_ready"), 1)
            own.wait()
            link(v.tensor_copy(top_f, top_i.bitcast(u32)))
            for blk in range(2):
                for k in range(TOPK):
                    done(v.tensor_scalar(one_hot[:, blk, k, :], ids[:, 0:NE], top_f[:, blk, k:k + 1], None, ALU.is_equal))
            own.wait()
            link(v.tensor_tensor(weighted[:, :, 0:2, :], one_hot[:, :, 0:2, :], one_hot[:, :, 2:4, :], ALU.add))
            v.tensor_tensor(chosen.rearrange("p a (b e) -> p a b e", b=1), weighted[:, :, 0:1, :], weighted[:, :, 1:2, :],
                            ALU.add).then_inc(sem("chosen_ready"), 1)
            dve.wait_ge(sem("product"), product("h2_turned", 2))
            dve.wait_ge(sem("g_ffn_loaded"), 16)
            v.scalar_tensor_tensor(u2[:, 1, :], bank(2, D), rs2[:, 1:2], g_ffn, ALU.mult, ALU.mult).then_inc(sem("u2_ready_dve"), 1)
            dve.wait_ge(sem("chosen_ready"), 1)
            dve.wait_ge(sem("product"), product("counted", 1))
            link(v.scalar_tensor_tensor(pos, bank(4, 3, NE)[:, 0:2, :], 1.0, chosen, ALU.add, ALU.mult))
            done(v.tensor_scalar(pos, pos, -1.0, None, ALU.add))
            link(v.tensor_copy(count, bank(4, 3, NE)[:, 2, :]))
            for blk in range(2):
                ins = v.tensor_scalar(gat[:, blk, :], slot_ids[:, 0:SLOTS], pos[:, blk, 0:1], None, ALU.is_equal)
                if blk == 0:
                    done(ins)
            ins.then_inc(sem("gather_ready"), 1)
            link(v.tensor_scalar(extra, count, float(SLOTS), None, ALU.is_gt))
            for b in range(2, BLOCKS):
                link(v.tensor_scalar(cmp_e, count, float(SLOTS * b), None, ALU.is_gt))
                link(v.tensor_tensor(extra, extra, cmp_e, ALU.add))
            link(v.tensor_tensor_scan(ends, ones[:, 0:NE], extra, 0.0, ALU.mult, ALU.add))
            link(v.tensor_scalar(cmp_e, ends, row_id[:, 0:1], None, ALU.is_le))
            done(v.reduce_sum(item_eb[:, 0:1], cmp_e, AX.X))
            link(v.tensor_tensor(cmp_x, cmp_e, extra, ALU.mult))
            link(v.reduce_sum(item_eb[:, 1:2], cmp_x, AX.X))
            link(v.scalar_tensor_tensor(item_eb[:, 1:2], item_eb[:, 1:2], -1.0, row_id[:, 0:1], ALU.mult, ALU.add))
            link(v.tensor_scalar(item_eb[:, 1:2], item_eb[:, 1:2], 1.0, float(BLOCKS - 1), ALU.add, ALU.min))
            link(v.tensor_scalar(item_eb[:, 0:1], item_eb[:, 0:1], float(NE - 1), None, ALU.min))
            link(v.tensor_scalar(bc_e, ones, item_eb[:, 0:1], None, ALU.mult))
            v.tensor_scalar(bc_b, ones, item_eb[:, 1:2], None, ALU.mult).then_inc(sem("extra_items"), 1)
            link(v.tensor_scalar(nitems[:, 1:2], ends[:, NE - 1:NE], float(NE), None, ALU.add))
            done(v.tensor_copy(nitems.bitcast(i32)[:, 0:1], nitems[:, 1:2]))
            dve.wait_ge(sem("product"), product("items_spread", 1))
            done(v.tensor_copy(item_e[:, NE:], bank(0, 2, P)[:, 0, :]))
            link(v.tensor_scalar(item_b[:, NE:], bank(0, 2, P)[:, 1, :], float(2 * SLOTS), None, ALU.mult))
            link(v.tensor_copy(item_ei.bitcast(i32), item_e))
            v.tensor_copy(item_bi.bitcast(i32), item_b).then_inc(sem("items_ready"), 1)
            def item(w):
                e = dve.value_load(item_ei.bitcast(i32)[0:1, ds(w, 1)], min_val=0, max_val=NE - 1)
                first = dve.value_load(item_bi.bitcast(i32)[0:1, ds(w, 1)], min_val=0, max_val=(BLOCKS - 1) * 2 * SLOTS)
                return e, first

            def select_tokens(e, first):
                for blk in range(2):
                    ins = v.tensor_scalar(gat[:, blk, :], slot_ids[:, ds(first, SLOTS)], pos[:, blk, ds(e, 1)], None,
                                          ALU.is_equal)
                ins.then_inc(sem("gather_ready"), 1)

            def select_row(w):
                v.tensor_scalar(sel, row_id[:, 0:1].broadcast_to((P, SLOTS)), item_e[:, ds(w, 1)], None, ALU.is_equal
                                ).then_inc(sem("select_ready"), 1)

            def select_results(e, first):
                for blk in range(2):
                    ins = v.tensor_scalar(scat[:, blk, :], slot_ids[:, ds(first, 2 * SLOTS)], pos[:, blk, ds(e, 1)],
                                          comb[:, blk, ds(e, 1)], ALU.is_equal, ALU.mult)
                ins.then_inc(sem("scat_ready"), 1)

            dve.wait_ge(sem("items_ready"), 1)
            select_row(0)
            v.memset(h_sig[:, 0:1], 0.0).then_inc(sem("loop_buffers"), 1)
            dve.wait_ge(sem("probs_ready"), 2)
            link(v.reciprocal(psums, psums))
            for blk in range(2):
                done(v.tensor_scalar(probs[:, blk, :], probs[:, blk, :], psums[:, blk:blk + 1], None, ALU.mult))
            own.wait()
            for blk in range(2):
                for k in range(TOPK):
                    done(v.tensor_scalar(weighted[:, blk, k, :], one_hot[:, blk, k, :], probs[:, blk, k:k + 1], None, ALU.mult))
            own.wait()
            link(v.tensor_tensor(one_hot[:, :, 0:2, :], weighted[:, :, 0:2, :], weighted[:, :, 2:4, :], ALU.add))
            v.tensor_tensor(comb.rearrange("p a (b e) -> p a b e", b=1), one_hot[:, :, 0:1, :], one_hot[:, :, 1:2, :],
                            ALU.add).then_inc(sem("comb_ready"), 1)
            dve.wait_ge(sem("comb_ready"), 1)
            e, first = item(0)
            select_results(e, first)
            dve.wait_ge(sem("h2_kept"), 2)
            n_items = dve.value_load(nitems.bitcast(i32)[0:1, 0:1], min_val=NE, max_val=ITEMS)

            def add_scattered(n, name):
                for blk in range(2):
                    dve.wait_ge(sem("scattered"), 2 * n - 1 + blk)
                    for q in (2 * blk, 2 * blk + 1):
                        part = acc.rearrange("p a (h d) -> p (a h) d", h=2)[:, q, :]
                        ins = v.tensor_tensor(part, bank(4 + q, 512), part, ALU.add)
                    if blk or name != "acc_added":
                        ins.then_inc(sem(name), 1)

            with dve.Fori(0, n_items) as w:
                own.enter(w, 2)
                e, first = item(w + 1)
                dve.wait_ge(sem("gathered"), w + 1)
                select_tokens(e, first)
                dve.wait_ge(sem("slot3_free"), w + 8)
                after(dve, "gate_sigmoid", w)
                after(dve, "act_turned", w)
                v.tensor_scalar(h_gate, bank(0, 512), LIMIT, None, ALU.min).then_inc(sem("gate_clamped"), 1)
                link(v.tensor_scalar(h_up, bank(1, 512), LIMIT, -LIMIT, ALU.min, ALU.max))
                dve.wait_ge(sem("gate_clamped"), w + 1)
                link(v.scalar_tensor_tensor(h_up, h_up, 1.0, h_gate, ALU.add, ALU.mult))
                after(dve, "gate_sigmoid", w + 1)
                v.tensor_tensor(h_up, h_up, h_sig, ALU.mult).then_inc(sem("act_ready"), 1)
                add_scattered(w + 1, "acc_added")
                dve.wait_ge(sem("scat_turned"), w + 1)
                select_results(e, first)
                dve.wait_ge(sem("row_used"), w + 1)
                select_row(w + 1)
            own.leave(0)
            add_scattered(n_items + 1, "acc_whole")
            for blk in range(2):
                dve.wait_ge(sem("final_std"), blk + 1)
                v.reciprocal(frs[:, blk:blk + 1], frs[:, blk:blk + 1]).then_inc(sem("final_rstd"), 1)
                dve.wait_ge(sem("final_rstd"), blk + 1)
                v.scalar_tensor_tensor(fin[:, blk, :], acc[:, blk, :], frs[:, blk:blk + 1], g_fin, ALU.mult, ALU.mult
                                       ).then_inc(sem("final_ready"), 1)

        @block.gpsimd
        def _(pool):
            g = nc.gpsimd
            pool.wait_ge(sem("factors_done"), 1)

            def chunk_extras(n):
                cols = ds(CHUNK * n, CHUNK)
                if not isinstance(n, int):
                    pool.wait_ge(sem("g_increment"), n)
                g.tensor_copy(g_v, gv[:, :, cols])
                g.tensor_copy(g_k, gk[:, :, cols])
                g.tensor_copy(g_q, gq[:, :, cols]).then_inc(sem("staged_pool"), 1)
                pool.wait_ge(sem("low_ready"), n + 1)
                for l in range(1, LEVELS):
                    ins = g.tensor_tensor(low_at[:, l - 1, :, :], low, levels[:, l:l + 1, :].broadcast_to((P, KC, TILE)),
                                          ALU.mult)
                ins.then_inc(sem("level_ready"), 1)
                pool.wait_ge(sem("g_scores_read"), n + 1)
                apart(pool, "pool_passed")
                g.affine_select(out=g_a[0:64, :, :], in_=g_a[0:64, :, :], compare_op=ALU.is_ge, fill=0.0, base=0,
                                pattern=[[0, GH], [1, CHUNK]], channel_multiplier=-1).then_inc(sem("g_a_ready"), 1)

            chunk_extras(0)
            with pool.Fori(1, NCHUNK) as n:
                chunk_extras(n)
            pool.wait_ge(sem("g_ffn_loaded"), 16)
            pool.wait_ge(sem("u2_scaled"), 1)
            g.tensor_tensor(u2[:, 0, :], u2[:, 0, :], g_ffn, ALU.mult).then_inc(sem("u2_ready"), 1)


def kernel(**inputs):
    import concourse.bacc as _bacc
    from concourse import mybir as _mybir
    from concourse.bass_utils import run_bass_kernel_spmd as _run

    x = {k: np.asarray(v) for k, v in inputs.items()}
    f = {k: (v[0] if k not in ("x", "meta_tokens", "norm_final_g") else v) for k, v in x.items()}

    def kmajor(w):
        return np.ascontiguousarray(w.reshape(KC, P, -1).transpose(1, 0, 2))

    w_in = f["w_in"]
    names = ("gq", "gk", "gv", "gr", "ga", "rr", "rk", "rv", "rw", "ra", "rg", "gate_gla", "gate_rwkv")
    sizes = (512, 512, 1024, 1024, 16, 1024, 1024, 1024, 64, 64, 160, 1024, 1024)
    ends = np.cumsum(sizes)
    W = {n: w_in[:, e - s:e] for n, s, e in zip(names, sizes, ends)}

    def units(v):
        v = np.asarray(v).reshape(-1)
        if v.size % P:
            v = np.concatenate([v, np.zeros(-v.size % P, v.dtype)])
        return v.reshape(-1, P).T

    consts, moe_consts = constants()
    mid = [W[n][:, 512 * j:512 * j + 512] for n in ("gr", "gate_gla", "gate_rwkv") for j in range(2)]
    mid += [f[n][:, 512 * j:512 * j + 512] for n in ("w_gla_o", "w_rwkv_o", "w_out") for j in range(2)]
    f["mu_wa"] = np.concatenate([f["mu_w"], f["mu_a"]], -1)
    arrays = {
        "hT": kmajor(np.concatenate([x["meta_tokens"], x["x"][0]], 0).T),
        "consts": consts,
        "moe_consts": moe_consts,
        "params": np.ascontiguousarray(np.concatenate([units(f[n]) for n in PARAMS], 1)),
        "w_small": kmajor(np.concatenate([W[n] for n in ("rw", "ra", "rg", "ga")], 1)),
        "w_gla_a2": f["w_gla_a2"], "w_wa2": np.concatenate([f["w_decay2"], f["w_a2"]], 0), "w_gate2": f["w_gate2"],
        "w_gla": np.stack([kmajor(np.concatenate([W["gq"][:, P * h:P * h + P], W["gk"][:, P * h:P * h + P],
                                                  W["gv"][:, GDV * h:GDV * h + GDV]], 1)) for h in range(GH)]),
        "w_rwkv": np.stack([kmajor(np.concatenate([W[n][:, P * m:P * m + P] for n in ("rk", "rr", "rv")], 1))
                            for m in range(KC)]),
        "w_mid": np.stack([kmajor(w) for w in mid]),
        "w_router": kmajor(f["w_router"]),
        "b_router": f["b_router"].reshape(1, NE),
        "norm_ffn_g": f["norm_ffn_g"].reshape(1, D),
        "w_gu": f["w_exp_gu"], "b_gu": f["b_exp_gu"], "w_dn": f["w_exp_down"], "b_dn": f["b_exp_down"],
        "norm_final_g": f["norm_final_g"].reshape(1, D),
    }
    nc = _bacc.Bacc("TRN2", target_bir_lowering=False, num_devices=1)
    ins, aps = {}, {}
    for name, a in arrays.items():
        a = np.ascontiguousarray(a)
        ins[f"in_{name}"] = a
        aps[name] = nc.dram_tensor(f"in_{name}", a.shape, _mybir.dt.from_np(a.dtype), kind="ExternalInput").ap()
    aps["out"] = nc.dram_tensor("out_0", (SEQ, D), _mybir.dt.float32, kind="ExternalOutput").ap()
    block_kernel(nc, aps)
    r = _run(nc, [ins], core_ids=[0])
    return r.results[0]["out_0"].reshape(1, SEQ, D)
```
